# Optimizing a Trainium2 kernel written in Bass

```python
import jax, jax.numpy as jnp
from jax import lax
import numpy as np

D_MODEL = 1024
BATCH = 1
SEQ = 512
DEPTH = 1

CHUNK = 64
PLE_DIM = 256
GMLP_BLOCK = 128
GMLP_GROUPS = 12
GMLP_GROUP_DIM = 128
GMLP_WIDTH = GMLP_GROUPS * GMLP_GROUP_DIM
MLA_HEADS = 8
QK_NOPE_DIM = 128
QK_ROPE_DIM = 64
V_HEAD_DIM = 128
Q_LORA = 384
KV_LORA = 256
ROPE_THETA = 10000.0
Q_BLOCK = 128
N_GROUPS = 8
EXPERTS_PER_GROUP = 8
N_EXPERTS = N_GROUPS * EXPERTS_PER_GROUP
TOPK = 2
D_EXPERT = 256
DISPATCH_BLOCK = 128
EPS = 1e-6
IN_COLS = 2 * GMLP_WIDTH + Q_LORA + KV_LORA + QK_ROPE_DIM + 2 * D_MODEL

kernel_name = "hybrid_gmlp_mla_hmoe_ple_block"

def rmsnorm(x, g):
    xf = x.astype(jnp.float32)
    xf = xf * lax.rsqrt(jnp.mean(xf * xf, axis=-1, keepdims=True) + EPS)
    return xf.astype(x.dtype) * g

def layernorm_gain(x, g):
    xf = x.astype(jnp.float32)
    mu = jnp.mean(xf, axis=-1, keepdims=True)
    xc = xf - mu
    xf = xc * lax.rsqrt(jnp.mean(xc * xc, axis=-1, keepdims=True) + EPS)
    return xf.astype(x.dtype) * g

def rope_tables(seq_len, dtype):
    inv_freq = ROPE_THETA ** (-jnp.arange(0, QK_ROPE_DIM, 2, dtype=jnp.float32) / QK_ROPE_DIM)
    ang = jnp.arange(seq_len, dtype=jnp.float32)[:, None] * inv_freq[None, :]
    return jnp.cos(ang).astype(dtype), jnp.sin(ang).astype(dtype)

def apply_rope(x, cos, sin):
    c = cos[None, :, None, :]
    s = sin[None, :, None, :]
    x1, x2 = jnp.split(x, 2, axis=-1)
    return jnp.concatenate([x1 * c - x2 * s, x1 * s + x2 * c], axis=-1)

def gmlp_branch(u, v, g_v, w_spatial, b_spatial, w_proj):
    B, S, _ = u.shape
    nb = S // GMLP_BLOCK
    v = layernorm_gain(v, g_v)
    vb = v.reshape(B, nb, GMLP_BLOCK, GMLP_GROUPS, GMLP_GROUP_DIM)
    t = jnp.arange(GMLP_BLOCK)
    mask = (t[None, :] // CHUNK) <= (t[:, None] // CHUNK)
    w = jnp.where(mask[None], w_spatial, jnp.zeros_like(w_spatial))
    sv = jnp.einsum('gts,bnsgc->bntgc', w, vb) + b_spatial.T[None, None, :, :, None]
    y = u * sv.reshape(B, S, GMLP_WIDTH)
    return y @ w_proj

def mla_branch(c_q, c_kv, k_rope, g_cq, w_uq, g_ckv, w_ukv, w_o):
    B, S, _ = c_q.shape
    H = MLA_HEADS
    cos, sin = rope_tables(S, c_q.dtype)
    q = (rmsnorm(c_q, g_cq) @ w_uq).reshape(B, S, H, QK_NOPE_DIM + QK_ROPE_DIM)
    q_nope, q_pe = jnp.split(q, [QK_NOPE_DIM], axis=-1)
    q = jnp.concatenate([q_nope, apply_rope(q_pe, cos, sin)], axis=-1)
    kv = (rmsnorm(c_kv, g_ckv) @ w_ukv).reshape(B, S, H, QK_NOPE_DIM + V_HEAD_DIM)
    k_nope, v = jnp.split(kv, [QK_NOPE_DIM], axis=-1)
    k_pe = apply_rope(k_rope[:, :, None, :], cos, sin)
    k = jnp.concatenate([k_nope, jnp.broadcast_to(k_pe, (B, S, H, QK_ROPE_DIM))], axis=-1)
    scale = (QK_NOPE_DIM + QK_ROPE_DIM) ** -0.5
    nq = S // Q_BLOCK
    kpos_chunk = jnp.arange(S) // CHUNK
    qb_all = q.reshape(B, nq, Q_BLOCK, H, QK_NOPE_DIM + QK_ROPE_DIM).transpose(1, 0, 2, 3, 4)

    def attend(args):
        qb, i = args
        qpos_chunk = (i * Q_BLOCK + jnp.arange(Q_BLOCK)) // CHUNK
        mask = kpos_chunk[None, :] <= qpos_chunk[:, None]
        s = jnp.einsum('bqhd,bkhd->bhqk', qb, k, preferred_element_type=jnp.float32) * scale
        s = jnp.where(mask[None, None], s, -jnp.inf)
        pr = jax.nn.softmax(s, axis=-1).astype(v.dtype)
        return jnp.einsum('bhqk,bkhv->bqhv', pr, v)

    o = lax.map(attend, (qb_all, jnp.arange(nq)))
    o = o.transpose(1, 0, 2, 3, 4).reshape(B, S, H * V_HEAD_DIM)
    return o @ w_o

def hierarchical_route(xf, w_rg, b_rg, w_re, b_re):
    N = xf.shape[0]
    g_logits = (xf @ w_rg).astype(jnp.float32)
    g_prob = jax.nn.softmax(g_logits, axis=-1)
    _, g_idx = lax.top_k(g_prob + b_rg[None, :].astype(jnp.float32), 1)
    g_w = jnp.take_along_axis(g_prob, g_idx, axis=-1)
    e_logits = (xf @ w_re).astype(jnp.float32).reshape(N, N_GROUPS, EXPERTS_PER_GROUP)
    e_logits = jnp.take_along_axis(e_logits, g_idx[:, :, None], axis=1)[:, 0]
    e_prob = jax.nn.softmax(e_logits, axis=-1)
    e_bias = b_re.astype(jnp.float32)[g_idx[:, 0]]
    _, e_local = lax.top_k(e_prob + e_bias, TOPK)
    e_sel = jnp.take_along_axis(e_prob, e_local, axis=-1)
    e_sel = e_sel / jnp.sum(e_sel, axis=-1, keepdims=True)
    weights = g_w * e_sel
    expert_ids = g_idx * EXPERTS_PER_GROUP + e_local
    return expert_ids, weights

def moe_dispatch(xf, expert_ids, weights, w_gate, w_up, w_down):
    N, D = xf.shape
    A = N * TOPK
    flat_e = expert_ids.reshape(-1)
    flat_t = jnp.repeat(jnp.arange(N), TOPK)
    flat_w = weights.reshape(-1)
    order = jnp.argsort(flat_e)
    se, st, sw = flat_e[order], flat_t[order], flat_w[order]
    counts = jnp.zeros((N_EXPERTS,), jnp.int32).at[flat_e].add(1)
    padded = (counts + DISPATCH_BLOCK - 1) // DISPATCH_BLOCK * DISPATCH_BLOCK
    pad_end = jnp.cumsum(padded)
    pad_start = pad_end - padded
    start = jnp.cumsum(counts) - counts
    dest = pad_start[se] + jnp.arange(A) - start[se]
    P = A + N_EXPERTS * DISPATCH_BLOCK
    nblk = P // DISPATCH_BLOCK
    buf = jnp.zeros((P, D), xf.dtype).at[dest].set(xf[st])
    blk_e = jnp.minimum(jnp.searchsorted(pad_end, jnp.arange(nblk) * DISPATCH_BLOCK, side='right'), N_EXPERTS - 1)

    def expert_block(args):
        xb, e = args
        hdn = jax.nn.silu(xb @ w_gate[e]) * (xb @ w_up[e])
        return hdn @ w_down[e]

    ys = lax.map(expert_block, (buf.reshape(nblk, DISPATCH_BLOCK, D), blk_e)).reshape(P, D)
    return jnp.zeros_like(xf).at[st].add(ys[dest] * sw[:, None].astype(ys.dtype))

def setup_inputs(seed: int = 0) -> dict:
    key = jax.random.key(seed)
    ks = jax.random.split(key, 32)
    f32 = jnp.float32

    def nrm(k, shape, fan_in):
        return jax.random.normal(k, shape, f32) * (fan_in ** -0.5)

    def gain(k, shape):
        return 1.0 + 0.05 * jax.random.normal(k, shape, f32)

    L = DEPTH
    return {
        "x": jax.random.normal(ks[0], (BATCH, SEQ, D_MODEL), f32),
        "p": jax.random.normal(ks[1], (DEPTH, BATCH, SEQ, PLE_DIM), f32),
        "g_mix": gain(ks[2], (L, D_MODEL)),
        "w_in": nrm(ks[3], (L, D_MODEL, IN_COLS), D_MODEL),
        "g_gv": gain(ks[4], (L, GMLP_WIDTH)),
        "w_spatial": nrm(ks[5], (L, GMLP_GROUPS, GMLP_BLOCK, GMLP_BLOCK), GMLP_BLOCK),
        "b_spatial": 1.0 + 0.1 * jax.random.normal(ks[6], (L, GMLP_GROUPS, GMLP_BLOCK), f32),
        "w_gproj": nrm(ks[7], (L, GMLP_WIDTH, D_MODEL), GMLP_WIDTH),
        "g_cq": gain(ks[8], (L, Q_LORA)),
        "w_uq": nrm(ks[9], (L, Q_LORA, MLA_HEADS * (QK_NOPE_DIM + QK_ROPE_DIM)), Q_LORA),
        "g_ckv": gain(ks[10], (L, KV_LORA)),
        "w_ukv": nrm(ks[11], (L, KV_LORA, MLA_HEADS * (QK_NOPE_DIM + V_HEAD_DIM)), KV_LORA),
        "w_mla_o": nrm(ks[12], (L, MLA_HEADS * V_HEAD_DIM, D_MODEL), MLA_HEADS * V_HEAD_DIM),
        "w_out": nrm(ks[13], (L, D_MODEL, D_MODEL), D_MODEL),
        "g_moe": gain(ks[14], (L, D_MODEL)),
        "w_router_g": nrm(ks[15], (L, D_MODEL, N_GROUPS), D_MODEL),
        "b_router_g": 0.01 * jax.random.normal(ks[16], (L, N_GROUPS), f32),
        "w_router_e": nrm(ks[17], (L, D_MODEL, N_EXPERTS), D_MODEL),
        "b_router_e": 0.01 * jax.random.normal(ks[18], (L, N_GROUPS, EXPERTS_PER_GROUP), f32),
        "w_e_gate": nrm(ks[19], (L, N_EXPERTS, D_MODEL, D_EXPERT), D_MODEL),
        "w_e_up": nrm(ks[20], (L, N_EXPERTS, D_MODEL, D_EXPERT), D_MODEL),
        "w_e_down": nrm(ks[21], (L, N_EXPERTS, D_EXPERT, D_MODEL), D_EXPERT),
        "g_ple": gain(ks[22], (L, D_MODEL)),
        "w_ple_gate": nrm(ks[23], (L, D_MODEL, D_MODEL), D_MODEL),
        "w_ple_proj": nrm(ks[24], (L, PLE_DIM, D_MODEL), PLE_DIM),
        "g_final": gain(ks[25], (D_MODEL,)),
    }

def reference(x, p, g_mix, w_in, g_gv, w_spatial, b_spatial, w_gproj, g_cq, w_uq, g_ckv, w_ukv,
              w_mla_o, w_out, g_moe, w_router_g, b_router_g, w_router_e, b_router_e,
              w_e_gate, w_e_up, w_e_down, g_ple, w_ple_gate, w_ple_proj, g_final):
    B, S, D = x.shape
    cuts = [GMLP_WIDTH, 2 * GMLP_WIDTH, 2 * GMLP_WIDTH + Q_LORA, 2 * GMLP_WIDTH + Q_LORA + KV_LORA,
            2 * GMLP_WIDTH + Q_LORA + KV_LORA + QK_ROPE_DIM,
            2 * GMLP_WIDTH + Q_LORA + KV_LORA + QK_ROPE_DIM + D_MODEL]
    h = x
    for i in range(DEPTH):
        a = rmsnorm(h, g_mix[i])
        z = a @ w_in[i]
        z_u, z_v, c_q, c_kv, k_rope, gate_a, gate_b = jnp.split(z, cuts, axis=-1)
        y_a = gmlp_branch(jax.nn.gelu(z_u), jax.nn.gelu(z_v), g_gv[i], w_spatial[i], b_spatial[i], w_gproj[i])
        y_b = mla_branch(c_q, c_kv, k_rope, g_cq[i], w_uq[i], g_ckv[i], w_ukv[i], w_mla_o[i])
        merged = jax.nn.sigmoid(gate_a) * y_a + jax.nn.sigmoid(gate_b) * y_b
        h = h + merged @ w_out[i]
        m = rmsnorm(h, g_moe[i]).reshape(B * S, D)
        ids, wts = hierarchical_route(m, w_router_g[i], b_router_g[i], w_router_e[i], b_router_e[i])
        h = h + moe_dispatch(m, ids, wts, w_e_gate[i], w_e_up[i], w_e_down[i]).reshape(B, S, D)
        n3 = rmsnorm(h, g_ple[i])
        h = h + jax.nn.sigmoid(n3 @ w_ple_gate[i]) * (p[i] @ w_ple_proj[i])
    return rmsnorm(h, g_final)


_drawn_inputs = setup_inputs


def setup_inputs(seed=0):
    import zlib

    import numpy as np

    out = dict(_drawn_inputs(seed))
    spreads = {}
    factors = {'g_gv': 11.724,
     'g_cq': 5.671,
     'g_ckv': 6.095,
     'b_router_e': 12.62,
     'g_ple': 39.878,
     'b_spatial': 4.919,
     'g_moe': 4.359,
     'b_router_g': 7.185}
    for name, (base, spread) in spreads.items():
        noise = np.random.default_rng([zlib.crc32(name.encode()), seed]).standard_normal(out[name].shape)
        drawn = base * np.exp(spread * noise) if base else spread * noise
        out[name] = __import__('jax').numpy.asarray(drawn.astype(out[name].dtype))
    for name, factor in factors.items():
        out[name] = (out[name] * factor).astype(out[name].dtype)
    return out
```

```python
from contextlib import ExitStack

import concourse.bass as bass
from concourse import mybir
from concourse.alu_op_type import AluOpType as ALU

ACT = mybir.ActivationFunctionType
F32 = mybir.dt.float32
I32 = mybir.dt.int32
AX_X = mybir.AxisListType.X

P = 128
S = 512
D = 1024
NT = S // P
ND = D // P
GW = 1536
NG = GW // P
NH = 8
QL = 384
KVL = 256
NOPE = 128
ROPE = 64
HR = ROPE // 2
VH = 128
QW = NOPE + ROPE
KVW = NOPE + VH
PLE = 256
NE = 64
NGRP = 8
EPG = NE // NGRP
FE = 256
CHUNK = 64
EPS = 1e-6
SCALE = float(QW) ** -0.5
MASKED = -1e30
CAP = 128
NBLK = S // CAP
EMPTY = 4096
TOKEN_BITS = EMPTY | (S - 1)
NBUF = 4
KB = 1024
SBUF0 = 16896
V_COL, C_COL = GW, 2 * GW
GA_COL = C_COL + QL + KVL + ROPE
GB_COL = GA_COL + D


def build(nc, x, p, g_mix, w_in, g_gv, w_spatial, b_spatial, w_gproj, g_cq, w_uq, g_ckv, w_ukv, w_mla_o, w_out,
          g_moe, w_router_g, b_router_g, w_router_e, b_router_e, w_e_gate, w_e_up, w_e_down, g_ple, w_ple_gate,
          w_ple_proj, g_final, cos_t, sin_t, out):
    with ExitStack() as ctx:
        def sem(name):
            return ctx.enter_context(nc.semaphore(name))

        def at(name, kb, shape, dt=F32):
            return nc.alloc_sbuf_tensor_at(name, shape, dt, offset=SBUF0 + int(kb * KB))

        RING, ARENA, CONST, SMALL = 0, 96, 184, 200
        slot = [at(f"slot{i}", RING + 16 * i, [P, 4096]) for i in range(5)]
        ring_tail = RING + 80
        gate_order = [2, 3, 0, 1]
        wgu = [at(f"wgu{i}", RING + 24 * gate_order[i], [P, 2, ND, FE]) for i in range(NBUF)]
        wdn = [at(f"wdn{i}", RING + 24 * gate_order[i] + 16, [P, 2, D]) for i in range(NBUF)]
        aT = at("aT", ARENA, [P, ND, S])
        wkr = at("wkr", ARENA + 16, [P, ND, 2, P])
        wpe = at("wpe", ARENA + 24, [P, 3, 4, ROPE])
        wpes = at("wpes", ARENA + 27, [P, 3, 4, ROPE])
        vv = at("vv", ARENA + 16, [P, NT, NH, VH])
        xs = at("xs", ARENA + 32, [P, NT, D])
        xn = at("xn", ARENA + 48, [P, NT, D])
        qn = at("qn", ARENA + 32, [P, NH, S])
        qpe = at("qpe", ARENA + 48, [P, NH // 2, S])
        kpe = at("kpe", ARENA + 56, [P, S])
        cT = at("cT", ARENA + 58, [P, 5, S])
        csq = at("csq", ARENA + 68, [P, 5, S])
        wsn = at("wsn", ARENA + 68, [P, NG, P])
        rbc = at("rbc", ARENA + 78, [P, 2, S])
        ropeA = at("ropeA", ARENA + 82, [P, S])
        ropeB = at("ropeB", ARENA + 84, [P, S])
        junk = at("junk", ARENA + 84, [P, D])
        pr = [at(f"pr{i}", ARENA + 58 + 5 * i, [P, 1280]) for i in range(2)]
        prT = [at(f"prT{i}", ARENA + 68 + 5 * i, [P, 1280]) for i in range(2)]
        kn = at("kn", ring_tail, [P, NH, S])
        sigB = at("sigB", ring_tail, [P, ND, S])
        merged = at("merged", ARENA + 16, [P, ND, S])
        vt = at("vt", ARENA + 32, [P, NT, GW])
        uT = at("uT", ARENA + 56, [P, NG, S])
        tmp = [at(f"tmp{i}", ARENA + 80 + 2 * i, [P, S]) for i in range(2)]
        sigA = at("sigA", ring_tail, [P, ND, S])
        hn = at("hn", ARENA, [P, NT, D])
        pp = at("pp", ARENA + 16, [P, NT, D])
        h = at("h", ARENA + 32, [P, NT, D])
        psb = at("psb", ARENA + 48, [P, NT, PLE])
        pT = at("pT", ARENA + 52, [P, 2, S])
        mT = at("mT", ARENA + 56, [P, ND, S])
        wpp = at("wpp", ARENA + 72, [P, 2, D])
        junk2 = at("junk2", ARENA + 80, [P, D])
        xg = [at(f"xg{i}", ARENA + 4 * i, [P, D]) for i in range(2)]
        xgT = [at(f"xgT{i}", ARENA + 8 + 4 * i, [P, ND, P]) for i in range(2)]
        ysb = [at(f"ysb{i}", ARENA + 48 + 4 * i, [P, D]) for i in range(2)]
        wpg = at("wpg", ARENA + 56, [P, ND, D])
        cosT = at("cosT", CONST, [P, S])
        sinT = at("sinT", CONST + 2, [P, S])
        gfin = at("gfin", CONST, [P, D])
        bsp = at("bsp", CONST + 4, [P, NG, P])
        sg = [at(f"sg{i}", CONST + 4 + i, [P, FE]) for i in range(2)]
        hm = [at(f"hm{i}", CONST + 6 + i, [P, FE]) for i in range(2)]
        hT = [at(f"hT{i}", CONST + 8 + i, [P, 2, P]) for i in range(2)]
        wsT = at("wsT", CONST + 10, [P, NG, P])
        rt_e = at("rt_e", CONST + 10, [P, NT, NGRP, EPG])
        sel1 = at("sel1", CONST + 11, [P, NT, NGRP, EPG])
        sel2 = at("sel2", CONST + 12, [P, NT, NGRP, EPG])
        sel = at("sel", CONST + 13, [P, NT, NE])
        adr = at("adr", CONST + 14, [P, NT, NE])
        adr2 = at("adr2", CONST + 15, [P, NT, NE])
        y1 = at("y1", RING, [P, NT, D])
        y2 = at("y2", RING + 16, [P, NT, D])
        n3 = at("n3", RING + 32, [P, NT, D])
        n3T = at("n3T", RING + 48, [P, ND, S])
        ysum = at("ysum", RING + 64, [P, 2, D])
        fin = at("fin", RING + 72, [P, NT, D])
        sgt = at("sgt", RING, [P, NT, D])

        place = [SMALL * KB]

        def small(name, shape, dt=F32):
            n = 4
            for k in shape[1:]:
                n *= k
            t = nc.alloc_sbuf_tensor_at(name, shape, dt, offset=SBUF0 + place[0])
            place[0] += (n + 31) // 32 * 32
            return t

        ident = small("ident", [P, P])
        ones = small("ones", [P, P])
        before = small("before", [P, P])
        mrow = small("mrow", [1, P])
        mcol = small("mcol", [1, P])
        gmx = small("gmx", [P, ND])
        gvg = small("gvg", [P, NG])
        gcq = small("gcq", [P, 3])
        gckv = small("gckv", [P, 2])
        gmo = small("gmo", [P, ND])
        gpl = small("gpl", [P, ND])
        brg = small("brg", [P, NGRP])
        bre = small("bre", [P, NGRP, EPG])
        stat = small("stat", [P, 3 * NT])
        rstd = small("rstd", [P, 3 * NT])
        bst = small("bst", [P, NT, 3, 6])
        bag = small("bag", [P, NT, 2])
        vrs = small("vrs", [P, NT])
        rnt = small("rnt", [P, 4])
        eps = small("eps", [P, 1])
        mx = small("mx", [P, 2, NT])
        rs = small("rs", [P, 2, NT])
        ri = small("ri", [P, 2, NT])
        wts = small("wts", [P, 2, NT])
        tabs = small("tabs", [CAP, NBLK, NE], I32)
        toks = small("toks", [CAP, NBLK, NE], I32)
        idx_x = [small(f"idx_x{i}", [CAP, 1], I32) for i in range(2)]
        idx_y = [small(f"idx_y{i}", [CAP, 1], I32) for i in range(2)]
        iota8 = small("iota8", [P, EPG])
        iota8up = small("iota8up", [P, EPG])
        most = small("most", [1, 1])
        most_i = small("most_i", [1, 1], I32)
        dst_i = small("dst_i", [P, 2, NT], I32)
        aid = small("aid", [P, 2, NT], I32)
        r8 = [at(f"r8_{i}", ARENA + 84 + i / 8, [P, NT, EPG]) for i in range(8)]
        r1 = [at(f"r1_{i}", ARENA + 85 + i / 32, [P, NT]) for i in range(14)]
        lg = at("lg", ARENA + 86, [P, NT, NGRP + NE])
        wr = at("wr", ARENA + 80, [P, ND, NGRP + NE])
        fill = at("fill", ARENA + 56, [P, S * NE // P], I32)
        iota_e = adr2
        assert SBUF0 + place[0] <= 229344, place[0]

        bank = [ctx.enter_context(nc.psum_tensor(f"bank{i}", [P, S], F32)) for i in range(8)]

        m_dram = nc.dram_tensor("m_rows", [S, D], F32)
        y_dram = nc.dram_tensor("y_rows", [2 * S, D], F32)
        tab_dram = nc.dram_tensor("slot_table", [S * NE, 1], I32)

        piece_in = [sem(f"piece_in{i}") for i in range(5)]
        piece_used = sem("piece_used")
        x_in = [sem(f"x_in{t}") for t in range(NT)]
        consts_in, rope_in, ws_in = sem("consts_in"), sem("rope_in"), sem("ws_in")
        x_again, p_in, wpp_in, wr_in, bias_in = (sem(n) for n in ("x_again", "p_in", "wpp_in", "wr_in", "bias_in"))
        gp_step, dv_step = sem("gp_step"), sem("dv_step")
        ident_ok, masks_ok, iota_ok, aid_ok = sem("ident_ok"), sem("masks_ok"), sem("iota_ok"), sem("aid_ok")
        ws_mm, ws_sb, ws_zero = sem("ws_mm"), sem("ws_sb"), sem("ws_zero")
        x_root, xn_ok, x_mm, aT_ok = sem("x_root"), sem("xn_ok"), sem("x_mm"), sem("aT_ok")
        c_mm, c_sb, c_sq, ss_mm, cT_ok = sem("c_mm"), sem("c_sb"), sem("c_sq"), sem("ss_mm"), sem("cT_ok")
        wkr_ok, kr_mm, kr_mul, kpe_ok = sem("wkr_ok"), sem("kr_mm"), sem("kr_mul"), sem("kpe_ok")
        wpe_ok, qkA_mm, qkD_mm, qkA_sb, qkD_sb, pe_add = (sem(n) for n in
                                                       ("wpe_ok", "qkA_mm", "qkD_mm", "qkA_sb", "qkD_sb", "pe_add"))
        s_mm, s_max, s_neg, s_exp, s_rec, p_ok, pt_mm, pt_sb, o_mm, o_sb = (sem(n) for n in (
            "s_mm", "s_max", "s_neg", "s_exp", "s_rec", "p_ok", "pt_mm", "pt_sb", "o_mm", "o_sb"))
        gb_mm, gb_sb, yb_mm, yb_sb = sem("gb_mm"), sem("gb_sb"), sem("yb_mm"), sem("yb_sb")
        v_mm, v_sb, v_ln, u_mm, u_sb = sem("v_mm"), sem("v_sb"), sem("v_ln"), sem("u_mm"), sem("u_sb")
        sp_mm, sp_sb, y_ok, ga_mm, ga_sb = sem("sp_mm"), sem("sp_sb"), sem("y_ok"), sem("ga_mm"), sem("ga_sb")
        gp_mm, gp_sb, mg_ok, w_mm, w_sb, h_ok = (sem(n) for n in ("gp_mm", "gp_sb", "mg_ok", "w_mm", "w_sb", "h_ok"))
        h_root, hn_ok, hn_out, m_mm, mT_ok = sem("h_root"), sem("hn_ok"), sem("hn_out"), sem("m_mm"), sem("mT_ok")
        pt2_mm, pt2_sb, pp_mm, pp_sb = sem("pt2_mm"), sem("pt2_sb"), sem("pp_mm"), sem("pp_sb")
        lg_mm, rt_sub, rt_exp, sel_ok, rank_mm, dst_ok = (sem(n) for n in (
            "lg_mm", "rt_sub", "rt_exp", "sel_ok", "rank_mm", "dst_ok"))
        fill_out, slots_out, tab_in, toks_ok, most_ok = (sem(n) for n in (
            "fill_out", "slots_out", "tab_in", "toks_ok", "most_ok"))
        gu_in = [sem(f"gu_in{i}") for i in range(NBUF)]
        dn_in = [sem(f"dn_in{i}") for i in range(NBUF)]
        xg_in = [sem(f"xg_in{i}") for i in range(2)]
        y_out = [sem(f"y_out{i}") for i in range(2)]
        ix_ok, iy_ok = sem("ix_ok"), sem("iy_ok")
        xt_mm, xt_sb, gu_mm, silu, h_mul, ht_mm, ht_sb, y_mm, ya_sb, yb2_sb = (sem(n) for n in (
            "xt_mm", "xt_sb", "gu_mm", "silu", "h_mul", "ht_mm", "ht_sb", "y_mm", "ya_sb", "yb2_sb"))
        block_free, dma_go = sem("block_free"), sem("dma_go")
        moe_done, wpg_in, gfin_in = sem("moe_done"), sem("wpg_in"), sem("gfin_in")
        y_in = [sem(f"y_in{t}") for t in range(NT)]
        ysum_ok, h2_ok, h2_root, n3_ok, n_mm, n3T_ok = (sem(n) for n in (
            "ysum_ok", "h2_ok", "h2_root", "n3_ok", "n_mm", "n3T_ok"))
        g_mm, g_sb, pg_ok, h3_ok, h3_root, fin_ok, fin_out = (sem(n) for n in (
            "g_mm", "g_sb", "pg_ok", "h3_ok", "h3_root", "fin_ok", "fin_out"))
        c_ms, c_rt, v_var, v_rt = sem("c_ms"), sem("c_rt"), sem("v_var"), sem("v_rt")

        wi = w_in[0].rearrange("(k p) n -> p k n", p=P)
        uq = w_uq[0].rearrange("(k p) n -> p k n", p=P)
        ukv = w_ukv[0].rearrange("(k p) n -> p k n", p=P)
        wo = w_mla_o[0].rearrange("(k p) n -> p k n", p=P)
        wgp = w_gproj[0].rearrange("(k p) n -> p k n", p=P)
        wot = w_out[0].rearrange("(k p) n -> p k n", p=P)
        pieces = [wi[:, :, C_COL:C_COL + 512], wi[:, :, C_COL + 512:GA_COL], uq[:, :, 0:768], uq[:, :, 768:1536], ukv]
        pieces += [wi[:, :, GB_COL + 512 * j:GB_COL + 512 * (j + 1)] for j in range(2)]
        pieces += [wo[:, :, 512 * j:512 * (j + 1)] for j in range(2)]
        pieces += [wi[:, :, V_COL + 512 * j:V_COL + 512 * (j + 1)] for j in range(3)]
        pieces += [wi[:, :, 512 * j:512 * (j + 1)] for j in range(3)]
        pieces += [wi[:, :, GA_COL + 512 * j:GA_COL + 512 * (j + 1)] for j in range(2)]
        pieces += [wgp[:, :, 256 * j:256 * (j + 1)] for j in range(4)]
        pieces += [wot[:, :, 512 * j:512 * (j + 1)] for j in range(2)]
        PC_C, PC_UQ, PC_UKV, PC_GB, PC_O, PC_V, PC_U, PC_GA, PC_GP, PC_W = 0, 2, 4, 5, 7, 9, 12, 15, 17, 21
        assert len(pieces) == PC_W + 2

        def piece(i):
            k, n = pieces[i].shape[1], pieces[i].shape[2]
            return slot[i % 5][:, 0:k * n].rearrange("p (k n) -> p k n", k=k)

        def arrived(eng, i):
            eng.wait_ge(piece_in[i % 5], 16 * (i // 5 + 1))

        def past(eng, s, v):
            if not isinstance(v, int) or v > 0:
                eng.wait_ge(s, v)

        s_bank = [(1, 384), (2, 0), (1, 0), (0, 0)]
        s_order = [0, 2, 3, 1]
        s_ready = [2, 4, 2, 3]
        p_off = [0, 128, 384, 768]
        t_bank = [(3, 0), (4, 0), (5, 0), (4, 384)]
        t_off = [0, 512, 896, 1152]

        def scores(i):
            b, c = s_bank[i]
            return bank[b][:, c:c + P * (i + 1)]

        def turned(j):
            b, c = t_bank[j]
            return bank[b][:, c:c + P * (NT - j)]

        block = ctx.enter_context(nc.Block())

        @block.sync
        def _(sp):
            for i in range(len(pieces)):
                past(sp, piece_used, i - 4)
                sp.dma_start(piece(i), pieces[i]).then_inc(piece_in[i % 5], 16)

            def load_expert(e, u, i):
                past(sp, gu_mm, e - (NBUF - 1))
                past(sp, y_mm, e - (NBUF - 1))
                sp.dma_start(wgu[u][:, 0], w_e_gate[0, bass.ds(e, 1)].rearrange("a (p k) n -> p (a k) n", p=P))\
                    .then_inc(gu_in[u], 16)
                sp.dma_start(wgu[u][:, 1], w_e_up[0, bass.ds(e, 1)].rearrange("a (p k) n -> p (a k) n", p=P))\
                    .then_inc(gu_in[u], 16)
                sp.dma_start(wdn[u][:], w_e_down[0, bass.ds(e, 1)].rearrange("a (p k) n -> p (a k) n", p=P))\
                    .then_inc(dn_in[u], 16)

            sp.wait_ge(piece_used, PC_W - 1)
            load_expert(0, 0, 0)
            sp.wait_ge(gp_sb, ND)
            load_expert(1, 1, 0)
            sp.wait_ge(piece_used, PC_W + 1)
            load_expert(2, 2, 0)
            sp.wait_ge(piece_used, PC_W + 2)
            load_expert(3, 3, 0)
            sp.wait_ge(most_ok, 1)
            sp.wait_ge(pp_mm, 2 * NT)
            sp.dma_start(wpg[:], w_ple_gate[0].rearrange("(p k) n -> p k n", p=P)).then_inc(wpg_in, 16)
            with sp.Fori(1, NE // NBUF) as i:
                for u in range(NBUF):
                    load_expert(i * NBUF + u, u, i)
            most_v = sp.value_load(most_i[0:1, 0:1], min_val=0, max_val=S)
            with sp.If(most_v > CAP):
                with sp.Fori(1, NBLK) as b:
                    with sp.Fori(0, NE) as e:
                        step = (b - 1) * NE + e
                        n = b * NE + e
                        sp.wait_ge(block_free, step + 1)
                        sp.dma_start(wgu[0][:, 0], w_e_gate[0, bass.ds(e, 1)].rearrange("a (p k) n -> p (a k) n", p=P))\
                            .then_inc(gu_in[0], 16)
                        sp.dma_start(wgu[0][:, 1], w_e_up[0, bass.ds(e, 1)].rearrange("a (p k) n -> p (a k) n", p=P))\
                            .then_inc(gu_in[0], 16)
                        sp.dma_start(wdn[0][:], w_e_down[0, bass.ds(e, 1)].rearrange("a (p k) n -> p (a k) n", p=P))\
                            .then_inc(dn_in[0], 16)
            sp.wait_ge(moe_done, 1)
            for t in range(NT):
                sp.dma_start(y1[:, t], y_dram[P * t:P * (t + 1), :]).then_inc(y_in[t], 16)
                sp.dma_start(y2[:, t], y_dram[S + P * t:S + P * (t + 1), :]).then_inc(y_in[t], 16)
            for t in range(NT):
                sp.wait_ge(fin_ok, t + 1)
                sp.dma_start(out[0, P * t:P * (t + 1), :], fin[:, t]).then_inc(fin_out, 16)
            sp.wait_ge(fin_out, 16 * NT)

        @block.gpsimd
        def _(pool):
            steps = [0]

            def link(ins):
                steps[0] += 1
                ins.then_inc(gp_step, 1)
                pool.wait_ge(gp_step, steps[0])

            pool.memset(eps[:], EPS).then_inc(ident_ok, 1)
            link(pool.memset(ident[:], 0.0))
            pool.affine_select(out=ident[:], in_=ident[:], compare_op=ALU.not_equal, fill=1.0, base=0,
                               pattern=[[-1, P]], channel_multiplier=1).then_inc(ident_ok, 1)
            link(pool.memset(mrow[:], 0.0))
            pool.memset(mrow[:, 0:CHUNK], 1.0).then_inc(masks_ok, 1)
            link(pool.memset(mcol[:], 0.0))
            pool.memset(mcol[:, CHUNK:P], MASKED).then_inc(masks_ok, 1)
            pool.memset(ones[:], 1.0).then_inc(masks_ok, 1)
            link(pool.memset(before[:], 1.0))
            pool.affine_select(out=before[:], in_=before[:], compare_op=ALU.is_gt, fill=0.0, base=0,
                               pattern=[[1, P]], channel_multiplier=-1).then_inc(masks_ok, 1)
            arrived(pool, PC_C + 1)
            kr = piece(PC_C + 1)[:, :, P:P + ROPE]
            for r in range(2):
                pool.tensor_copy(wkr[:, :, 0, ROPE * r:ROPE * (r + 1)], kr).then_inc(wkr_ok, 1)
                pool.tensor_copy(wkr[:, :, 1, ROPE * r:ROPE * r + HR], kr[:, :, HR:ROPE]).then_inc(wkr_ok, 1)
                pool.tensor_copy(wkr[:, :, 1, ROPE * r + HR:ROPE * (r + 1)], kr[:, :, 0:HR]).then_inc(wkr_ok, 1)
            for half in range(2):
                arrived(pool, PC_UQ + half)
                if half:
                    pool.wait_ge(qkD_mm, 4)
                wq = piece(PC_UQ + half).rearrange("p k (h c) -> p k h c", c=QW)[:, :, :, NOPE:QW]
                pool.tensor_copy(wpe[:], wq).then_inc(wpe_ok, 1)
                pool.tensor_copy(wpes[:, :, :, 0:HR], wq[:, :, :, HR:ROPE]).then_inc(wpe_ok, 1)
                pool.tensor_copy(wpes[:, :, :, HR:ROPE], wq[:, :, :, 0:HR]).then_inc(wpe_ok, 1)
                if half == 0:
                    pool.wait_ge(kr_mul, 2)
                    pool.tensor_tensor(kpe[:], ropeA[:], ropeB[:], ALU.add).then_inc(kpe_ok, 1)
                for j in range(2 * half, 2 * half + 2):
                    pool.wait_ge(qkD_sb, 2 * j + 2)
                    pool.tensor_tensor(qpe[:, j], ropeA[:], ropeB[:], ALU.add).then_inc(pe_add, 1)
            pool.wait_ge(o_sb, NH)
            link(pool.memset(fill[:], EMPTY))
            pool.dma_start(tab_dram.rearrange("(p n) a -> p (n a)", p=P), fill[:]).then_inc(fill_out, 16)
            pool.iota(aid[:], pattern=[[S, 2], [P, NT]], base=0, channel_multiplier=1).then_inc(aid_ok, 1)
            for g in range(NG):
                pool.wait_ge(sp_sb, g + 1)
                pool.wait_ge(u_sb, g + 1)
                pool.tensor_tensor(uT[:, g], uT[:, g], tmp[g % 2][:], ALU.mult).then_inc(y_ok, 1)
            for c in range(ND):
                pool.wait_ge(gp_sb, c + 1)
                pool.tensor_tensor(merged[:, c], merged[:, c], tmp[c % 2][:], ALU.add).then_inc(mg_ok, 1)
            pool.wait_ge(gp_mm, ND)
            pool.iota(iota_e[:], pattern=[[0, NT], [1, NE]], base=0, channel_multiplier=0,
                      allow_small_or_imprecise_dtypes=True).then_inc(iota_ok, 1)
            pool.wait_ge(fill_out, 16)
            pool.wait_ge(aid_ok, 1)
            pool.wait_ge(dst_ok, 1)
            for k in range(2):
                for t in range(NT):
                    pool.indirect_dma_start(
                        out=tab_dram[:, :], out_offset=bass.IndirectOffsetOnAxis(ap=dst_i[:, k, t:t + 1], axis=0),
                        in_=aid[:, k, t:t + 1], in_offset=None,
                        bounds_check=S * NE - 1, oob_is_err=False).then_inc(slots_out, 16)
            pool.wait_ge(slots_out, 16 * 2 * NT)
            pool.dma_start(tabs[:], tab_dram.rearrange("(b c e) a -> c b (e a)", b=NBLK, c=CAP)).then_inc(tab_in, 16)
            pool.wait_ge(toks_ok, 1)
            pool.wait_ge(hn_out, 16 * NT)
            pool.wait_ge(m_mm, 2 * NT)

            def gather(e, u, i):
                b, n = u % 2, i * 2 + u // 2
                past(pool, xg_in[b], 16 * n)
                pool.tensor_copy(idx_x[b][:], toks[:, 0, bass.ds(e, 1)]).then_inc(ix_ok, 1)
                pool.wait_ge(ix_ok, e + 1)
                past(pool, xt_mm, e - 1)
                pool.sem_inc(dma_go, 1)
                pool.indirect_dma_start(out=xg[b][0:CAP, :], out_offset=None, in_=m_dram[:, :],
                                        in_offset=bass.IndirectOffsetOnAxis(ap=idx_x[b][:], axis=0),
                                        bounds_check=last_row, oob_is_err=False).then_inc(xg_in[b], 16)

            def scatter(e, u, i):
                b, n = u % 2, i * 2 + u // 2
                past(pool, y_out[b], 16 * n)
                pool.tensor_copy(idx_y[b][:], tabs[:, 0, bass.ds(e, 1)]).then_inc(iy_ok, 1)
                pool.wait_ge(iy_ok, e + 1)
                pool.wait_ge(ya_sb, e + 1)
                pool.wait_ge(yb2_sb, e + 1)
                pool.sem_inc(dma_go, 1)
                pool.indirect_dma_start(out=y_dram[:, :],
                                        out_offset=bass.IndirectOffsetOnAxis(ap=idx_y[b][:], axis=0),
                                        in_=ysb[b][0:CAP, :], in_offset=None,
                                        bounds_check=last_result, oob_is_err=False).then_inc(y_out[b], 16)

            last_row, last_result = pool.to_reg(S - 1), pool.to_reg(2 * S - 1)
            LAG = 3
            for u in range(NBUF):
                gather(u, u, 0)
                if u >= LAG:
                    scatter(u - LAG, u - LAG, 0)
            with pool.Fori(1, NE // NBUF) as i:
                for u in range(NBUF):
                    gather(i * NBUF + u, u, i)
                    if u >= LAG:
                        scatter(i * NBUF + u - LAG, u - LAG, i)
                    else:
                        scatter(i * NBUF + u - LAG, u - LAG + NBUF, i - 1)
            last = NE // NBUF - 1
            for e in range(NE - LAG, NE):
                scatter(e, e % NBUF, last)
            for b in range(2):
                pool.wait_ge(y_out[b], 16 * NE // 2)
            most_v = pool.value_load(most_i[0:1, 0:1], min_val=0, max_val=S)
            with pool.If(most_v > CAP):
                pool.sem_inc(block_free, 1)
                with pool.Fori(1, NBLK) as b:
                    with pool.Fori(0, NE) as e:
                        step = (b - 1) * NE + e
                        n = b * NE + e
                        pool.tensor_copy(idx_x[0][:], toks[:].rearrange("c b e -> c (b e)")[:, bass.ds(n, 1)])\
                            .then_inc(ix_ok, 1)
                        pool.tensor_copy(idx_y[0][:], tabs[:].rearrange("c b e -> c (b e)")[:, bass.ds(n, 1)])\
                            .then_inc(iy_ok, 1)
                        pool.wait_ge(ix_ok, n + 1)
                        pool.wait_ge(iy_ok, n + 1)
                        pool.sem_inc(dma_go, 1)
                        pool.indirect_dma_start(out=xg[0][0:CAP, :], out_offset=None, in_=m_dram[:, :],
                                                in_offset=bass.IndirectOffsetOnAxis(ap=idx_x[0][:], axis=0),
                                                bounds_check=last_row, oob_is_err=False).then_inc(xg_in[0], 16)
                        pool.wait_ge(ya_sb, n + 1)
                        pool.wait_ge(yb2_sb, n + 1)
                        pool.sem_inc(dma_go, 1)
                        pool.indirect_dma_start(out=y_dram[:, :],
                                                out_offset=bass.IndirectOffsetOnAxis(ap=idx_y[0][:], axis=0),
                                                in_=ysb[0][0:CAP, :], in_offset=None,
                                                bounds_check=last_result, oob_is_err=False).then_inc(y_out[0], 16)
                        pool.wait_ge(y_out[0], step * 16 + (16 * NE // 2 + 16))
                        pool.sem_inc(block_free, 1)
            pool.sem_inc(moe_done, 1)

        @block.scalar
        def _(act):
            for t in range(NT):
                act.dma_start(xs[:, t], x[0, P * t:P * (t + 1), :]).then_inc(x_in[t], 16)
                if t == 0:
                    act.dma_start(wsn[:], w_spatial[0].rearrange("g t s -> t g s")).then_inc(ws_in, 16)
            with nc.allow_non_contiguous_dma(reason="gains, one per partition"):
                act.dma_start(gmx[:], g_mix[0].rearrange("(k p) -> p k", p=P)).then_inc(consts_in, 16)
                act.dma_start(gcq[:], g_cq[0].rearrange("(k p) -> p k", p=P)).then_inc(consts_in, 16)
                act.dma_start(gckv[:], g_ckv[0].rearrange("(k p) -> p k", p=P)).then_inc(consts_in, 16)
                act.dma_start(gvg[:], g_gv[0].rearrange("(k p) -> p k", p=P)).then_inc(consts_in, 16)
            act.dma_start(gmo[:], g_moe[0].rearrange("(p k) -> p k", p=P)).then_inc(consts_in, 16)
            act.dma_start(gpl[:], g_ple[0].rearrange("(p k) -> p k", p=P)).then_inc(consts_in, 16)
            act.dma_start(cosT[:], cos_t).then_inc(rope_in, 16)
            act.dma_start(sinT[:], sin_t).then_inc(rope_in, 16)
            act.dma_start(bsp[:], b_spatial[0:1].to_broadcast([P, NG, P])).then_inc(bias_in, 16)
            act.dma_start(brg[:], b_router_g[0:1, :].to_broadcast([P, NGRP])).then_inc(bias_in, 16)
            act.dma_start(bre[:], b_router_e[0:1].to_broadcast([P, NGRP, EPG])).then_inc(bias_in, 16)

            act.wait_ge(ident_ok, 1)

            def row_root(src, trash, n, t, root):
                act.activation(trash, src, ACT.Square, scale=float(D) ** -0.5,
                               accum_out=stat[:, n:n + 1]).then_inc(root, 1)
                act.wait_ge(root, 2 * t + 1)
                act.activation(rstd[:, n:n + 1], stat[:, n:n + 1], ACT.Sqrt, bias=eps[:]).then_inc(root, 1)

            for t in range(NT):
                act.wait_ge(x_in[t], 16)
                row_root(xs[:, t], junk[:], t, t, x_root)
            for b in range(3):
                act.wait_ge(ws_mm, b + 1)
                act.activation(wsT[:, 4 * b:4 * b + 4].rearrange("p g t -> p (g t)"), bank[b][:], ACT.Copy)\
                    .then_inc(ws_sb, 1)
            for c in range(5):
                act.wait_ge(c_sb, c + 1)
                act.activation(csq[:, c], cT[:, c], ACT.Square).then_inc(c_sq, 1)
            for n in range(2):
                act.wait_ge(c_ms, n + 1)
                act.activation(ropeA[:] if n == 0 else ropeB[:], rbc[:, n], ACT.Sqrt, bias=eps[:]).then_inc(c_rt, 1)
            for a in range(16):
                act.wait_ge(qkA_mm, a + 1)
                dst = qn[:, a] if a < NH else kn[:, a - NH]
                act.activation(dst, bank[1 + a % 4][:], ACT.Copy).then_inc(qkA_sb, 1)

            def softmax_exp(hd):
                for i in range(NT):
                    if i == 0:
                        act.wait_ge(s_neg, hd + 1)
                        past(act, pt_mm, hd - 1)
                    act.activation(pr[hd % 2][:, p_off[i]:p_off[i] + P * (i + 1)], scores(i), ACT.Exp,
                                   bias=mx[:, hd % 2, i:i + 1], scale=SCALE,
                                   accum_out=rs[:, hd % 2, i:i + 1]).then_inc(s_exp, 1)

            def probs_out(hd):
                act.wait_ge(pt_mm, hd + 1)
                past(act, o_mm, hd - 1)
                for j in range(NT):
                    act.activation(prT[hd % 2][:, t_off[j]:t_off[j] + P * (NT - j)], turned(j), ACT.Copy)\
                        .then_inc(pt_sb, 1)
                act.wait_ge(o_mm, hd + 1)
                act.activation(qn[:, hd], bank[6 + hd % 2][:], ACT.Copy).then_inc(o_sb, 1)

            softmax_exp(0)
            for hd in range(NH):
                if hd + 1 < NH:
                    softmax_exp(hd + 1)
                probs_out(hd)
            for c in range(ND):
                act.wait_ge(gb_mm, c + 1)
                act.activation(sigB[:, c], bank[c][:], ACT.Sigmoid).then_inc(gb_sb, 1)
            for g in range(12):
                act.wait_ge(v_mm, g + 1)
                act.activation(vt[:, g % 4, 512 * (g // 4):512 * (g // 4 + 1)], bank[g % 8][:],
                               ACT.Gelu_apprx_tanh).then_inc(v_sb, 1)
            act.wait_ge(v_var, NT)
            act.activation(vrs[:], bag[:, :, 1], ACT.Sqrt, bias=eps[:]).then_inc(v_rt, 1)
            act.wait_ge(fill_out, 16)
            for c in range(NG):
                act.wait_ge(u_mm, c + 1)
                act.activation(uT[:, c], bank[(4 + c) % 8][:], ACT.Gelu_apprx_tanh).then_inc(u_sb, 1)
            act.wait_ge(sp_mm, NG)
            act.dma_start(h[:], x[0].rearrange("(t p) d -> p t d", p=P)).then_inc(x_again, 16)
            act.dma_start(psb[:], p[0, 0].rearrange("(t p) d -> p t d", p=P)).then_inc(p_in, 16)
            for c in range(ND):
                act.wait_ge(ga_mm, c + 1)
                act.activation(sigA[:, c], bank[(4 + c) % 8][:], ACT.Sigmoid).then_inc(ga_sb, 1)
            act.wait_ge(gp_mm, ND)
            act.dma_start(wpp[:], w_ple_proj[0].rearrange("(k p) n -> p k n", p=P)).then_inc(wpp_in, 16)
            act.wait_ge(mg_ok, ND)
            with nc.allow_non_contiguous_dma(reason="the router's rows"):
                act.dma_start(wr[:, :, 0:NGRP], w_router_g[0].rearrange("(p k) n -> p k n", p=P)).then_inc(wr_in, 16)
                act.dma_start(wr[:, :, NGRP:NGRP + NE], w_router_e[0].rearrange("(p k) n -> p k n", p=P))\
                    .then_inc(wr_in, 16)
            for k in range(2):
                act.wait_ge(pt2_mm, k + 1)
                act.activation(pT[:, k], bank[4 + k][:], ACT.Copy).then_inc(pt2_sb, 1)

            def pp_out(g):
                act.wait_ge(pp_mm, g + 1)
                act.activation(pp[:, g // 2, 512 * (g % 2):512 * (g % 2 + 1)], bank[(6 + g) % 8 if g < 4 else g][:],
                               ACT.Copy).then_inc(pp_sb, 1)

            for g in range(4):
                pp_out(g)
            for t in range(NT):
                act.wait_ge(h_ok, t + 1)
                row_root(h[:, t], mT[:].rearrange("p k s -> p (k s)")[:, 0:D], NT + t, t, h_root)
            for t in range(NT):
                act.wait_ge(hn_ok, t + 1)
                act.dma_start(m_dram[P * t:P * (t + 1), :], hn[:, t]).then_inc(hn_out, 16)
            for s in range(2):
                act.wait_ge(rt_sub, s + 1)
                act.activation(r8[1 + s][:], r8[1 + s][:], ACT.Exp).then_inc(rt_exp, 1)
            for g in range(4, 8):
                pp_out(g)
            act.dma_start(gfin[:], g_final.rearrange("(a d) -> a d", a=1).to_broadcast([P, D])).then_inc(gfin_in, 16)

            def silu_step(e, u):
                act.wait_ge(gu_mm, e + 1)
                past(act, h_mul, e - 1)
                act.activation(sg[u % 2][0:CAP], bank[2 + u % 2][0:CAP, 0:FE], ACT.Silu).then_inc(silu, 1)

            def hidden_out(e, u):
                act.wait_ge(ht_mm, e + 1)
                past(act, y_mm, e - 1)
                act.activation(hT[u % 2][:, :, 0:CAP],
                               bank[4 + u % 2][:, 0:2 * CAP].rearrange("p (j c) -> p j c", j=2), ACT.Copy)\
                    .then_inc(ht_sb, 1)

            def result_out(e, u, i):
                act.wait_ge(y_mm, e + 1)
                past(act, y_out[u % 2], 16 * (i * 2 + u // 2))
                act.activation(ysb[u % 2][0:CAP, 0:512], bank[6][0:CAP, :], ACT.Copy).then_inc(ya_sb, 1)

            def prior(i, u):
                return (i, u - 1) if u else (i - 1, NBUF - 1)

            for u in range(NBUF):
                silu_step(u, u)
                if u:
                    hidden_out(u - 1, u - 1)
                    result_out(u - 1, u - 1, 0)
            with act.Fori(1, NE // NBUF) as i:
                for u in range(NBUF):
                    e = i * NBUF + u
                    silu_step(e, u)
                    pi, pu = prior(i, u)
                    hidden_out(e - 1, pu)
                    result_out(e - 1, pu, pi)
            hidden_out(NE - 1, NBUF - 1)
            result_out(NE - 1, NBUF - 1, NE // NBUF - 1)
            most_v = act.value_load(most_i[0:1, 0:1], min_val=0, max_val=S)
            with act.If(most_v > CAP):
                with act.Fori(1, NBLK) as b:
                    with act.Fori(0, NE) as e:
                        step = (b - 1) * NE + e
                        n = b * NE + e
                        act.wait_ge(gu_mm, n + 1)
                        act.activation(sg[0][0:CAP], bank[2][0:CAP, 0:FE], ACT.Silu).then_inc(silu, 1)
                        act.wait_ge(ht_mm, n + 1)
                        act.activation(hT[0][:, :, 0:CAP],
                                       bank[4][:, 0:2 * CAP].rearrange("p (j c) -> p j c", j=2), ACT.Copy)\
                            .then_inc(ht_sb, 1)
                        act.wait_ge(y_mm, n + 1)
                        act.activation(ysb[0][0:CAP, 0:512], bank[6][0:CAP, :], ACT.Copy).then_inc(ya_sb, 1)
            for t in range(NT):
                act.wait_ge(h2_ok, t + 1)
                row_root(h[:, t], fin[:, t], 2 * NT + t, t, h2_root)
            for t in range(NT):
                act.wait_ge(g_mm, t + 1)
                act.wait_ge(h2_ok, t + 1)
                for half in range(2):
                    act.activation(sgt[:, t, 512 * half:512 * (half + 1)], bank[4 + 2 * (t % 2) + half][:],
                                   ACT.Sigmoid).then_inc(g_sb, 1)
                act.wait_ge(h3_ok, t + 1)
                act.activation(fin[:, t], h[:, t], ACT.Square, scale=float(D) ** -0.5,
                               accum_out=stat[:, t:t + 1]).then_inc(h3_root, 1)
            act.wait_ge(h3_root, NT)
            act.activation(rstd[:, 0:NT], stat[:, 0:NT], ACT.Sqrt, bias=eps[:]).then_inc(h3_root, 1)

        @block.vector
        def _(dve):
            steps = [0]

            def link(ins):
                steps[0] += 1
                ins.then_inc(dv_step, 1)
                dve.wait_ge(dv_step, steps[0])

            def invert(y, v, w):
                link(dve.reciprocal(y, y))
                link(dve.scalar_tensor_tensor(w, v, EPS, y, ALU.add, ALU.mult))
                link(dve.scalar_tensor_tensor(w, w, -0.5, y, ALU.mult, ALU.mult))
                link(dve.scalar_tensor_tensor(y, w, 1.5, y, ALU.add, ALU.mult))

            def inv_rms(n, count=1):
                invert(rstd[:, n:n + count], stat[:, n:n + count], rnt[:, 0:count])

            def gain_out(dst, b, g, half):
                return dve.tensor_tensor(dst, bank[b][:].rearrange("p (k s) -> p k s", k=4),
                                         g[:, 4 * half:4 * half + 4].unsqueeze(2).to_broadcast([P, 4, P]), ALU.mult)

            for t in range(NT):
                dve.wait_ge(x_root, 2 * t + 2)
                inv_rms(t)
                dve.tensor_scalar(xn[:, t], xs[:, t], rstd[:, t:t + 1], None, ALU.mult).then_inc(xn_ok, 1)
            dve.wait_ge(consts_in, 16 * 6)
            for t in range(NT):
                for half in range(2):
                    dve.wait_ge(x_mm, 2 * t + half + 1)
                    gain_out(aT[:, 4 * half:4 * half + 4, P * t:P * (t + 1)], (3 + 2 * t + half) % 8, gmx, half)\
                        .then_inc(aT_ok, 1)
            dve.wait_ge(ws_sb, 3)
            dve.memset(wsT[CHUNK:P, :, 0:CHUNK], 0.0).then_inc(ws_zero, 1)
            for c in range(5):
                dve.wait_ge(c_mm, c + 1)
                dve.tensor_copy(cT[:, c], bank[c][:]).then_inc(c_sb, 1)
            for n, (b, w) in enumerate(((5, QL), (6, KVL))):
                dve.wait_ge(ss_mm, n + 1)
                dve.tensor_scalar(rbc[:, n], bank[b][:], 1.0 / w, None, ALU.mult).then_inc(c_ms, 1)
            for n in range(2):
                root = (ropeA, ropeB)[n]
                dve.wait_ge(c_rt, n + 1)
                invert(root[:], rbc[:, n], csq[:, n])
            dve.wait_ge(c_sb, 5)
            for c in range(5):
                g = gcq[:, c:c + 1] if c < 3 else gckv[:, c - 3:c - 2]
                dve.scalar_tensor_tensor(cT[:, c], cT[:, c], g, (ropeA if c < 3 else ropeB)[:], ALU.mult, ALU.mult)\
                    .then_inc(cT_ok, 1)
            dve.wait_ge(cT_ok, 5)
            dve.wait_ge(rope_in, 32)
            dve.wait_ge(kr_mm, 1)
            dve.tensor_tensor(ropeA[:], bank[7][:], cosT[:], ALU.mult).then_inc(kr_mul, 1)
            dve.wait_ge(kr_mm, 2)
            dve.tensor_tensor(ropeB[:], bank[0][:], sinT[:], ALU.mult).then_inc(kr_mul, 1)
            DB = [5, 6, 7, 0]
            for d in range(16):
                dve.wait_ge(qkD_mm, d + 1)
                if d < 8:
                    if d % 2 == 0:
                        dve.wait_ge(kpe_ok, 1)
                        past(dve, pe_add, d // 2)
                    dve.tensor_tensor((ropeA, ropeB)[d % 2][:], bank[DB[d % 4]][:], (cosT, sinT)[d % 2][:], ALU.mult)\
                        .then_inc(qkD_sb, 1)
                else:
                    t, q = (d - 8) // 2, (d - 8) % 2
                    dve.tensor_copy(vv[:, t, 4 * q:4 * q + 4].rearrange("p h v -> p (h v)"), bank[DB[d % 4]][:])\
                        .then_inc(qkD_sb, 1)

            def maxima(hd):
                past(dve, s_exp, NT * (hd - 1))
                for i in s_order:
                    dve.wait_ge(s_mm, NT * hd + s_ready[i])
                    dve.tensor_reduce(mx[:, hd % 2, i:i + 1], scores(i), AX_X, ALU.max).then_inc(s_max, 1)
                dve.wait_ge(s_max, NT * (hd + 1))
                dve.tensor_scalar(mx[:, hd % 2], mx[:, hd % 2], -SCALE, None, ALU.mult).then_inc(s_neg, 1)

            def normalise(hd):
                dve.wait_ge(s_exp, NT * (hd + 1))
                dve.reciprocal(ri[:, hd % 2], rs[:, hd % 2]).then_inc(s_rec, 1)
                dve.wait_ge(s_rec, hd + 1)
                for i in range(NT):
                    v = pr[hd % 2][:, p_off[i]:p_off[i] + P * (i + 1)]
                    dve.tensor_scalar(v, v, ri[:, hd % 2, i:i + 1], None, ALU.mult).then_inc(p_ok, 1)

            maxima(0)
            for hd in range(NH):
                normalise(hd)
                if hd + 1 < NH:
                    maxima(hd + 1)
            for c in range(ND):
                dve.wait_ge(yb_mm, c + 1)
                dve.wait_ge(gb_sb, c + 1)
                dve.tensor_tensor(merged[:, c], bank[c][:], sigB[:, c], ALU.mult).then_inc(yb_sb, 1)
            for g in range(12):
                dve.wait_ge(v_sb, g + 1)
                link(dve.bn_stats(bst[:, g % 4, g // 4], vt[:, g % 4, 512 * (g // 4):512 * (g // 4 + 1)]))
            for t in range(NT):
                dve.bn_aggr(bag[:, t], bst[:, t].rearrange("p a b -> p (a b)")).then_inc(v_var, 1)
            dve.wait_ge(v_rt, 1)
            invert(vrs[:], bag[:, :, 1], rnt[:])
            for t in range(NT):
                dve.tensor_scalar(vt[:, t], vt[:, t], bag[:, t, 0:1], vrs[:, t:t + 1], ALU.subtract, ALU.mult)\
                    .then_inc(v_ln, 1)
            dve.wait_ge(bias_in, 48)
            for g in range(NG):
                dve.wait_ge(sp_mm, g + 1)
                past(dve, y_ok, g - 1)
                dve.scalar_tensor_tensor(tmp[g % 2][:].rearrange("p (n t) -> p n t", n=NT),
                                         bank[g % 8][:].rearrange("p (n t) -> p n t", n=NT), gvg[:, g:g + 1],
                                         bsp[:, g].unsqueeze(1).to_broadcast([P, NT, P]), ALU.mult, ALU.add)\
                    .then_inc(sp_sb, 1)
            dve.wait_ge(y_ok, NG)
            for c in range(ND):
                dve.wait_ge(gp_mm, c + 1)
                dve.wait_ge(ga_sb, c + 1)
                past(dve, mg_ok, c - 1)
                dve.tensor_tensor(tmp[c % 2][:], bank[(4 + c) % 8][:], sigA[:, c], ALU.mult).then_inc(gp_sb, 1)
            dve.wait_ge(x_again, 16)
            for g in range(2 * NT):
                t, half = g % NT, g // NT
                dve.wait_ge(w_mm, g + 1)
                hs = h[:, t, 512 * half:512 * (half + 1)]
                ins = dve.tensor_tensor(hs, hs, bank[(4 + g) % 8][:], ALU.add)
                if half == 0:
                    ins.then_inc(w_sb, 1)
                else:
                    ins.then_inc(h_ok, 1)
            for t in range(NT):
                dve.wait_ge(h_root, 2 * t + 2)
                inv_rms(NT + t)
                dve.tensor_scalar(hn[:, t], h[:, t], rstd[:, NT + t:NT + t + 1], None, ALU.mult).then_inc(hn_ok, 1)
            MB = [2, 3, 4, 5, 6, 7, 0, 1]
            for t in range(NT):
                for half in range(2):
                    dve.wait_ge(m_mm, 2 * t + half + 1)
                    gain_out(mT[:, 4 * half:4 * half + 4, P * t:P * (t + 1)], MB[2 * t + half], gmo, half)\
                        .then_inc(mT_ok, 1)

            grp, prob, eprob, score, cand, oh1, oh2, esel = r8
            m1, s1, i1, gw, p1, p2, ps, d1 = r1[:8]

            def bc8(v):
                return v[:].unsqueeze(2).to_broadcast([P, NT, EPG])

            def bct(v):
                return v[:].unsqueeze(1).to_broadcast([P, NT, EPG])

            def softmax8(src, dst, n):
                link(dve.tensor_reduce(m1[:], src, AX_X, ALU.max))
                dve.tensor_tensor(dst[:], src, bc8(m1), ALU.subtract).then_inc(rt_sub, 1)
                dve.wait_ge(rt_exp, n + 1)
                link(dve.tensor_reduce(s1[:], dst[:], AX_X, ALU.add))
                link(dve.reciprocal(s1[:], s1[:]))
                link(dve.tensor_tensor(dst[:], dst[:], bc8(s1), ALU.mult))

            def first_max(src, onehot):
                link(dve.tensor_reduce(m1[:], src[:], AX_X, ALU.max))
                link(dve.tensor_tensor(cand[:], src[:], bc8(m1), ALU.is_equal))
                link(dve.scalar_tensor_tensor(cand[:], cand[:], float(-EPG), bct(iota8up), ALU.mult, ALU.add))
                link(dve.tensor_reduce(i1[:], cand[:], AX_X, ALU.min))
                link(dve.tensor_tensor(onehot[:], bct(iota8), bc8(i1), ALU.is_equal))

            link(dve.memset(iota8[:, 0:1], 0.0))
            for k in range(1, EPG):
                link(dve.memset(iota8[:, k:k + 1], float(k)))
            link(dve.tensor_scalar(iota8up[:], iota8[:], float(EPG), None, ALU.add))
            dve.wait_ge(lg_mm, 1)
            link(dve.tensor_copy(lg[:], bank[2][:, 0:NT * (NGRP + NE)].rearrange("p (t n) -> p t n", t=NT)))
            softmax8(lg[:, :, 0:NGRP], prob, 0)
            link(dve.tensor_tensor(score[:], prob[:], bct(brg), ALU.add))
            first_max(score, grp)
            link(dve.tensor_tensor(score[:], prob[:], grp[:], ALU.mult))
            link(dve.tensor_reduce(gw[:], score[:], AX_X, ALU.add))

            def choose(src):
                for t in range(NT):
                    ins = dve.tensor_tensor(rt_e[:, t], src(t), grp[:, t].unsqueeze(2).to_broadcast([P, NGRP, EPG]),
                                            ALU.mult)
                link(ins)
                link(dve.tensor_reduce(esel[:], rt_e[:].rearrange("p t g e -> p t e g"), AX_X, ALU.add))

            choose(lambda t: lg[:, t, NGRP:NGRP + NE].rearrange("p (g e) -> p g e", g=NGRP))
            softmax8(esel[:], eprob, 1)
            choose(lambda t: bre[:])
            link(dve.tensor_tensor(score[:], eprob[:], esel[:], ALU.add))
            first_max(score, oh1)
            link(dve.scalar_tensor_tensor(score[:], oh1[:], MASKED, score[:], ALU.mult, ALU.add))
            first_max(score, oh2)
            for oh, s4 in ((oh1, sel1), (oh2, sel2)):
                for t in range(NT):
                    ins = dve.tensor_tensor(s4[:, t], grp[:, t].unsqueeze(2).to_broadcast([P, NGRP, EPG]),
                                            oh[:, t].unsqueeze(1).to_broadcast([P, NGRP, EPG]), ALU.mult)
            link(ins)
            flat = "p t g e -> p t (g e)"
            dve.tensor_tensor(sel[:], sel1[:].rearrange(flat), sel2[:].rearrange(flat), ALU.add).then_inc(sel_ok, 1)
            for oh, pk in ((oh1, p1), (oh2, p2)):
                link(dve.tensor_tensor(cand[:], oh[:], eprob[:], ALU.mult))
                link(dve.tensor_reduce(pk[:], cand[:], AX_X, ALU.add))
            link(dve.tensor_tensor(ps[:], p1[:], p2[:], ALU.add))
            link(dve.reciprocal(ps[:], ps[:]))
            link(dve.tensor_tensor(ps[:], ps[:], gw[:], ALU.mult))
            link(dve.tensor_tensor(wts[:, 0], p1[:], ps[:], ALU.mult))
            link(dve.tensor_tensor(wts[:, 1], p2[:], ps[:], ALU.mult))
            dve.wait_ge(iota_ok, 1)
            dve.wait_ge(rank_mm, 1)
            link(dve.scalar_tensor_tensor(adr[:], bank[3][:, 0:NT * NE].rearrange("p (t e) -> p t e", t=NT), float(NE),
                                          iota_e[:], ALU.mult, ALU.add))
            for k, s4 in enumerate((sel1, sel2)):
                link(dve.tensor_tensor(rt_e[:].rearrange(flat), s4[:].rearrange(flat), adr[:], ALU.mult))
                link(dve.tensor_reduce(d1[:], rt_e[:].rearrange(flat), AX_X, ALU.add))
                link(dve.tensor_copy(dst_i[:, k], d1[:]))
            dve.tensor_reduce(most[:], bank[3][0:1, NT * NE:NT * NE + NE], AX_X, ALU.max).then_inc(dst_ok, 1)
            dve.wait_ge(dst_ok, 1)
            dve.tensor_copy(most_i[:], most[:]).then_inc(most_ok, 1)
            dve.wait_ge(tab_in, 16)
            dve.tensor_scalar(toks[:], tabs[:], TOKEN_BITS, None, ALU.bitwise_and).then_inc(toks_ok, 1)

            def rows_out(e, u):
                dve.wait_ge(xt_mm, e + 1)
                past(dve, gu_mm, e - 1)
                for half in range(2):
                    ins = dve.tensor_tensor(
                        xgT[u % 2][:, 4 * half:4 * half + 4, 0:CAP],
                        bank[half][:, 0:4 * CAP].rearrange("p (k c) -> p k c", k=4),
                        gmo[:, 4 * half:4 * half + 4].unsqueeze(2).to_broadcast([P, 4, CAP]), ALU.mult)
                ins.then_inc(xt_sb, 1)

            def gated(e, u):
                dve.wait_ge(silu, e + 1)
                past(dve, ht_mm, e - 1)
                dve.tensor_tensor(hm[u % 2][0:CAP], sg[u % 2][0:CAP], bank[2 + u % 2][0:CAP, FE:2 * FE], ALU.mult)\
                    .then_inc(h_mul, 1)

            def result_out(e, u, i):
                dve.wait_ge(y_mm, e + 1)
                past(dve, y_out[u % 2], 16 * (i * 2 + u // 2))
                dve.tensor_copy(ysb[u % 2][0:CAP, 512:D], bank[7][0:CAP, :]).then_inc(yb2_sb, 1)

            rows_out(0, 0)
            for u in range(NBUF):
                rows_out(u + 1, (u + 1) % NBUF)
                gated(u, u)
                if u:
                    result_out(u - 1, u - 1, 0)
            with dve.Fori(1, NE // NBUF - 1) as i:
                for u in range(NBUF):
                    e = i * NBUF + u
                    rows_out(e + 1, (u + 1) % NBUF)
                    gated(e, u)
                    if u:
                        result_out(e - 1, u - 1, i)
                    else:
                        result_out(e - 1, NBUF - 1, i - 1)
            last = NE // NBUF - 1
            for e in range(NE - NBUF, NE):
                if e + 1 < NE:
                    rows_out(e + 1, (e + 1) % NBUF)
                gated(e, e % NBUF)
                result_out(e - 1, (e - 1) % NBUF, (e - 1) // NBUF)
            result_out(NE - 1, NBUF - 1, last)
            most_v = dve.value_load(most_i[0:1, 0:1], min_val=0, max_val=S)
            with dve.If(most_v > CAP):
                with dve.Fori(1, NBLK) as b:
                    with dve.Fori(0, NE) as e:
                        step = (b - 1) * NE + e
                        n = b * NE + e
                        dve.wait_ge(xt_mm, n + 1)
                        for half in range(2):
                            ins = dve.tensor_tensor(
                                xgT[0][:, 4 * half:4 * half + 4, 0:CAP],
                                bank[half][:, 0:4 * CAP].rearrange("p (k c) -> p k c", k=4),
                                gmo[:, 4 * half:4 * half + 4].unsqueeze(2).to_broadcast([P, 4, CAP]), ALU.mult)
                        ins.then_inc(xt_sb, 1)
                        dve.wait_ge(silu, n + 1)
                        dve.tensor_tensor(hm[0][0:CAP], sg[0][0:CAP], bank[2][0:CAP, FE:2 * FE], ALU.mult)\
                            .then_inc(h_mul, 1)
                        dve.wait_ge(y_mm, n + 1)
                        dve.tensor_copy(ysb[0][0:CAP, 512:D], bank[7][0:CAP, :]).then_inc(yb2_sb, 1)

            def third_norm(t):
                dve.wait_ge(h2_root, 2 * t + 2)
                inv_rms(2 * NT + t)
                dve.tensor_scalar(n3[:, t], h[:, t], rstd[:, 2 * NT + t:2 * NT + t + 1], None, ALU.mult)\
                    .then_inc(n3_ok, 1)

            def third_out(t):
                for half in range(2):
                    dve.wait_ge(n_mm, 2 * t + half + 1)
                    gain_out(n3T[:, 4 * half:4 * half + 4, P * t:P * (t + 1)], 2 * (t % 2) + half, gpl, half)\
                        .then_inc(n3T_ok, 1)

            for t in range(NT):
                dve.wait_ge(y_in[t], 32)
                link(dve.scalar_tensor_tensor(ysum[:, t % 2], y1[:, t], wts[:, 0, t:t + 1], h[:, t],
                                              ALU.mult, ALU.add))
                dve.scalar_tensor_tensor(h[:, t], y2[:, t], wts[:, 1, t:t + 1], ysum[:, t % 2], ALU.mult, ALU.add)\
                    .then_inc(h2_ok, 1)
                if t:
                    third_norm(t - 1)
            third_norm(NT - 1)
            dve.wait_ge(pp_sb, 8)
            dve.wait_ge(gfin_in, 16)
            third_out(0)
            for t in range(NT):
                if t + 1 < NT:
                    third_out(t + 1)
                dve.wait_ge(g_sb, 2 * t + 2)
                dve.tensor_tensor(sgt[:, t], sgt[:, t], pp[:, t], ALU.mult).then_inc(pg_ok, 1)
                dve.wait_ge(pg_ok, t + 1)
                dve.tensor_tensor(h[:, t], h[:, t], sgt[:, t], ALU.add).then_inc(h3_ok, 1)
            dve.wait_ge(h3_root, NT + 1)
            inv_rms(0, NT)
            for t in range(NT):
                dve.scalar_tensor_tensor(fin[:, t], h[:, t], rstd[:, t:t + 1], gfin[:], ALU.mult, ALU.mult)\
                    .then_inc(fin_ok, 1)

        @block.tensor
        def _(pe):
            def product(dst, pairs):
                for n, (l, r) in enumerate(pairs):
                    ins = pe.matmul(dst, l, r, start=(n == 0), stop=(n == len(pairs) - 1))
                return ins

            pe.wait_ge(ident_ok, 2)
            pe.wait_ge(ws_in, 16)
            for b in range(3):
                for g in range(4 * b, 4 * b + 4):
                    ins = pe.transpose(bank[b][:, P * (g % 4):P * (g % 4 + 1)], wsn[:, g], ident[:])
                ins.then_inc(ws_mm, 1)
            for t in range(NT):
                pe.wait_ge(xn_ok, t + 1)
                for half in range(2):
                    b = (3 + 2 * t + half) % 8
                    if b < 3:
                        pe.wait_ge(ws_sb, b + 1)
                    for k in range(4):
                        ins = pe.transpose(bank[b][:, P * k:P * (k + 1)],
                                           xn[:, t, P * (4 * half + k):P * (4 * half + k + 1)], ident[:])
                    ins.then_inc(x_mm, 1)
            pe.wait_ge(aT_ok, 2 * NT)

            arrived(pe, PC_C)
            for c in range(5):
                if c == 4:
                    arrived(pe, PC_C + 1)
                w = piece(PC_C)[:, :, P * c:P * (c + 1)] if c < 4 else piece(PC_C + 1)[:, :, 0:P]
                ins = product(bank[c][:], [(w[:, k], aT[:, k]) for k in range(ND)])
                ins.then_inc(c_mm, 1)
            pe.wait_ge(c_sq, 4)
            pe.sem_inc(piece_used, 1)
            pe.wait_ge(wkr_ok, 6)
            product(bank[7][:], [(wkr[:, k, 0], aT[:, k]) for k in range(ND)]).then_inc(kr_mm, 1)
            pe.wait_ge(masks_ok, 4)
            pe.wait_ge(c_sq, 5)
            product(bank[5][:], [(ones[:], csq[:, c]) for c in range(3)]).then_inc(ss_mm, 1)
            product(bank[6][:], [(ones[:], csq[:, c]) for c in range(3, 5)]).then_inc(ss_mm, 1)
            pe.wait_ge(c_sb, 1)
            product(bank[0][:], [(wkr[:, k, 1], aT[:, k]) for k in range(ND)]).then_inc(kr_mm, 1)
            pe.wait_ge(c_sq, 5)
            pe.sem_inc(piece_used, 1)

            pe.wait_ge(cT_ok, 5)
            DB = [5, 6, 7, 0]
            na, nd = [0], [0]

            def to_act(pairs):
                a = na[0]
                na[0] += 1
                past(pe, qkA_sb, a - 3)
                return product(bank[1 + a % 4][:], pairs)

            def to_dve(pairs):
                d = nd[0]
                nd[0] += 1
                if d == 2:
                    pe.wait_ge(kr_mul, 2)
                past(pe, qkD_sb, d - 3)
                return product(bank[DB[d % 4]][:], pairs)

            for half in range(2):
                arrived(pe, PC_UQ + half)
                w = piece(PC_UQ + half)
                for j in range(4):
                    to_act([(w[:, k, QW * j:QW * j + NOPE], cT[:, k]) for k in range(3)]).then_inc(qkA_mm, 1)
                pe.wait_ge(wpe_ok, 3 * half + 3)
                for j in range(2):
                    to_dve([(wpe[:, k, 2 * j:2 * j + 2].rearrange("p h c -> p (h c)"), cT[:, k]) for k in range(3)])\
                        .then_inc(qkD_mm, 1)
                    to_dve([(wpes[:, k, 2 * j:2 * j + 2].rearrange("p h c -> p (h c)"), cT[:, k]) for k in range(3)])\
                        .then_inc(qkD_mm, 1)
                pe.wait_ge(qkA_sb, 4 * half + 4)
                pe.sem_inc(piece_used, 1)
            arrived(pe, PC_UKV)
            w = piece(PC_UKV)
            for j in range(NH):
                to_act([(w[:, k, KVW * j:KVW * j + NOPE], cT[:, 3 + k]) for k in range(2)]).then_inc(qkA_mm, 1)
                t, q = j // 2, j % 2
                wv = w.rearrange("p k (h c) -> p k h c", c=KVW)[:, :, 4 * q:4 * q + 4, NOPE:KVW]
                ins = to_dve([(cT[:, 3 + k, P * t:P * (t + 1)], wv[:, k]) for k in range(2)])
                ins.then_inc(qkD_mm, 1)
            pe.wait_ge(qkA_sb, 16)
            pe.wait_ge(qkD_sb, 16)
            pe.sem_inc(piece_used, 1)
            pe.wait_ge(kpe_ok, 1)
            pe.wait_ge(pe_add, NH // 2)

            def head_scores(hd):
                past(pe, s_exp, NT * hd)
                r = ROPE * (hd % 2)
                for i in s_order:
                    o, kw = scores(i), P * (i + 1)
                    pe.matmul(o, qn[:, hd, P * i:P * (i + 1)], kn[:, hd, 0:kw], start=True, stop=False)
                    pe.matmul(o, qpe[r:r + ROPE, hd // 2, P * i:P * (i + 1)], kpe[r:r + ROPE, 0:kw],
                              start=False, stop=False)
                    pe.matmul(o[:, P * i:kw], mrow[:], mcol[:], start=False, stop=True).then_inc(s_mm, 1)

            def head_values(hd):
                pe.wait_ge(p_ok, NT * (hd + 1))
                past(pe, pt_sb, NT * hd)
                for j in range(NT):
                    for i in range(j, NT):
                        ins = pe.transpose(turned(j)[:, P * (i - j):P * (i - j + 1)],
                                           pr[hd % 2][:, p_off[i] + P * j:p_off[i] + P * (j + 1)], ident[:])
                ins.then_inc(pt_mm, 1)
                past(pe, o_sb, hd - 1)
                for j in range(NT):
                    pe.wait_ge(pt_sb, NT * hd + j + 1)
                    ins = pe.matmul(bank[6 + hd % 2][:, P * j:S], vv[:, j, hd],
                                    prT[hd % 2][:, t_off[j]:t_off[j] + P * (NT - j)], start=(j == 0), stop=(j == NT - 1))
                ins.then_inc(o_mm, 1)

            head_scores(0)
            for hd in range(NH):
                if hd + 1 < NH:
                    head_scores(hd + 1)
                head_values(hd)

            def feature_chunks(first, n_pieces, act_t, n_k, width, free, done):
                c = 0
                for j in range(n_pieces):
                    arrived(pe, first + j)
                    w = piece(first + j)
                    for cc in range(width // P):
                        b = free(c)
                        ins = product(bank[b][:], [(w[:, k, P * cc:P * (cc + 1)], act_t[:, k]) for k in range(n_k)])
                        ins.then_inc(done, 1)
                        c += 1
                    pe.wait_ge(done, c)
                    pe.sem_inc(piece_used, 1)

            def gb_bank(c):
                if c == 3:
                    pe.wait_ge(pt_sb, NT * NH)
                if c == 6:
                    pe.wait_ge(o_sb, NH)
                return c

            pe.wait_ge(s_exp, NT * NH)
            feature_chunks(PC_GB, 2, aT, ND, 512, gb_bank, gb_mm)

            def yb_bank(c):
                pe.wait_ge(gb_sb, c + 1)
                return c

            pe.wait_ge(o_sb, NH)
            feature_chunks(PC_O, 2, qn, NH, 512, yb_bank, yb_mm)

            for j in range(3):
                arrived(pe, PC_V + j)
                w = piece(PC_V + j)
                for t in range(NT):
                    g = NT * j + t
                    if g < 8:
                        pe.wait_ge(yb_sb, g + 1)
                    else:
                        pe.wait_ge(v_sb, g - 7)
                    product(bank[g % 8][:], [(aT[:, k, P * t:P * (t + 1)], w[:, k]) for k in range(ND)])\
                        .then_inc(v_mm, 1)
                pe.wait_ge(v_mm, NT * (j + 1))
                pe.sem_inc(piece_used, 1)

            def u_bank(c):
                if c < 8:
                    pe.wait_ge(v_sb, c + 5)
                else:
                    pe.wait_ge(u_sb, c - 7)
                return (4 + c) % 8

            feature_chunks(PC_U, 3, aT, ND, 512, u_bank, u_mm)

            pe.wait_ge(v_ln, NT)
            pe.wait_ge(ws_zero, 1)
            for g in range(NG):
                if g < 8:
                    pe.wait_ge(u_sb, g + 5)
                else:
                    pe.wait_ge(sp_sb, g - 7)
                for n in range(NT):
                    ins = pe.matmul(bank[g % 8][:, P * n:P * (n + 1)], vt[:, n, P * g:P * (g + 1)], wsT[:, g],
                                    start=True, stop=True)
                ins.then_inc(sp_mm, 1)

            def ga_bank(c):
                pe.wait_ge(sp_sb, c + 5)
                return (4 + c) % 8

            feature_chunks(PC_GA, 2, aT, ND, 512, ga_bank, ga_mm)

            def gp_bank(c):
                pe.wait_ge(ga_sb, c + 1)
                return (4 + c) % 8

            pe.wait_ge(y_ok, NG)
            feature_chunks(PC_GP, 4, uT, NG, 256, gp_bank, gp_mm)

            pe.wait_ge(mg_ok, ND)
            for j in range(2):
                arrived(pe, PC_W + j)
                w = piece(PC_W + j)
                for t in range(NT):
                    g = NT * j + t
                    pe.wait_ge(gp_sb, g + 1)
                    product(bank[(4 + g) % 8][:], [(merged[:, k, P * t:P * (t + 1)], w[:, k]) for k in range(ND)])\
                        .then_inc(w_mm, 1)
                pe.wait_ge(w_mm, NT * (j + 1))
                pe.sem_inc(piece_used, 1)

            pe.wait_ge(p_in, 16)
            pe.wait_ge(w_sb, 2)
            for k in range(2):
                for t in range(NT):
                    ins = pe.transpose(bank[4 + k][:, P * t:P * (t + 1)], psb[:, t, P * k:P * (k + 1)], ident[:])
                ins.then_inc(pt2_mm, 1)
            pe.wait_ge(pt2_sb, 2)
            pe.wait_ge(wpp_in, 16)

            def embed(g, b):
                t, half = g // 2, g % 2
                return product(bank[b][:], [(pT[:, k, P * t:P * (t + 1)], wpp[:, k, 512 * half:512 * (half + 1)])
                                            for k in range(2)])

            pe.wait_ge(w_sb, NT)
            pe.wait_ge(h_ok, 2)
            for g in range(4):
                embed(g, (6 + g) % 8).then_inc(pp_mm, 1)
            MB = [2, 3, 4, 5, 6, 7, 0, 1]
            pe.wait_ge(h_ok, NT)
            pe.wait_ge(pp_sb, 4)
            for t in range(NT):
                pe.wait_ge(hn_ok, t + 1)
                for half in range(2):
                    for k in range(4):
                        ins = pe.transpose(bank[MB[2 * t + half]][:, P * k:P * (k + 1)],
                                           hn[:, t, 4 * half + k:D:ND], ident[:])
                    ins.then_inc(m_mm, 1)
            pe.wait_ge(mT_ok, 2 * NT)
            pe.wait_ge(wr_in, 32)
            for t in range(NT):
                ins = product(bank[2][:, (NGRP + NE) * t:(NGRP + NE) * (t + 1)],
                              [(mT[:, k, P * t:P * (t + 1)], wr[:, k]) for k in range(ND)])
            ins.then_inc(lg_mm, 1)
            pe.wait_ge(sel_ok, 1)
            for t in range(NT):
                product(bank[3][:, NE * t:NE * (t + 1)],
                        [(ones[:], sel[:, s]) for s in range(t)] + [(before[:], sel[:, t])])
            product(bank[3][:, NE * NT:NE * (NT + 1)], [(ones[:], sel[:, s]) for s in range(NT)]).then_inc(rank_mm, 1)
            for g in range(4, 8):
                embed(g, g).then_inc(pp_mm, 1)

            def turn_rows(e, u, i):
                b = u % 2
                pe.wait_ge(xg_in[b], 16 * (i * 2 + u // 2 + 1))
                past(pe, xt_sb, e)
                for k in range(ND):
                    ins = pe.transpose(bank[k // 4][:, CAP * (k % 4):CAP * (k % 4 + 1)], xg[b][0:CAP, k:D:ND],
                                       ident[0:CAP, 0:CAP])
                ins.then_inc(xt_mm, 1)

            def gate_up(e, u, i):
                pe.wait_ge(xt_sb, e + 1)
                pe.wait_ge(gu_in[u], 32 * (i + 1))
                past(pe, h_mul, e - 1)
                product(bank[2 + u % 2][0:CAP, :], [(xgT[u % 2][:, k, 0:CAP], wgu[u][:, :, k]) for k in range(ND)])\
                    .then_inc(gu_mm, 1)

            def down(e, u, i):
                b = u % 2
                pe.wait_ge(h_mul, e + 1)
                past(pe, ht_sb, e - 1)
                for j in range(2):
                    ins = pe.transpose(bank[4 + b][:, CAP * j:CAP * (j + 1)], hm[b][0:CAP, j:FE:2],
                                       ident[0:CAP, 0:CAP])
                ins.then_inc(ht_mm, 1)
                pe.wait_ge(ht_sb, e + 1)
                pe.wait_ge(dn_in[u], 16 * (i + 1))
                past(pe, ya_sb, e)
                past(pe, yb2_sb, e)
                for half in range(2):
                    ins = product(bank[6 + half][0:CAP, :],
                                  [(hT[b][:, j, 0:CAP], wdn[u][:, j, 512 * half:512 * (half + 1)]) for j in range(2)])
                ins.then_inc(y_mm, 1)

            pe.wait_ge(pp_sb, 8)
            pe.wait_ge(most_ok, 1)
            turn_rows(0, 0, 0)
            for u in range(NBUF):
                turn_rows(u + 1, (u + 1) % NBUF, (u + 1) // NBUF)
                gate_up(u, u, 0)
                if u:
                    down(u - 1, u - 1, 0)
            with pe.Fori(1, NE // NBUF - 1) as i:
                for u in range(NBUF):
                    e = i * NBUF + u
                    if u + 1 < NBUF:
                        turn_rows(e + 1, u + 1, i)
                    else:
                        turn_rows(e + 1, 0, i + 1)
                    gate_up(e, u, i)
                    if u:
                        down(e - 1, u - 1, i)
                    else:
                        down(e - 1, NBUF - 1, i - 1)
            for e in range(NE - NBUF, NE):
                if e + 1 < NE:
                    turn_rows(e + 1, (e + 1) % NBUF, (e + 1) // NBUF)
                gate_up(e, e % NBUF, e // NBUF)
                down(e - 1, (e - 1) % NBUF, (e - 1) // NBUF)
            down(NE - 1, NBUF - 1, NE // NBUF - 1)
            most_v = pe.value_load(most_i[0:1, 0:1], min_val=0, max_val=S)
            with pe.If(most_v > CAP):
                with pe.Fori(1, NBLK) as b:
                    with pe.Fori(0, NE) as e:
                        step = (b - 1) * NE + e
                        n = b * NE + e
                        pe.wait_ge(xg_in[0], step * 16 + (16 * NE // 2 + 16))
                        for k in range(ND):
                            ins = pe.transpose(bank[k // 4][:, CAP * (k % 4):CAP * (k % 4 + 1)],
                                               xg[0][0:CAP, k:D:ND], ident[0:CAP, 0:CAP])
                        ins.then_inc(xt_mm, 1)
                        pe.wait_ge(xt_sb, n + 1)
                        pe.wait_ge(gu_in[0], step * 32 + (32 * NE // NBUF + 32))
                        pe.wait_ge(dn_in[0], step * 16 + (16 * NE // NBUF + 16))
                        product(bank[2][0:CAP, :], [(xgT[0][:, k, 0:CAP], wgu[0][:, :, k]) for k in range(ND)])\
                            .then_inc(gu_mm, 1)
                        pe.wait_ge(h_mul, n + 1)
                        for j in range(2):
                            ins = pe.transpose(bank[4][:, CAP * j:CAP * (j + 1)], hm[0][0:CAP, j:FE:2],
                                               ident[0:CAP, 0:CAP])
                        ins.then_inc(ht_mm, 1)
                        pe.wait_ge(ht_sb, n + 1)
                        for half in range(2):
                            ins = product(bank[6 + half][0:CAP, :],
                                          [(hT[0][:, j, 0:CAP], wdn[0][:, j, 512 * half:512 * (half + 1)])
                                           for j in range(2)])
                        ins.then_inc(y_mm, 1)

            def turn_third(t):
                pe.wait_ge(n3_ok, t + 1)
                for half in range(2):
                    past(pe, n3T_ok, 2 * t + half - 3)
                    for k in range(4):
                        ins = pe.transpose(bank[2 * (t % 2) + half][:, P * k:P * (k + 1)],
                                           n3[:, t, 4 * half + k:D:ND], ident[:])
                    ins.then_inc(n_mm, 1)

            turn_third(0)
            pe.wait_ge(wpg_in, 16)
            for t in range(NT):
                if t + 1 < NT:
                    turn_third(t + 1)
                pe.wait_ge(n3T_ok, 2 * t + 2)
                past(pe, g_sb, 2 * (t - 1))
                for half in range(2):
                    ins = product(bank[4 + 2 * (t % 2) + half][:],
                                  [(n3T[:, k, P * t:P * (t + 1)], wpg[:, k, 512 * half:512 * (half + 1)])
                                   for k in range(ND)])
                ins.then_inc(g_mm, 1)


_INS = ["x", "p", "g_mix", "w_in", "g_gv", "w_spatial", "b_spatial", "w_gproj", "g_cq", "w_uq", "g_ckv", "w_ukv",
        "w_mla_o", "w_out", "g_moe", "w_router_g", "b_router_g", "w_router_e", "b_router_e", "w_e_gate", "w_e_up",
        "w_e_down", "g_ple", "w_ple_gate", "w_ple_proj", "g_final"]


def _rope_tables(np):
    inv = (10000.0 ** (-np.arange(0, 64, 2, dtype=np.float32) / np.float32(64))).astype(np.float32)
    ang = (np.arange(512, dtype=np.float32)[None, :] * inv[:, None]).astype(np.float32)
    cos, sin = np.cos(ang).astype(np.float32), np.sin(ang).astype(np.float32)
    return np.concatenate([cos] * 4), np.concatenate([-sin, sin, -sin, sin])


def kernel(**inputs):
    import numpy as _np
    import concourse.bacc as _bacc
    from concourse import mybir as _mybir
    from concourse.bass_utils import run_bass_kernel_spmd as _run

    nc = _bacc.Bacc("TRN2", target_bir_lowering=False, num_devices=1)
    arrays, args = {}, []
    cos, sin = _rope_tables(_np)
    for name, a in [(n, inputs[n]) for n in _INS] + [("cos", cos), ("sin", sin)]:
        a = _np.ascontiguousarray(a)
        arrays[f"in_{name}_dram"] = a
        args.append(nc.dram_tensor(f"in_{name}_dram", a.shape, _mybir.dt.from_np(a.dtype), kind="ExternalInput").ap())
    args.append(nc.dram_tensor("out_0_dram", (1, 512, 1024), _mybir.dt.float32, kind="ExternalOutput").ap())
    build(nc, *args)
    r = _run(nc, [arrays], core_ids=[0])
    return r.results[0]["out_0_dram"]
```

```python
from contextlib import ExitStack

import concourse.bass as bass
from concourse import mybir
from concourse.alu_op_type import AluOpType as ALU

ACT = mybir.ActivationFunctionType
F32 = mybir.dt.float32
F32R = mybir.dt.float32r
I32 = mybir.dt.int32
AX_X = mybir.AxisListType.X

P = 128
S = 512
D = 1024
NT = S // P
ND = D // P
GW = 1536
NG = GW // P
NH = 8
QL = 384
KVL = 256
NOPE = 128
ROPE = 64
HR = ROPE // 2
VH = 128
QW = NOPE + ROPE
KVW = NOPE + VH
PLE = 256
NE = 64
NGRP = 8
EPG = NE // NGRP
FE = 256
CHUNK = 64
EPS = 1e-6
SCALE = float(QW) ** -0.5
MASKED = -1e30
CAP = 80
NBLK = (S + CAP - 1) // CAP
SLOTS = NBLK * CAP * NE
NRAW = 4
UNITS = 3
EMPTY = 4096
TOKEN_BITS = EMPTY | (S - 1)
NBUF = 4
KB = 1024
SBUF0 = 16896
V_COL, C_COL = GW, 2 * GW
GA_COL = C_COL + QL + KVL + ROPE
GB_COL = GA_COL + D


def build(nc, x, p, g_mix, w_in, g_gv, w_spatial, b_spatial, w_gproj, g_cq, w_uq, g_ckv, w_ukv, w_mla_o, w_out,
          g_moe, w_router_g, b_router_g, w_router_e, b_router_e, w_e_gate, w_e_up, w_e_down, g_ple, w_ple_gate,
          w_ple_proj, g_final, cos_t, sin_t, out):
    with ExitStack() as ctx:
        def sem(name):
            return ctx.enter_context(nc.semaphore(name))

        def at(name, kb, shape, dt=F32):
            return nc.alloc_sbuf_tensor_at(name, shape, dt, offset=SBUF0 + int(kb * KB))

        CONST, SMALL = 184, 200
        PIECE_AT = [0, 16, 22, 31, 40]
        unit_raw = [at(f"unit_raw{i}", 8 * i, [P, ND * FE]) for i in range(3)]
        unit_hi = [at(f"unit_hi{i}", 24 + 16 * i, [P, ND * FE], F32R) for i in range(2)]
        unit_lo = [at(f"unit_lo{i}", 32 + 16 * i, [P, ND * FE], F32R) for i in range(2)]
        a_hi = at("a_hi", 56, [P, ND, S], F32R)
        aT = at("aT", 72, [P, ND, S])
        a_lo = at("a_lo", 72, [P, ND, S], F32R)
        wkr = at("wkr", 88, [P, ND, 2, P])
        wpe = at("wpe", 96, [P, 3, 4, ROPE])
        wpes = at("wpes", 99, [P, 3, 4, ROPE])
        vv = at("vv", 88, [P, NT, NH, VH])
        xs = at("xs", 104, [P, NT, D])
        xn = at("xn", 120, [P, NT, D])
        qn = at("qn", 104, [P, NH, S])
        o_lo = at("o_lo", 104, [P, NH, S], F32R)
        qpe = at("qpe", 120, [P, NH // 2, S])
        kpe = at("kpe", 128, [P, S])
        o_hi = at("o_hi", 120, [P, NH, S], F32R)
        kn = at("kn", 136, [P, NH, S])
        sigB = at("sigB", 136, [P, ND, S])
        cT = at("cT", 152, [P, 5, S])
        csq = at("csq", 162, [P, 5, S])
        wsn = at("wsn", 162, [P, NG, P])
        rbc = at("rbc", 172, [P, 2, S])
        ropeA = at("ropeA", 176, [P, S])
        ropeB = at("ropeB", 178, [P, S])
        junk = at("junk", 180, [P, D])
        pr = [at(f"pr{i}", 152 + 5 * i, [P, 1280]) for i in range(2)]
        prT = [at(f"prT{i}", 162 + 5 * i, [P, 1280]) for i in range(2)]
        merged = at("merged", 88, [P, ND, S])
        mg_lo = at("mg_lo", 88, [P, ND, S], F32R)
        mg_hi = at("mg_hi", 72, [P, ND, S], F32R)
        vt = at("vt", 104, [P, NT, GW])
        sigA = at("sigA", 104, [P, ND, S])
        uT = at("uT", 128, [P, NG, S])
        y_lo = at("y_lo", 128, [P, NG, S], F32R)
        y_hi = at("y_hi", 152, [P, NG, S], F32R)
        tmp = [at(f"tmp{i}", 176 + 2 * i, [P, S]) for i in range(2)]
        h = at("h", 56, [P, NT, D])
        pp = at("pp", 88, [P, NT, D])
        hn = at("hn", 104, [P, NT, D])
        psb = at("psb", 120, [P, NT, PLE])
        pT = at("pT", 124, [P, 2, S])
        m_hi = at("m_hi", 160, [P, ND, S], F32R)
        m_lo = at("m_lo", 72, [P, ND, S], F32R)
        trash2 = at("trash2", 160, [P, D])
        gmb = at("gmb", 172, [P, D])
        wpp = at("wpp", 176, [P, 2, D])
        raw = [at(f"raw{i}", 128 + 8 * i, [P, ND * FE]) for i in range(NRAW)]
        gu_hi = [at("gu_hi0", 0, [P, 2, ND, FE], F32R), at("gu_hi1", 72, [P, 2, ND, FE], F32R)]
        gu_lo = [at("gu_lo0", 16, [P, 2, ND, FE], F32R), at("gu_lo1", 160, [P, 2, ND, FE], F32R)]
        dn_hi = [at("dn_hi0", 32, [P, 2, D], F32R), at("dn_hi1", 48, [P, 2, D], F32R)]
        dn_lo = [at("dn_lo0", 40, [P, 2, D], F32R), at("dn_lo1", 176, [P, 2, D], F32R)]
        xg = [at(f"xg{i}", 104 + 4 * i, [P, D]) for i in range(2)]
        XT_KB = ND * CAP * 4 / KB
        xt_place = [112, CONST + 16 - 2 * XT_KB]
        xt_hi = [at(f"xt_hi{i}", xt_place[i], [P, ND, CAP], F32R) for i in range(2)]
        xt_lo = [at(f"xt_lo{i}", xt_place[i] + XT_KB, [P, ND, CAP], F32R) for i in range(2)]
        ysb = [at(f"ysb{i}", 120 + 4 * i, [P, D]) for i in range(2)]
        cosT = at("cosT", CONST, [P, S])
        sinT = at("sinT", CONST + 2, [P, S])
        gfin = at("gfin", CONST, [P, D])
        bsp = at("bsp", CONST + 4, [P, NG, P])
        wr = at("wr", CONST + 4, [P, ND, NGRP + NE])
        wr_hi = at("wr_hi", 48, [P, ND, NGRP + NE], F32R)
        wr_lo = at("wr_lo", 51, [P, ND, NGRP + NE], F32R)
        lgT = at("lgT", 54, [NGRP + NE, S])
        at_rank = [at(f"at_rank{k}", 48 + 2 * k, [P, NT, CAP]) for k in range(2)]
        number = [at(f"number{k}", 52 + k, [P, NT, NE]) for k in range(2)]
        r8 = [at(f"r8_{i}", CONST + 6.5 + i / 8, [P, NT, EPG]) for i in range(8)]
        r1 = [at(f"r1_{i}", CONST + 7.5 + i / 32, [P, NT]) for i in range(8)]
        lg = at("lg", CONST + 8, [P, NT, NGRP + NE])
        sg = [at(f"sg{i}", CONST + 4 + i, [P, FE]) for i in range(2)]
        hm = [at(f"hm{i}", CONST + 6 + i, [P, FE]) for i in range(2)]
        HT_KB = 2 * CAP * 4 / KB
        ht_hi = [at(f"ht_hi{i}", CONST + 8 + HT_KB * i, [P, 2, CAP], F32R) for i in range(2)]
        ht_lo = [at(f"ht_lo{i}", CONST + 8 + HT_KB * (2 + i), [P, 2, CAP], F32R) for i in range(2)]
        wsT = at("wsT", CONST + 10, [P, NG, P])
        rt_e = at("rt_e", CONST + 10, [P, NT, NGRP, EPG])
        sel1 = at("sel1", CONST + 11, [P, NT, NGRP, EPG])
        sel2 = at("sel2", CONST + 12, [P, NT, NGRP, EPG])
        sel = at("sel", CONST + 13, [P, NT + 1, NE])
        iota_e = at("iota_e", CONST + 15, [P, NT, NE])
        iota_r = at("iota_r", CONST + 9.5, [P, CAP])
        fill = at("fill", 152, [P, SLOTS // P], I32)
        wpg = at("wpg", 128, [P, ND, D])
        wpg_lo = at("wpg_lo", 128, [P, ND, D], F32R)
        wpg_hi = at("wpg_hi", 0, [P, ND, D], F32R)
        y1 = at("y1", 32, [P, NT, D])
        sgt = at("sgt", 32, [P, NT, D])
        ysum = at("ysum", 48, [P, 2, D])
        y2 = at("y2", 104, [P, NT, D])
        fin = at("fin", 104, [P, NT, D])
        n3 = [at(f"n3_{t}", (120, 124, 176, 180)[t], [P, D]) for t in range(NT)]
        n3_hi = at("n3_hi", 72, [P, ND, S], F32R)
        n3_lo = at("n3_lo", 160, [P, ND, S], F32R)
        trash3 = at("trash3", CONST + 12, [P, D])
        gplb = at("gplb", CONST + 4, [P, D])

        place = [SMALL * KB]

        def small(name, shape, dt=F32):
            n = 4
            for k in shape[1:]:
                n *= k
            t = nc.alloc_sbuf_tensor_at(name, shape, dt, offset=SBUF0 + place[0])
            place[0] += (n + 31) // 32 * 32
            return t

        ident = small("ident", [P, P])
        ones = small("ones", [P, P])
        before = small("before", [P, P])
        mrow = small("mrow", [1, P])
        mcol = small("mcol", [1, P])
        gmx = small("gmx", [P, ND])
        gvg = small("gvg", [P, NG])
        gcq = small("gcq", [P, 3])
        gckv = small("gckv", [P, 2])
        brg = small("brg", [P, NGRP])
        bre = small("bre", [P, NGRP, EPG])
        stat = small("stat", [P, 3 * NT])
        rstd = small("rstd", [P, 3 * NT])
        bst = small("bst", [P, NT, 3, 6])
        bag = small("bag", [P, NT, 2])
        vrs = small("vrs", [P, NT])
        rnt = small("rnt", [P, 4])
        eps = small("eps", [P, 1])
        mx = small("mx", [P, 2, NT])
        rs = small("rs", [P, 2, NT])
        ri = small("ri", [P, 2, NT])
        wts = small("wts", [P, 2, NT])
        tabs = small("tabs", [CAP, NBLK, NE], I32)
        toks = small("toks", [CAP, NBLK, NE], I32)
        idx_x = [small(f"idx_x{i}", [CAP, 1], I32) for i in range(2)]
        idx_y = [small(f"idx_y{i}", [CAP, 1], I32) for i in range(2)]
        iota8 = small("iota8", [P, EPG])
        iota8up = small("iota8up", [P, EPG])
        most = small("most", [1, 1])
        most_i = small("most_i", [1, 1], I32)
        dst_i = small("dst_i", [P, 2, NT], I32)
        aid = small("aid", [P, 2, NT], I32)
        aid_1 = small("aid_1", [P, 2, NT])
        r_of = small("r_of", [P, 2, NT])
        e_of = at("e_of", CONST + 7.75, [P, 2, NT])
        tab_f = at("tab_f", CONST + 6, [CAP, NE])
        assert SBUF0 + place[0] <= 229344, place[0]

        bank = [ctx.enter_context(nc.psum_tensor(f"bank{i}", [P, S], F32)) for i in range(8)]

        m_dram = nc.dram_tensor("m_rows", [S, D], F32)
        y_dram = nc.dram_tensor("y_rows", [2 * S, D], F32)
        tab_dram = nc.dram_tensor("slot_table", [SLOTS, 1], I32)

        piece_in = [sem(f"piece_in{i}") for i in range(5)]
        piece_used = sem("piece_used")
        unit_in = [sem(f"unit_in{i}") for i in range(3)]
        unit_top, unit_rest, half_mm = sem("unit_top"), sem("unit_rest"), sem("half_mm")
        op_top, op_rest = sem("op_top"), sem("op_rest")
        A_SPLIT = 4
        O_SPLIT = A_SPLIT + NH
        Y_SPLIT = O_SPLIT + NG
        M_SPLIT = Y_SPLIT + ND
        WR_SPLIT = M_SPLIT + 1
        H_SPLIT = WR_SPLIT + 2 * NT
        PG_SPLIT = H_SPLIT + 4
        N3_REST = H_SPLIT + 3
        x_in = [sem(f"x_in{t}") for t in range(NT)]
        consts_in, rope_in, ws_in = sem("consts_in"), sem("rope_in"), sem("ws_in")
        x_again, p_in, wpp_in, wr_in, bias_in = (sem(n) for n in ("x_again", "p_in", "wpp_in", "wr_in", "bias_in"))
        gp_step, dv_step = sem("gp_step"), sem("dv_step")
        ident_ok, masks_ok, iota_ok, aid_ok = sem("ident_ok"), sem("masks_ok"), sem("iota_ok"), sem("aid_ok")
        ws_mm, ws_sb, ws_zero = sem("ws_mm"), sem("ws_sb"), sem("ws_zero")
        x_root, xn_ok, x_mm, aT_ok = sem("x_root"), sem("xn_ok"), sem("x_mm"), sem("aT_ok")
        c_mm, c_sb, c_sq, ss_mm, cT_ok = sem("c_mm"), sem("c_sb"), sem("c_sq"), sem("ss_mm"), sem("cT_ok")
        wkr_ok, kr_mm, kr_mul, kpe_ok = sem("wkr_ok"), sem("kr_mm"), sem("kr_mul"), sem("kpe_ok")
        wpe_ok, qkA_mm, qkD_mm, qkA_sb, qkD_sb, pe_add = (sem(n) for n in
                                                       ("wpe_ok", "qkA_mm", "qkD_mm", "qkA_sb", "qkD_sb", "pe_add"))
        s_mm, s_max, s_neg, s_exp, s_rec, p_ok, pt_mm, pt_sb, o_mm, o_sb = (sem(n) for n in (
            "s_mm", "s_max", "s_neg", "s_exp", "s_rec", "p_ok", "pt_mm", "pt_sb", "o_mm", "o_sb"))
        gb_mm, gb_sb, yb_mm, yb_sb = sem("gb_mm"), sem("gb_sb"), sem("yb_mm"), sem("yb_sb")
        v_mm, v_sb, v_ln, u_mm, u_sb = sem("v_mm"), sem("v_sb"), sem("v_ln"), sem("u_mm"), sem("u_sb")
        sp_mm, sp_sb, y_ok, ga_mm, ga_sb = sem("sp_mm"), sem("sp_sb"), sem("y_ok"), sem("ga_mm"), sem("ga_sb")
        gp_mm, gp_sb, mg_ok, w_mm, w_sb, h_ok = (sem(n) for n in ("gp_mm", "gp_sb", "mg_ok", "w_mm", "w_sb", "h_ok"))
        h_root, hn_ok, hn_out, m_mm = sem("h_root"), sem("hn_ok"), sem("hn_out"), sem("m_mm")
        pt2_mm, pt2_sb, pp_mm, pp_sb = sem("pt2_mm"), sem("pt2_sb"), sem("pp_mm"), sem("pp_sb")
        lg_mm, rt_sub, rt_exp, sel_ok, rank_mm, dst_ok = (sem(n) for n in (
            "lg_mm", "rt_sub", "rt_exp", "sel_ok", "rank_mm", "dst_ok"))
        fill_out, slots_out, tab_in, toks_ok, most_ok = (sem(n) for n in (
            "fill_out", "slots_out", "tab_in", "toks_ok", "most_ok"))
        raw_in = [sem(f"raw_in{i}") for i in range(NRAW)]
        gmb_in = sem("gmb_in")
        xg_in = [sem(f"xg_in{i}") for i in range(2)]
        y_out = [sem(f"y_out{i}") for i in range(2)]
        ix_ok, iy_ok = sem("ix_ok"), sem("iy_ok")
        w_hi, w_lo, xt_mm, xt_top, xt_rest, gu_mm, silu, h_mul, ht_mm, ht_top, ht_rest, y_mm, y_sb = (
            sem(n) for n in ("w_hi", "w_lo", "xt_mm", "xt_top", "xt_rest", "gu_mm", "silu", "h_mul", "ht_mm",
                             "ht_top", "ht_rest", "y_mm", "y_sb"))
        block_free, dma_go = sem("block_free"), sem("dma_go")
        moe_done, gfin_in = sem("moe_done"), sem("gfin_in")
        gplb_in, at_ok, tab_mm, lgT_ok, wpg_rest = (sem(n) for n in (
            "gplb_in", "at_ok", "tab_mm", "lgT_ok", "wpg_rest"))
        y_in = [sem(f"y_in{t}") for t in range(NT)]
        ysum_ok, h2_ok, h2_root, n3_ok, n_mm = (sem(n) for n in (
            "ysum_ok", "h2_ok", "h2_root", "n3_ok", "n_mm"))
        g_mm, g_sb, pg_ok, h3_ok, h3_root, fin_ok, fin_out = (sem(n) for n in (
            "g_mm", "g_sb", "pg_ok", "h3_ok", "h3_root", "fin_ok", "fin_out"))
        c_ms, c_rt, v_var, v_rt = sem("c_ms"), sem("c_rt"), sem("v_var"), sem("v_rt")

        wi = w_in[0].rearrange("(k p) n -> p k n", p=P)
        uq = w_uq[0].rearrange("(k p) n -> p k n", p=P)
        ukv = w_ukv[0].rearrange("(k p) n -> p k n", p=P)
        wo = w_mla_o[0].rearrange("(k p) n -> p k n", p=P)
        wgp = w_gproj[0].rearrange("(k p) n -> p k n", p=P)
        wot = w_out[0].rearrange("(k p) n -> p k n", p=P)
        pieces = [wi[:, :, C_COL:C_COL + 512], wi[:, :, C_COL + 512:GA_COL], uq[:, :, 0:768], uq[:, :, 768:1536], ukv]
        PC_C, PC_UQ, PC_UKV = 0, 2, 4

        HK = ND // 2
        units, unit_read = [], []

        def add_units(views, reads):
            units.extend(views)
            unit_read.extend(reads)
            return len(units) - len(views)

        def halves(w, c, groups):
            return [w[:, HK * kh:HK * (kh + 1), c + 512 * j:c + 512 * (j + 1)] for j in range(groups) for kh in range(2)]

        U_GB = add_units([wi[:, :, GB_COL + FE * j:GB_COL + FE * (j + 1)] for j in range(4)],
                         [(gb_mm, 2 * j + 2) for j in range(4)])
        U_O = add_units([wo[:, :, FE * j:FE * (j + 1)] for j in range(4)], [(yb_mm, 2 * j + 2) for j in range(4)])
        U_V = add_units(halves(wi, V_COL, 3),
                        [r for j in range(3) for r in ((half_mm, j + 1), (v_mm, NT * (j + 1)))])
        U_U = add_units([wi[:, :, FE * j:FE * (j + 1)] for j in range(6)], [(u_mm, 2 * j + 2) for j in range(6)])
        U_GA = add_units([wi[:, :, GA_COL + FE * j:GA_COL + FE * (j + 1)] for j in range(4)],
                         [(ga_mm, 2 * j + 2) for j in range(4)])
        U_GP = add_units([wgp[:, :, P * j:P * (j + 1)] for j in range(8)], [(gp_mm, j + 1) for j in range(8)])
        U_W = add_units(halves(wot, 0, 2), [r for j in range(2) for r in ((half_mm, 4 + j), (w_mm, NT * (j + 1)))])
        N_UNITS = len(units)

        def piece(i):
            k, n = pieces[i].shape[1], pieces[i].shape[2]
            return piece_mem[i][:].rearrange("p (k n) -> p k n", k=k)

        piece_mem = [at(f"piece{i}", PIECE_AT[i], [P, pieces[i].shape[1] * pieces[i].shape[2]])
                     for i in range(len(pieces))]

        def unit_view(mem, n):
            k, c = units[n].shape[1], units[n].shape[2]
            return mem[:, 0:k * c].rearrange("p (k c) -> p k c", k=k)

        def arrived(eng, i):
            eng.wait_ge(piece_in[i], 16)

        def past(eng, s, v):
            if not isinstance(v, int) or v > 0:
                eng.wait_ge(s, v)

        s_bank = [(1, 384), (2, 0), (1, 0), (0, 0)]
        s_order = [0, 2, 3, 1]
        s_ready = [2, 4, 2, 3]
        p_off = [0, 128, 384, 768]
        t_bank = [(3, 0), (4, 0), (5, 0), (4, 384)]
        t_off = [0, 512, 896, 1152]

        MB = [2, 3, 4, 5, 6, 7, 0, 1]

        def scores(i):
            b, c = s_bank[i]
            return bank[b][:, c:c + P * (i + 1)]

        def turned(j):
            b, c = t_bank[j]
            return bank[b][:, c:c + P * (NT - j)]

        block = ctx.enter_context(nc.Block())

        @block.sync
        def _(sp):
            for i in range(len(pieces)):
                sp.dma_start(piece(i), pieces[i]).then_inc(piece_in[i], 16)
            sp.wait_ge(piece_used, 1)
            for n in range(N_UNITS):
                if n == 2:
                    sp.wait_ge(piece_used, 3)
                if n >= 3:
                    sp.wait_ge(unit_rest, n - 2)
                sp.dma_start(unit_view(unit_raw[n % 3], n), units[n]).then_inc(unit_in[n % 3], 16)

            def matrix(e, r):
                w = (w_e_gate, w_e_up, w_e_down)[r]
                return w[0, bass.ds(e, 1)].rearrange("a (p k) n -> p (a k n)", p=P)

            sp.wait_ge(gp_mm, ND)
            for n in range(NRAW):
                sp.dma_start(raw[n][:], matrix(n // UNITS, n % UNITS)).then_inc(raw_in[n], 16)
            for n in range(NRAW, UNITS * NBUF):
                sp.wait_ge(w_lo, n - NRAW + 1)
                sp.dma_start(raw[n % NRAW][:], matrix(n // UNITS, n % UNITS)).then_inc(raw_in[n % NRAW], 16)
            with sp.Fori(1, NE // NBUF) as i:
                for n in range(UNITS * NBUF):
                    sp.wait_ge(w_lo, i * (UNITS * NBUF) + (n - NRAW + 1))
                    sp.dma_start(raw[n % NRAW][:], matrix(i * NBUF + n // UNITS, n % UNITS))\
                        .then_inc(raw_in[n % NRAW], 16)
            sp.wait_ge(most_ok, 2)
            most_v = sp.value_load(most_i[0:1, 0:1], min_val=0, max_val=S)
            with sp.If(most_v > CAP):
                with sp.Fori(1, NBLK) as b:
                    with sp.Fori(0, NE) as e:
                        sp.wait_ge(block_free, (b - 1) * NE + e + 1)
                        for r in range(UNITS):
                            sp.dma_start(raw[r][:], matrix(e, r)).then_inc(raw_in[r], 16)
                sp.wait_ge(w_lo, UNITS * NE * NBLK)
            sp.wait_ge(w_lo, UNITS * NE)
            for q in range(4):
                sp.dma_start(wpg[:, 2 * q:2 * q + 2], w_ple_gate[0].rearrange("(p k) n -> p k n", p=P)[:, 2 * q:2 * q + 2])\
                    .then_inc(piece_in[q], 16)
            sp.wait_ge(moe_done, 1)
            for t in range(NT):
                sp.dma_start(y1[:, t], y_dram[P * t:P * (t + 1), :]).then_inc(y_in[t], 16)
                sp.dma_start(y2[:, t], y_dram[S + P * t:S + P * (t + 1), :]).then_inc(y_in[t], 16)
                if t == 0:
                    sp.dma_start(gplb[:], g_ple[0:1, :].to_broadcast([P, D])).then_inc(gplb_in, 16)
            for t in range(NT):
                sp.wait_ge(fin_ok, t + 1)
                sp.dma_start(out[0, P * t:P * (t + 1), :], fin[:, t]).then_inc(fin_out, 16)
            sp.wait_ge(fin_out, 16 * NT)

        @block.gpsimd
        def _(pool):
            steps = [0]

            def link(ins):
                steps[0] += 1
                ins.then_inc(gp_step, 1)
                pool.wait_ge(gp_step, steps[0])

            pool.memset(eps[:], EPS).then_inc(ident_ok, 1)
            link(pool.memset(ident[:], 0.0))
            pool.affine_select(out=ident[:], in_=ident[:], compare_op=ALU.not_equal, fill=1.0, base=0,
                               pattern=[[-1, P]], channel_multiplier=1).then_inc(ident_ok, 1)
            link(pool.memset(mrow[:], 0.0))
            pool.memset(mrow[:, 0:CHUNK], 1.0).then_inc(masks_ok, 1)
            link(pool.memset(mcol[:], 0.0))
            pool.memset(mcol[:, CHUNK:P], MASKED).then_inc(masks_ok, 1)
            pool.memset(ones[:], 1.0).then_inc(masks_ok, 1)
            link(pool.memset(before[:], 1.0))
            pool.affine_select(out=before[:], in_=before[:], compare_op=ALU.is_gt, fill=0.0, base=0,
                               pattern=[[1, P]], channel_multiplier=-1).then_inc(masks_ok, 1)
            arrived(pool, PC_C + 1)
            kr = piece(PC_C + 1)[:, :, P:P + ROPE]
            for r in range(2):
                pool.tensor_copy(wkr[:, :, 0, ROPE * r:ROPE * (r + 1)], kr).then_inc(wkr_ok, 1)
                pool.tensor_copy(wkr[:, :, 1, ROPE * r:ROPE * r + HR], kr[:, :, HR:ROPE]).then_inc(wkr_ok, 1)
                pool.tensor_copy(wkr[:, :, 1, ROPE * r + HR:ROPE * (r + 1)], kr[:, :, 0:HR]).then_inc(wkr_ok, 1)
            for half in range(2):
                arrived(pool, PC_UQ + half)
                if half:
                    pool.wait_ge(qkD_mm, 4)
                wq = piece(PC_UQ + half).rearrange("p k (h c) -> p k h c", c=QW)[:, :, :, NOPE:QW]
                pool.tensor_copy(wpe[:], wq).then_inc(wpe_ok, 1)
                pool.tensor_copy(wpes[:, :, :, 0:HR], wq[:, :, :, HR:ROPE]).then_inc(wpe_ok, 1)
                pool.tensor_copy(wpes[:, :, :, HR:ROPE], wq[:, :, :, 0:HR]).then_inc(wpe_ok, 1)
                if half == 0:
                    pool.wait_ge(kr_mul, 2)
                    pool.tensor_tensor(kpe[:], ropeA[:], ropeB[:], ALU.add).then_inc(kpe_ok, 1)
                for j in range(2 * half, 2 * half + 2):
                    pool.wait_ge(qkD_sb, 2 * j + 2)
                    pool.tensor_tensor(qpe[:, j], ropeA[:], ropeB[:], ALU.add).then_inc(pe_add, 1)
            pool.wait_ge(o_sb, NH)
            link(pool.memset(fill[:], EMPTY))
            pool.dma_start(tab_dram.rearrange("(p n) a -> p (n a)", p=P), fill[:]).then_inc(fill_out, 16)
            pool.iota(aid_1[:], pattern=[[S, 2], [P, NT]], base=1, channel_multiplier=1,
                      allow_small_or_imprecise_dtypes=True).then_inc(aid_ok, 1)
            pool.iota(aid[:], pattern=[[S, 2], [P, NT]], base=0, channel_multiplier=1).then_inc(aid_ok, 1)
            for g in range(NG):
                pool.wait_ge(sp_sb, g + 1)
                pool.wait_ge(u_sb, g + 1)
                pool.tensor_tensor(uT[:, g], uT[:, g], tmp[g % 2][:], ALU.mult).then_inc(y_ok, 1)
            for c in range(ND):
                pool.wait_ge(gp_sb, c + 1)
                pool.tensor_tensor(merged[:, c], merged[:, c], tmp[c % 2][:], ALU.add).then_inc(mg_ok, 1)
            pool.wait_ge(gp_mm, ND)
            pool.iota(iota_e[:], pattern=[[0, NT], [1, NE]], base=0, channel_multiplier=0,
                      allow_small_or_imprecise_dtypes=True).then_inc(iota_ok, 1)
            pool.wait_ge(w_mm, 2 * NT)
            pool.iota(iota_r[:], pattern=[[1, CAP]], base=0, channel_multiplier=0,
                      allow_small_or_imprecise_dtypes=True).then_inc(iota_ok, 1)
            pool.wait_ge(toks_ok, 1)
            pool.wait_ge(hn_out, 16 * NT)
            pool.wait_ge(m_mm, 2 * NT)

            def gather(e, u, i):
                b, n = u % 2, i * 2 + u // 2
                past(pool, xg_in[b], 16 * n)
                pool.tensor_copy(idx_x[b][:], toks[:, 0, bass.ds(e, 1)]).then_inc(ix_ok, 1)
                pool.wait_ge(ix_ok, e + 1)
                past(pool, xt_mm, e - 1)
                pool.sem_inc(dma_go, 1)
                pool.indirect_dma_start(out=xg[b][0:CAP, :], out_offset=None, in_=m_dram[:, :],
                                        in_offset=bass.IndirectOffsetOnAxis(ap=idx_x[b][:], axis=0),
                                        bounds_check=last_row, oob_is_err=False).then_inc(xg_in[b], 16)

            def scatter(e, u, i):
                b, n = u % 2, i * 2 + u // 2
                past(pool, y_out[b], 16 * n)
                pool.tensor_copy(idx_y[b][:], tabs[:, 0, bass.ds(e, 1)]).then_inc(iy_ok, 1)
                pool.wait_ge(iy_ok, e + 1)
                pool.wait_ge(y_sb, e + 1)
                pool.sem_inc(dma_go, 1)
                pool.indirect_dma_start(out=y_dram[:, :],
                                        out_offset=bass.IndirectOffsetOnAxis(ap=idx_y[b][:], axis=0),
                                        in_=ysb[b][0:CAP, :], in_offset=None,
                                        bounds_check=last_result, oob_is_err=False).then_inc(y_out[b], 16)

            last_row, last_result = pool.to_reg(S - 1), pool.to_reg(2 * S - 1)
            LAG = 3
            for u in range(NBUF):
                gather(u, u, 0)
                if u >= LAG:
                    scatter(u - LAG, u - LAG, 0)
            with pool.Fori(1, NE // NBUF) as i:
                for u in range(NBUF):
                    gather(i * NBUF + u, u, i)
                    if u >= LAG:
                        scatter(i * NBUF + u - LAG, u - LAG, i)
                    else:
                        scatter(i * NBUF + u - LAG, u - LAG + NBUF, i - 1)
            last = NE // NBUF - 1
            for e in range(NE - LAG, NE):
                scatter(e, e % NBUF, last)
            for b in range(2):
                pool.wait_ge(y_out[b], 16 * NE // 2)
            most_v = pool.value_load(most_i[0:1, 0:1], min_val=0, max_val=S)
            with pool.If(most_v > CAP):
                pool.wait_ge(fill_out, 16)
                pool.wait_ge(dst_ok, 1)
                for k in range(2):
                    for t in range(NT):
                        pool.indirect_dma_start(
                            out=tab_dram[:, :], out_offset=bass.IndirectOffsetOnAxis(ap=dst_i[:, k, t:t + 1], axis=0),
                            in_=aid[:, k, t:t + 1], in_offset=None,
                            bounds_check=SLOTS - 1, oob_is_err=False).then_inc(slots_out, 16)
                pool.wait_ge(slots_out, 16 * 2 * NT)
                pool.dma_start(tabs[:], tab_dram.rearrange("(b c e) a -> c b (e a)", b=NBLK, c=CAP)).then_inc(tab_in, 16)
                pool.wait_ge(toks_ok, 2)
                pool.sem_inc(block_free, 1)
                with pool.Fori(1, NBLK) as b:
                    with pool.Fori(0, NE) as e:
                        step = (b - 1) * NE + e
                        n = b * NE + e
                        pool.tensor_copy(idx_x[0][:], toks[:].rearrange("c b e -> c (b e)")[:, bass.ds(n, 1)])\
                            .then_inc(ix_ok, 1)
                        pool.tensor_copy(idx_y[0][:], tabs[:].rearrange("c b e -> c (b e)")[:, bass.ds(n, 1)])\
                            .then_inc(iy_ok, 1)
                        pool.wait_ge(ix_ok, n + 1)
                        pool.wait_ge(iy_ok, n + 1)
                        pool.sem_inc(dma_go, 1)
                        pool.indirect_dma_start(out=xg[0][0:CAP, :], out_offset=None, in_=m_dram[:, :],
                                                in_offset=bass.IndirectOffsetOnAxis(ap=idx_x[0][:], axis=0),
                                                bounds_check=last_row, oob_is_err=False).then_inc(xg_in[0], 16)
                        pool.wait_ge(y_sb, n + 1)
                        pool.sem_inc(dma_go, 1)
                        pool.indirect_dma_start(out=y_dram[:, :],
                                                out_offset=bass.IndirectOffsetOnAxis(ap=idx_y[0][:], axis=0),
                                                in_=ysb[0][0:CAP, :], in_offset=None,
                                                bounds_check=last_result, oob_is_err=False).then_inc(y_out[0], 16)
                        pool.wait_ge(y_out[0], step * 16 + (16 * NE // 2 + 16))
                        pool.sem_inc(block_free, 1)
            pool.sem_inc(moe_done, 1)
            pool.wait_ge(op_top, H_SPLIT + 4)
            pool.tensor_tensor(wpg_lo[:, 6:8], wpg[:, 6:8], wpg_hi[:, 6:8].bitcast(F32), ALU.subtract)\
                .then_inc(wpg_rest, 1)

        @block.scalar
        def _(act):
            for t in range(NT):
                act.dma_start(xs[:, t], x[0, P * t:P * (t + 1), :]).then_inc(x_in[t], 16)
                if t == 0:
                    act.dma_start(wsn[:], w_spatial[0].rearrange("g t s -> t g s")).then_inc(ws_in, 16)
            with nc.allow_non_contiguous_dma(reason="gains, one per partition"):
                act.dma_start(gmx[:], g_mix[0].rearrange("(k p) -> p k", p=P)).then_inc(consts_in, 16)
                act.dma_start(gcq[:], g_cq[0].rearrange("(k p) -> p k", p=P)).then_inc(consts_in, 16)
                act.dma_start(gckv[:], g_ckv[0].rearrange("(k p) -> p k", p=P)).then_inc(consts_in, 16)
                act.dma_start(gvg[:], g_gv[0].rearrange("(k p) -> p k", p=P)).then_inc(consts_in, 16)
            act.dma_start(cosT[:], cos_t).then_inc(rope_in, 16)
            act.dma_start(sinT[:], sin_t).then_inc(rope_in, 16)
            act.dma_start(bsp[:], b_spatial[0:1].to_broadcast([P, NG, P])).then_inc(bias_in, 16)
            act.dma_start(brg[:], b_router_g[0:1, :].to_broadcast([P, NGRP])).then_inc(bias_in, 16)
            act.dma_start(bre[:], b_router_e[0:1].to_broadcast([P, NGRP, EPG])).then_inc(bias_in, 16)

            act.wait_ge(ident_ok, 1)

            def row_root(src, trash, n, t, root):
                act.activation(trash, src, ACT.Square, scale=float(D) ** -0.5,
                               accum_out=stat[:, n:n + 1]).then_inc(root, 1)
                act.wait_ge(root, 2 * t + 1)
                act.activation(rstd[:, n:n + 1], stat[:, n:n + 1], ACT.Sqrt, bias=eps[:]).then_inc(root, 1)

            for t in range(NT):
                act.wait_ge(x_in[t], 16)
                row_root(xs[:, t], junk[:], t, t, x_root)
            for b in range(3):
                act.wait_ge(ws_mm, b + 1)
                act.activation(wsT[:, 4 * b:4 * b + 4].rearrange("p g t -> p (g t)"), bank[b][:], ACT.Copy)\
                    .then_inc(ws_sb, 1)
            for c in range(5):
                act.wait_ge(c_sb, c + 1)
                act.activation(csq[:, c], cT[:, c], ACT.Square).then_inc(c_sq, 1)
            act.wait_ge(aT_ok, 2 * NT)
            for q in range(4):
                act.activation(a_hi[:, 2 * q:2 * q + 2], aT[:, 2 * q:2 * q + 2], ACT.Copy).then_inc(op_top, 1)
            for n in range(2):
                act.wait_ge(c_ms, n + 1)
                act.activation(ropeA[:] if n == 0 else ropeB[:], rbc[:, n], ACT.Sqrt, bias=eps[:]).then_inc(c_rt, 1)
            for a in range(16):
                act.wait_ge(qkA_mm, a + 1)
                dst = qn[:, a] if a < NH else kn[:, a - NH]
                act.activation(dst, bank[1 + a % 4][:], ACT.Copy).then_inc(qkA_sb, 1)

            def softmax_exp(hd):
                for i in range(NT):
                    if i == 0:
                        act.wait_ge(s_neg, hd + 1)
                        past(act, pt_mm, hd - 1)
                    act.activation(pr[hd % 2][:, p_off[i]:p_off[i] + P * (i + 1)], scores(i), ACT.Exp,
                                   bias=mx[:, hd % 2, i:i + 1], scale=SCALE,
                                   accum_out=rs[:, hd % 2, i:i + 1]).then_inc(s_exp, 1)

            def probs_out(hd):
                act.wait_ge(pt_mm, hd + 1)
                past(act, o_mm, hd - 1)
                for j in range(NT):
                    act.activation(prT[hd % 2][:, t_off[j]:t_off[j] + P * (NT - j)], turned(j), ACT.Copy)\
                        .then_inc(pt_sb, 1)
                act.wait_ge(o_mm, hd + 1)
                act.activation(qn[:, hd], bank[6 + hd % 2][:], ACT.Copy).then_inc(o_sb, 1)

            def unit_split(n):
                if n >= N_UNITS:
                    return
                act.wait_ge(unit_in[n % 3], 16 * (n // 3 + 1))
                if n >= 2:
                    act.wait_ge(*unit_read[n - 2])
                else:
                    act.wait_ge(piece_used, 4 + n)
                act.activation(unit_view(unit_hi[n % 2], n), unit_view(unit_raw[n % 3], n), ACT.Copy)\
                    .then_inc(unit_top, 1)

            softmax_exp(0)
            for hd in range(NH):
                if hd + 1 < NH:
                    softmax_exp(hd + 1)
                probs_out(hd)
                if hd in (2, 4):
                    unit_split(hd // 2 - 1)
            for hd in range(NH):
                act.wait_ge(o_sb, hd + 1)
                act.activation(o_hi[:, hd], qn[:, hd], ACT.Copy).then_inc(op_top, 1)
            for c in range(ND):
                act.wait_ge(gb_mm, c + 1)
                act.activation(sigB[:, c], bank[c][:], ACT.Sigmoid).then_inc(gb_sb, 1)
                if c % 2:
                    unit_split(U_GB + c // 2 + 2)
            for j in range(4):
                unit_split(U_O + j + 2)
            for g in range(12):
                if g % 4 == 0:
                    unit_split(U_V + g // 2 + 2)
                act.wait_ge(v_mm, g + 1)
                act.activation(vt[:, g % 4, 512 * (g // 4):512 * (g // 4 + 1)], bank[g % 8][:],
                               ACT.Gelu_apprx_tanh).then_inc(v_sb, 1)
                if g % 4 == 3:
                    unit_split(U_V + g // 2 + 2)
            act.wait_ge(v_var, NT)
            act.activation(vrs[:], bag[:, :, 1], ACT.Sqrt, bias=eps[:]).then_inc(v_rt, 1)
            act.wait_ge(fill_out, 16)
            for c in range(NG):
                act.wait_ge(u_mm, c + 1)
                act.activation(uT[:, c], bank[(4 + c) % 8][:], ACT.Gelu_apprx_tanh).then_inc(u_sb, 1)
                if c % 2:
                    unit_split(U_U + c // 2 + 2)
            act.wait_ge(sp_mm, NG)
            act.dma_start(psb[:], p[0, 0].rearrange("(t p) d -> p t d", p=P)).then_inc(p_in, 16)

            def y_top(g):
                act.wait_ge(y_ok, g + 1)
                act.activation(y_hi[:, g], uT[:, g], ACT.Copy).then_inc(op_top, 1)

            for g in range(NG // 2):
                y_top(g)
            for c in range(ND):
                act.wait_ge(ga_mm, c + 1)
                act.activation(sigA[:, c], bank[(4 + c) % 8][:], ACT.Sigmoid).then_inc(ga_sb, 1)
                if c % 2:
                    unit_split(U_GA + c // 2 + 2)
                if 1 <= c < 7:
                    y_top(NG // 2 + c - 1)
            act.dma_start(h[:], x[0].rearrange("(t p) d -> p t d", p=P)).then_inc(x_again, 16)

            def merged_top(c):
                act.wait_ge(mg_ok, c + 1)
                act.activation(mg_hi[:, c], merged[:, c], ACT.Copy).then_inc(op_top, 1)

            for c in range(ND):
                unit_split(U_GP + c + 2)
                if c:
                    merged_top(c - 1)
            merged_top(ND - 1)
            act.dma_start(wpp[:], w_ple_proj[0].rearrange("(k p) n -> p k n", p=P)).then_inc(wpp_in, 16)
            act.dma_start(gmb[:], g_moe[0:1, :].to_broadcast([P, D])).then_inc(gmb_in, 16)
            with nc.allow_non_contiguous_dma(reason="the router's rows"):
                act.dma_start(wr[:, :, 0:NGRP], w_router_g[0].rearrange("(p k) n -> p k n", p=P)).then_inc(wr_in, 16)
                act.dma_start(wr[:, :, NGRP:NGRP + NE], w_router_e[0].rearrange("(p k) n -> p k n", p=P))\
                    .then_inc(wr_in, 16)
            unit_split(U_W + 2)
            unit_split(U_W + 3)
            for k in range(2):
                act.wait_ge(pt2_mm, k + 1)
                act.activation(pT[:, k], bank[4 + k][:], ACT.Copy).then_inc(pt2_sb, 1)

            def pp_out(g):
                act.wait_ge(pp_mm, g + 1)
                act.activation(pp[:, g // 2, 512 * (g % 2):512 * (g % 2 + 1)], bank[6 + g if g < 2 else (g + 2) % 8][:],
                               ACT.Copy).then_inc(pp_sb, 1)

            for t in range(NT):
                act.wait_ge(h_ok, t + 1)
                row_root(h[:, t], trash2[:], NT + t, t, h_root)
            act.wait_ge(wr_in, 32)
            act.wait_ge(w_mm, 2 * NT)
            act.activation(wr_hi[:], wr[:], ACT.Copy).then_inc(op_top, 1)
            for g in range(2):
                pp_out(g)
            act.wait_ge(hn_ok, NT)
            act.wait_ge(h_root, 2 * NT)
            for t in range(NT):
                act.dma_start(m_dram[P * t:P * (t + 1), :], hn[:, t]).then_inc(hn_out, 16)
            for t in range(NT):
                for half in range(2):
                    act.wait_ge(m_mm, 2 * t + half + 1)
                    act.activation(m_hi[:, 4 * half:4 * half + 4, P * t:P * (t + 1)],
                                   bank[MB[2 * t + half]][:].rearrange("p (k s) -> p k s", k=4), ACT.Copy)\
                        .then_inc(op_top, 1)
            for r in range(2):
                act.wait_ge(raw_in[r], 16)
                if r == 1:
                    act.wait_ge(lg_mm, 1)
                    act.activation(lgT[:], bank[2][0:NGRP + NE, :], ACT.Copy).then_inc(lgT_ok, 1)
                act.activation(gu_hi[0][:, r].rearrange("p k n -> p (k n)"), raw[r][:], ACT.Copy).then_inc(w_hi, 1)
            act.wait_ge(raw_in[2], 16)
            act.activation(dn_hi[0][:].rearrange("p k n -> p (k n)"), raw[2][:], ACT.Copy).then_inc(w_hi, 1)
            for s in range(2):
                act.wait_ge(rt_sub, s + 1)
                act.activation(r8[1 + s][:], r8[1 + s][:], ACT.Exp).then_inc(rt_exp, 1)
            for g in range(2, 8):
                pp_out(g)
            act.dma_start(gfin[:], g_final.rearrange("(a d) -> a d", a=1).to_broadcast([P, D])).then_inc(gfin_in, 16)

            def split(n, e, g, r, b):
                slot_of, count = g
                act.wait_ge(raw_in[slot_of], 16 * count)
                if r < 2:
                    past(act, gu_mm, e - 1)
                    dst = gu_hi[b][:, r].rearrange("p k n -> p (k n)")
                else:
                    past(act, y_mm, e - 1)
                    dst = dn_hi[b][:].rearrange("p k n -> p (k n)")
                act.activation(dst, raw[slot_of][:], ACT.Copy).then_inc(w_hi, 1)

            def unit(i, u, r):
                n = UNITS * u + r
                return n % NRAW, i * (UNITS * NBUF // NRAW) + (n // NRAW + 1)

            def rows_top(e, b, wait_gu=True):
                act.wait_ge(xt_mm, e + 1)
                if wait_gu:
                    past(act, gu_mm, e - 1)
                for half in range(2):
                    ins = act.activation(xt_hi[b][:, 4 * half:4 * half + 4],
                                         bank[half][:, 0:4 * CAP].rearrange("p (k c) -> p k c", k=4), ACT.Copy)
                ins.then_inc(xt_top, 1)

            def hidden_top(e, b, wait_y=True):
                act.wait_ge(ht_mm, e + 1)
                if wait_y:
                    past(act, y_mm, e - 1)
                act.activation(ht_hi[b][:], bank[4 + b][:, 0:2 * CAP].rearrange("p (j c) -> p j c", j=2), ACT.Copy)\
                    .then_inc(ht_top, 1)

            def silu_step(e, b, wait_mul=True):
                act.wait_ge(gu_mm, e + 1)
                if wait_mul:
                    past(act, h_mul, e - 1)
                act.activation(sg[b][0:CAP], bank[2 + b][0:CAP, 0:FE], ACT.Silu).then_inc(silu, 1)

            def result_out(e, b, uses):
                act.wait_ge(y_mm, e + 1)
                past(act, y_out[b], uses)
                for half in range(2):
                    ins = act.activation(ysb[b][0:CAP, 512 * half:512 * (half + 1)], bank[6 + half][0:CAP, :], ACT.Copy)
                ins.then_inc(y_sb, 1)

            def expert_step(i, u, first=False, last=False):
                e = i * NBUF + u
                pi, pu = (i, u - 1) if u else (i - 1, NBUF - 1)
                ni, nu = (i, u + 1) if u + 1 < NBUF else (i + 1, 0)
                if not first:
                    hidden_top(e - 1, pu % 2)
                if not last:
                    rows_top(e + 1, nu % 2)
                if not first:
                    split(UNITS * e + 2, e, unit(i, u, 2), 2, u % 2)
                if not last:
                    split(UNITS * e + 3, e + 1, unit(ni, nu, 0), 0, nu % 2)
                    split(UNITS * e + 4, e + 1, unit(ni, nu, 1), 1, nu % 2)
                silu_step(e, u % 2)
                if not first:
                    result_out(e - 1, pu % 2, 16 * (pi * 2 + pu // 2))

            rows_top(0, 0)
            for u in range(NBUF):
                expert_step(0, u, first=(u == 0))
            with act.Fori(1, NE // NBUF - 1) as i:
                for u in range(NBUF):
                    expert_step(i, u)
            for u in range(NBUF):
                expert_step(NE // NBUF - 1, u, last=(u == NBUF - 1))
            hidden_top(NE - 1, 1)
            result_out(NE - 1, 1, 16 * (NE // 2 - 1))
            most_v = act.value_load(most_i[0:1, 0:1], min_val=0, max_val=S)
            with act.If(most_v > CAP):
                with act.Fori(1, NBLK) as b:
                    with act.Fori(0, NE) as e:
                        n = b * NE + e
                        rows_top(n, 0, wait_gu=False)
                        for r in range(UNITS):
                            act.wait_ge(raw_in[r], ((b - 1) * NE + e) * 16 + (16 * UNITS * NE // NRAW + 16))
                            dst = gu_hi[0][:, r] if r < 2 else dn_hi[0][:]
                            act.activation(dst.rearrange("p k n -> p (k n)"), raw[r][:], ACT.Copy).then_inc(w_hi, 1)
                        silu_step(n, 0, wait_mul=False)
                        hidden_top(n, 0, wait_y=False)
                        act.wait_ge(y_mm, n + 1)
                        for half in range(2):
                            ins = act.activation(ysb[0][0:CAP, 512 * half:512 * (half + 1)], bank[6 + half][0:CAP, :],
                                                 ACT.Copy)
                        ins.then_inc(y_sb, 1)
            act.wait_ge(y_mm, NE)
            for q in range(4):
                act.wait_ge(piece_in[q], 32)
                act.activation(wpg_hi[:, 2 * q:2 * q + 2], wpg[:, 2 * q:2 * q + 2], ACT.Copy).then_inc(op_top, 1)

            def third_root(t):
                act.wait_ge(h2_ok, t + 1)
                row_root(h[:, t], trash3[:], 2 * NT + t, t, h2_root)

            def third_top(t):
                for half in range(2):
                    act.wait_ge(n_mm, 2 * t + half + 1)
                    act.activation(n3_hi[:, 4 * half:4 * half + 4, P * t:P * (t + 1)],
                                   bank[2 * (t % 2) + half][:].rearrange("p (k s) -> p k s", k=4), ACT.Copy)\
                        .then_inc(op_top, 1)

            third_root(0)
            third_root(1)
            third_top(0)
            third_root(2)
            third_root(3)
            for t in range(NT):
                if t + 1 < NT:
                    third_top(t + 1)
                act.wait_ge(g_mm, t + 1)
                for half in range(2):
                    act.activation(sgt[:, t, 512 * half:512 * (half + 1)], bank[4 + 2 * (t % 2) + half][:],
                                   ACT.Sigmoid).then_inc(g_sb, 1)
                act.wait_ge(h3_ok, t + 1)
                row_root(h[:, t], fin[:, t], t, t, h3_root)

        @block.vector
        def _(dve):
            steps = [0]

            def link(ins):
                steps[0] += 1
                ins.then_inc(dv_step, 1)
                dve.wait_ge(dv_step, steps[0])

            def invert(y, v, w):
                link(dve.reciprocal(y, y))
                link(dve.scalar_tensor_tensor(w, v, EPS, y, ALU.add, ALU.mult))
                link(dve.scalar_tensor_tensor(w, w, -0.5, y, ALU.mult, ALU.mult))
                link(dve.scalar_tensor_tensor(y, w, 1.5, y, ALU.add, ALU.mult))

            def inv_rms(n, count=1):
                invert(rstd[:, n:n + count], stat[:, n:n + count], rnt[:, 0:count])

            def gain_out(dst, b, g, half):
                return dve.tensor_tensor(dst, bank[b][:].rearrange("p (k s) -> p k s", k=4),
                                         g[:, 4 * half:4 * half + 4].unsqueeze(2).to_broadcast([P, 4, P]), ALU.mult)

            for t in range(NT):
                dve.wait_ge(x_root, 2 * t + 2)
                inv_rms(t)
                dve.tensor_scalar(xn[:, t], xs[:, t], rstd[:, t:t + 1], None, ALU.mult).then_inc(xn_ok, 1)
            dve.wait_ge(consts_in, 16 * 4)
            for t in range(NT):
                for half in range(2):
                    dve.wait_ge(x_mm, 2 * t + half + 1)
                    gain_out(aT[:, 4 * half:4 * half + 4, P * t:P * (t + 1)], (3 + 2 * t + half) % 8, gmx, half)\
                        .then_inc(aT_ok, 1)
            dve.wait_ge(ws_sb, 3)
            dve.memset(wsT[CHUNK:P, :, 0:CHUNK], 0.0).then_inc(ws_zero, 1)
            for c in range(5):
                dve.wait_ge(c_mm, c + 1)
                dve.tensor_copy(cT[:, c], bank[c][:]).then_inc(c_sb, 1)
            for n, (b, w) in enumerate(((5, QL), (6, KVL))):
                dve.wait_ge(ss_mm, n + 1)
                dve.tensor_scalar(rbc[:, n], bank[b][:], 1.0 / w, None, ALU.mult).then_inc(c_ms, 1)
            for n in range(2):
                root = (ropeA, ropeB)[n]
                dve.wait_ge(c_rt, n + 1)
                invert(root[:], rbc[:, n], csq[:, n])
            dve.wait_ge(c_sb, 5)
            for c in range(5):
                g = gcq[:, c:c + 1] if c < 3 else gckv[:, c - 3:c - 2]
                dve.scalar_tensor_tensor(cT[:, c], cT[:, c], g, (ropeA if c < 3 else ropeB)[:], ALU.mult, ALU.mult)\
                    .then_inc(cT_ok, 1)
            dve.wait_ge(cT_ok, 5)
            dve.wait_ge(rope_in, 32)
            dve.wait_ge(kr_mm, 1)
            dve.tensor_tensor(ropeA[:], bank[7][:], cosT[:], ALU.mult).then_inc(kr_mul, 1)
            dve.wait_ge(kr_mm, 2)
            dve.tensor_tensor(ropeB[:], bank[0][:], sinT[:], ALU.mult).then_inc(kr_mul, 1)
            DB = [5, 6, 7, 0]
            for d in range(16):
                dve.wait_ge(qkD_mm, d + 1)
                if d < 8:
                    if d % 2 == 0:
                        dve.wait_ge(kpe_ok, 1)
                        past(dve, pe_add, d // 2)
                    dve.tensor_tensor((ropeA, ropeB)[d % 2][:], bank[DB[d % 4]][:], (cosT, sinT)[d % 2][:], ALU.mult)\
                        .then_inc(qkD_sb, 1)
                    if d < 4:
                        dve.wait_ge(op_top, d + 1)
                        dve.tensor_tensor(a_lo[:, 2 * d:2 * d + 2], aT[:, 2 * d:2 * d + 2],
                                          a_hi[:, 2 * d:2 * d + 2].bitcast(F32), ALU.subtract).then_inc(op_rest, 1)
                else:
                    t, q = (d - 8) // 2, (d - 8) % 2
                    dve.tensor_copy(vv[:, t, 4 * q:4 * q + 4].rearrange("p h v -> p (h v)"), bank[DB[d % 4]][:])\
                        .then_inc(qkD_sb, 1)

            def maxima(hd):
                past(dve, s_exp, NT * (hd - 1))
                for i in s_order:
                    dve.wait_ge(s_mm, NT * hd + s_ready[i])
                    dve.tensor_reduce(mx[:, hd % 2, i:i + 1], scores(i), AX_X, ALU.max).then_inc(s_max, 1)
                dve.wait_ge(s_max, NT * (hd + 1))
                dve.tensor_scalar(mx[:, hd % 2], mx[:, hd % 2], -SCALE, None, ALU.mult).then_inc(s_neg, 1)

            def normalise(hd):
                dve.wait_ge(s_exp, NT * (hd + 1))
                dve.reciprocal(ri[:, hd % 2], rs[:, hd % 2]).then_inc(s_rec, 1)
                dve.wait_ge(s_rec, hd + 1)
                for i in range(NT):
                    v = pr[hd % 2][:, p_off[i]:p_off[i] + P * (i + 1)]
                    dve.tensor_scalar(v, v, ri[:, hd % 2, i:i + 1], None, ALU.mult).then_inc(p_ok, 1)

            def unit_left(n):
                if n >= N_UNITS:
                    return
                dve.wait_ge(unit_top, n + 1)
                dve.tensor_tensor(unit_view(unit_lo[n % 2], n), unit_view(unit_raw[n % 3], n),
                                  unit_view(unit_hi[n % 2], n).bitcast(F32), ALU.subtract).then_inc(unit_rest, 1)

            def operand_left(lo, full, hi, n):
                dve.wait_ge(op_top, n + 1)
                dve.tensor_tensor(lo, full, hi.bitcast(F32), ALU.subtract).then_inc(op_rest, 1)

            maxima(0)
            for hd in range(NH):
                normalise(hd)
                if hd + 1 < NH:
                    maxima(hd + 1)
                if hd in (4, 6):
                    unit_left(hd // 2 - 2)
            for hd in range(NH):
                operand_left(o_lo[:, hd], qn[:, hd], o_hi[:, hd], A_SPLIT + hd)
            for j in range(4):
                unit_left(U_GB + j + 2)
            for c in range(ND):
                dve.wait_ge(yb_mm, c + 1)
                dve.wait_ge(gb_sb, c + 1)
                dve.tensor_tensor(merged[:, c], bank[c][:], sigB[:, c], ALU.mult).then_inc(yb_sb, 1)
                if c % 2:
                    unit_left(U_O + c // 2 + 2)
            for g in range(12):
                if g % 4 == 0:
                    unit_left(U_V + g // 2 + 2)
                dve.wait_ge(v_sb, g + 1)
                link(dve.bn_stats(bst[:, g % 4, g // 4], vt[:, g % 4, 512 * (g // 4):512 * (g // 4 + 1)]))
                if g % 4 == 3:
                    unit_left(U_V + g // 2 + 2)
            for t in range(NT):
                dve.bn_aggr(bag[:, t], bst[:, t].rearrange("p a b -> p (a b)")).then_inc(v_var, 1)
            dve.wait_ge(v_rt, 1)
            invert(vrs[:], bag[:, :, 1], rnt[:])
            for t in range(NT):
                dve.tensor_scalar(vt[:, t], vt[:, t], bag[:, t, 0:1], vrs[:, t:t + 1], ALU.subtract, ALU.mult)\
                    .then_inc(v_ln, 1)
            for j in range(6):
                unit_left(U_U + j + 2)
            dve.wait_ge(bias_in, 48)
            for g in range(NG):
                dve.wait_ge(sp_mm, g + 1)
                past(dve, y_ok, g - 1)
                dve.scalar_tensor_tensor(tmp[g % 2][:].rearrange("p (n t) -> p n t", n=NT),
                                         bank[g % 8][:].rearrange("p (n t) -> p n t", n=NT), gvg[:, g:g + 1],
                                         bsp[:, g].unsqueeze(1).to_broadcast([P, NT, P]), ALU.mult, ALU.add)\
                    .then_inc(sp_sb, 1)
            for g in range(NG // 2):
                operand_left(y_lo[:, g], uT[:, g], y_hi[:, g], O_SPLIT + g)
            for j in range(4):
                unit_left(U_GA + j + 2)
                for g in range(NG // 2 + 2 * j, min(NG // 2 + 2 * j + 2, NG)):
                    operand_left(y_lo[:, g], uT[:, g], y_hi[:, g], O_SPLIT + g)
            for c in range(ND):
                dve.wait_ge(gp_mm, c + 1)
                dve.wait_ge(ga_sb, c + 1)
                past(dve, mg_ok, c - 1)
                dve.tensor_tensor(tmp[c % 2][:], bank[(4 + c) % 8][:], sigA[:, c], ALU.mult).then_inc(gp_sb, 1)
                unit_left(U_GP + c + 2)
                if c:
                    operand_left(mg_lo[:, c - 1], merged[:, c - 1], mg_hi[:, c - 1], Y_SPLIT + c - 1)
            operand_left(mg_lo[:, ND - 1], merged[:, ND - 1], mg_hi[:, ND - 1], M_SPLIT - 1)
            unit_left(U_W + 2)
            dve.wait_ge(x_again, 16)
            for g in range(2 * NT):
                t, half = g % NT, g // NT
                dve.wait_ge(w_mm, g + 1)
                hs = h[:, t, 512 * half:512 * (half + 1)]
                ins = dve.tensor_tensor(hs, hs, bank[(4 + g) % 8][:], ALU.add)
                if half == 0:
                    ins.then_inc(w_sb, 1)
                else:
                    ins.then_inc(h_ok, 1)
                if g == 0:
                    unit_left(U_W + 3)
            for t in range(NT):
                dve.wait_ge(h_root, 2 * t + 2)
                inv_rms(NT + t)
                if t == 0:
                    dve.wait_ge(gmb_in, 16)
                dve.scalar_tensor_tensor(hn[:, t], h[:, t], rstd[:, NT + t:NT + t + 1], gmb[:], ALU.mult, ALU.mult)\
                    .then_inc(hn_ok, 1)
            dve.wait_ge(op_top, WR_SPLIT)
            dve.tensor_tensor(wr_lo[:], wr[:], wr_hi[:].bitcast(F32), ALU.subtract).then_inc(op_rest, 1)
            for t in range(NT):
                for half in range(2):
                    dve.wait_ge(op_top, WR_SPLIT + 2 * t + half + 1)
                    dst = (slice(None), slice(4 * half, 4 * half + 4), slice(P * t, P * (t + 1)))
                    dve.tensor_tensor(m_lo[dst], bank[MB[2 * t + half]][:].rearrange("p (k s) -> p k s", k=4),
                                      m_hi[dst].bitcast(F32), ALU.subtract).then_inc(op_rest, 1)

            grp, prob, eprob, score, cand, oh1, oh2, esel = r8
            m1, s1, i1, gw, p1, p2, ps, d1 = r1[:8]

            def bc8(v):
                return v[:].unsqueeze(2).to_broadcast([P, NT, EPG])

            def bct(v):
                return v[:].unsqueeze(1).to_broadcast([P, NT, EPG])

            def softmax8(src, dst, n):
                link(dve.tensor_reduce(m1[:], src, AX_X, ALU.max))
                dve.tensor_tensor(dst[:], src, bc8(m1), ALU.subtract).then_inc(rt_sub, 1)
                dve.wait_ge(rt_exp, n + 1)
                link(dve.tensor_reduce(s1[:], dst[:], AX_X, ALU.add))
                link(dve.reciprocal(s1[:], s1[:]))
                link(dve.tensor_tensor(dst[:], dst[:], bc8(s1), ALU.mult))

            def first_max(src, onehot):
                link(dve.tensor_reduce(m1[:], src[:], AX_X, ALU.max))
                link(dve.tensor_tensor(cand[:], src[:], bc8(m1), ALU.is_equal))
                link(dve.scalar_tensor_tensor(cand[:], cand[:], float(-EPG), bct(iota8up), ALU.mult, ALU.add))
                link(dve.tensor_reduce(i1[:], cand[:], AX_X, ALU.min))
                link(dve.tensor_tensor(onehot[:], bct(iota8), bc8(i1), ALU.is_equal))

            link(dve.memset(sel[:, NT], 0.0))
            link(dve.memset(iota8[:, 0:1], 0.0))
            for k in range(1, EPG):
                link(dve.memset(iota8[:, k:k + 1], float(k)))
            link(dve.tensor_scalar(iota8up[:], iota8[:], float(EPG), None, ALU.add))
            for r in range(2):
                dve.wait_ge(w_hi, r + 1)
                dve.tensor_tensor(gu_lo[0][:, r].rearrange("p k n -> p (k n)"), raw[r][:],
                                  gu_hi[0][:, r].rearrange("p k n -> p (k n)").bitcast(F32), ALU.subtract)\
                    .then_inc(w_lo, 1)
            dve.wait_ge(w_hi, 3)
            dve.tensor_tensor(dn_lo[0][:].rearrange("p k n -> p (k n)"), raw[2][:],
                              dn_hi[0][:].rearrange("p k n -> p (k n)").bitcast(F32), ALU.subtract).then_inc(w_lo, 1)
            dve.wait_ge(lg_mm, 2)
            link(dve.tensor_copy(lg[:], bank[3][:, 0:NT * (NGRP + NE)].rearrange("p (t n) -> p t n", t=NT)))
            softmax8(lg[:, :, 0:NGRP], prob, 0)
            link(dve.tensor_tensor(score[:], prob[:], bct(brg), ALU.add))
            first_max(score, grp)
            link(dve.tensor_tensor(score[:], prob[:], grp[:], ALU.mult))
            link(dve.tensor_reduce(gw[:], score[:], AX_X, ALU.add))

            def choose(src):
                for t in range(NT):
                    ins = dve.tensor_tensor(rt_e[:, t], src(t), grp[:, t].unsqueeze(2).to_broadcast([P, NGRP, EPG]),
                                            ALU.mult)
                link(ins)
                link(dve.tensor_reduce(esel[:], rt_e[:].rearrange("p t g e -> p t e g"), AX_X, ALU.add))

            choose(lambda t: lg[:, t, NGRP:NGRP + NE].rearrange("p (g e) -> p g e", g=NGRP))
            softmax8(esel[:], eprob, 1)
            choose(lambda t: bre[:])
            link(dve.tensor_tensor(score[:], eprob[:], esel[:], ALU.add))
            first_max(score, oh1)
            link(dve.scalar_tensor_tensor(score[:], oh1[:], MASKED, score[:], ALU.mult, ALU.add))
            first_max(score, oh2)
            for oh, s4 in ((oh1, sel1), (oh2, sel2)):
                for t in range(NT):
                    ins = dve.tensor_tensor(s4[:, t], grp[:, t].unsqueeze(2).to_broadcast([P, NGRP, EPG]),
                                            oh[:, t].unsqueeze(1).to_broadcast([P, NGRP, EPG]), ALU.mult)
            link(ins)
            flat = "p t g e -> p t (g e)"
            dve.tensor_tensor(sel[:, 0:NT], sel1[:].rearrange(flat), sel2[:].rearrange(flat), ALU.add).then_inc(sel_ok, 1)
            for oh, pk in ((oh1, p1), (oh2, p2)):
                link(dve.tensor_tensor(cand[:], oh[:], eprob[:], ALU.mult))
                link(dve.tensor_reduce(pk[:], cand[:], AX_X, ALU.add))
            link(dve.tensor_tensor(ps[:], p1[:], p2[:], ALU.add))
            link(dve.reciprocal(ps[:], ps[:]))
            link(dve.tensor_tensor(ps[:], ps[:], gw[:], ALU.mult))
            link(dve.tensor_tensor(wts[:, 0], p1[:], ps[:], ALU.mult))
            link(dve.tensor_tensor(wts[:, 1], p2[:], ps[:], ALU.mult))
            dve.wait_ge(iota_ok, 2)
            dve.wait_ge(aid_ok, 2)
            for k, s4 in enumerate((sel1, sel2)):
                dve.tensor_tensor(number[k][:], s4[:].rearrange(flat),
                                  aid_1[:, k].unsqueeze(2).to_broadcast([P, NT, NE]), ALU.mult).then_inc(at_ok, 1)
            dve.wait_ge(rank_mm, 1)
            for k, s4 in enumerate((sel1, sel2)):
                link(dve.tensor_tensor(rt_e[:].rearrange(flat), s4[:].rearrange(flat),
                                       bank[2][:, 0:NT * NE].rearrange("p (t e) -> p t e", t=NT), ALU.mult))
                link(dve.tensor_reduce(r_of[:, k], rt_e[:].rearrange(flat), AX_X, ALU.add))
                dve.tensor_tensor(at_rank[k][:], iota_r[:].unsqueeze(1).to_broadcast([P, NT, CAP]),
                                  r_of[:, k].unsqueeze(2).to_broadcast([P, NT, CAP]), ALU.is_equal).then_inc(at_ok, 1)
            dve.tensor_reduce(most[:], bank[2][0:1, NT * NE:NT * NE + NE], AX_X, ALU.max).then_inc(most_ok, 1)
            dve.wait_ge(most_ok, 1)
            dve.tensor_copy(most_i[:], most[:]).then_inc(most_ok, 1)
            dve.wait_ge(tab_mm, 1)
            link(dve.tensor_scalar(tab_f[:], bank[3][0:CAP, 0:NE], 0.0, float(EMPTY + 1), ALU.is_equal, ALU.mult))
            link(dve.tensor_tensor(tab_f[:], tab_f[:], bank[3][0:CAP, 0:NE], ALU.add))
            link(dve.tensor_scalar(tabs[:, 0], tab_f[:], -1.0, None, ALU.add))
            dve.tensor_scalar(toks[:, 0], tabs[:, 0], TOKEN_BITS, None, ALU.bitwise_and).then_inc(toks_ok, 1)
            for k in range(2):
                link(dve.tensor_scalar(r_of[:, k], r_of[:, k], float(NE), None, ALU.mult))
                s4 = (sel1, sel2)[k]
                link(dve.tensor_tensor(rt_e[:].rearrange(flat), s4[:].rearrange(flat), iota_e[:], ALU.mult))
                link(dve.tensor_reduce(e_of[:, k], rt_e[:].rearrange(flat), AX_X, ALU.add))
                link(dve.tensor_tensor(r_of[:, k], r_of[:, k], e_of[:, k], ALU.add))
                ins = dve.tensor_copy(dst_i[:, k], r_of[:, k])
            ins.then_inc(dst_ok, 1)

            def rest(n, slot_of, r, b):
                dve.wait_ge(w_hi, n + 1)
                hi, lo = (gu_hi[b][:, r], gu_lo[b][:, r]) if r < 2 else (dn_hi[b][:], dn_lo[b][:])
                dve.tensor_tensor(lo.rearrange("p k n -> p (k n)"), raw[slot_of][:],
                                  hi.rearrange("p k n -> p (k n)").bitcast(F32), ALU.subtract).then_inc(w_lo, 1)

            def rows_rest(e, b):
                dve.wait_ge(xt_top, e + 1)
                for half in range(2):
                    ins = dve.tensor_tensor(xt_lo[b][:, 4 * half:4 * half + 4],
                                            bank[half][:, 0:4 * CAP].rearrange("p (k c) -> p k c", k=4),
                                            xt_hi[b][:, 4 * half:4 * half + 4].bitcast(F32), ALU.subtract)
                ins.then_inc(xt_rest, 1)

            def hidden_rest(e, b):
                dve.wait_ge(ht_top, e + 1)
                dve.tensor_tensor(ht_lo[b][:], bank[4 + b][:, 0:2 * CAP].rearrange("p (j c) -> p j c", j=2),
                                  ht_hi[b][:].bitcast(F32), ALU.subtract).then_inc(ht_rest, 1)

            def gated(e, b, wait_ht=True):
                dve.wait_ge(silu, e + 1)
                if wait_ht:
                    past(dve, ht_mm, e - 1)
                dve.tensor_tensor(hm[b][0:CAP], sg[b][0:CAP], bank[2 + b][0:CAP, FE:2 * FE], ALU.mult)\
                    .then_inc(h_mul, 1)

            def expert_step(i, u, first=False, last=False):
                e = i * NBUF + u
                n = UNITS * u + 2
                if not first:
                    hidden_rest(e - 1, (u + 1) % 2)
                if not last:
                    rows_rest(e + 1, (u + 1) % 2)
                if not first:
                    rest(UNITS * e + 2, n % NRAW, 2, u % 2)
                if not last:
                    rest(UNITS * e + 3, (n + 1) % NRAW, 0, (u + 1) % 2)
                gated(e, u % 2)
                if not last:
                    rest(UNITS * e + 4, (n + 2) % NRAW, 1, (u + 1) % 2)

            rows_rest(0, 0)
            for u in range(NBUF):
                expert_step(0, u, first=(u == 0))
            with dve.Fori(1, NE // NBUF - 1) as i:
                for u in range(NBUF):
                    expert_step(i, u)
            for u in range(NBUF):
                expert_step(NE // NBUF - 1, u, last=(u == NBUF - 1))
            hidden_rest(NE - 1, 1)
            most_v = dve.value_load(most_i[0:1, 0:1], min_val=0, max_val=S)
            with dve.If(most_v > CAP):
                dve.wait_ge(tab_in, 16)
                dve.tensor_scalar(toks[:], tabs[:], TOKEN_BITS, None, ALU.bitwise_and).then_inc(toks_ok, 1)
                with dve.Fori(1, NBLK) as b:
                    with dve.Fori(0, NE) as e:
                        n = b * NE + e
                        rows_rest(n, 0)
                        for r in range(UNITS):
                            rest(n * UNITS + r, r, r, 0)
                        gated(n, 0, wait_ht=False)
                        hidden_rest(n, 0)

            for q in range(3):
                dve.wait_ge(op_top, H_SPLIT + q + 1)
                dve.tensor_tensor(wpg_lo[:, 2 * q:2 * q + 2], wpg[:, 2 * q:2 * q + 2],
                                  wpg_hi[:, 2 * q:2 * q + 2].bitcast(F32), ALU.subtract).then_inc(op_rest, 1)

            def third_norm(t):
                dve.wait_ge(h2_root, 2 * t + 2)
                inv_rms(2 * NT + t)
                dve.scalar_tensor_tensor(n3[t][:], h[:, t], rstd[:, 2 * NT + t:2 * NT + t + 1], gplb[:],
                                         ALU.mult, ALU.mult).then_inc(n3_ok, 1)

            def third_rest(t):
                for half in range(2):
                    dve.wait_ge(op_top, PG_SPLIT + 2 * t + half + 1)
                    dst = (slice(None), slice(4 * half, 4 * half + 4), slice(P * t, P * (t + 1)))
                    dve.tensor_tensor(n3_lo[dst], bank[2 * (t % 2) + half][:].rearrange("p (k s) -> p k s", k=4),
                                      n3_hi[dst].bitcast(F32), ALU.subtract).then_inc(op_rest, 1)

            def add_experts(t):
                dve.wait_ge(y_in[t], 32)
                link(dve.scalar_tensor_tensor(ysum[:, t % 2], y1[:, t], wts[:, 0, t:t + 1], h[:, t],
                                              ALU.mult, ALU.add))
                dve.scalar_tensor_tensor(h[:, t], y2[:, t], wts[:, 1, t:t + 1], ysum[:, t % 2], ALU.mult, ALU.add)\
                    .then_inc(h2_ok, 1)

            add_experts(0)
            add_experts(1)
            dve.wait_ge(gplb_in, 16)
            third_norm(0)
            third_rest(0)
            third_norm(1)
            add_experts(2)
            third_norm(2)
            add_experts(3)
            third_norm(3)
            dve.wait_ge(pp_sb, 8)
            dve.wait_ge(gfin_in, 16)
            for t in range(NT):
                if t + 1 < NT:
                    third_rest(t + 1)
                dve.wait_ge(g_sb, 2 * t + 2)
                dve.tensor_tensor(sgt[:, t], sgt[:, t], pp[:, t], ALU.mult).then_inc(pg_ok, 1)
                dve.wait_ge(pg_ok, t + 1)
                dve.tensor_tensor(h[:, t], h[:, t], sgt[:, t], ALU.add).then_inc(h3_ok, 1)
                dve.wait_ge(h3_root, 2 * t + 2)
                inv_rms(t)
                dve.scalar_tensor_tensor(fin[:, t], h[:, t], rstd[:, t:t + 1], gfin[:], ALU.mult, ALU.mult)\
                    .then_inc(fin_ok, 1)

        @block.tensor
        def _(pe):
            def product(dst, pairs):
                for n, (l, r) in enumerate(pairs):
                    ins = pe.matmul(dst, l, r, start=(n == 0), stop=(n == len(pairs) - 1))
                return ins

            pe.wait_ge(ident_ok, 2)
            pe.wait_ge(ws_in, 16)
            for b in range(3):
                for g in range(4 * b, 4 * b + 4):
                    ins = pe.transpose(bank[b][:, P * (g % 4):P * (g % 4 + 1)], wsn[:, g], ident[:])
                ins.then_inc(ws_mm, 1)
            for t in range(NT):
                pe.wait_ge(xn_ok, t + 1)
                for half in range(2):
                    b = (3 + 2 * t + half) % 8
                    if b < 3:
                        pe.wait_ge(ws_sb, b + 1)
                    for k in range(4):
                        ins = pe.transpose(bank[b][:, P * k:P * (k + 1)],
                                           xn[:, t, P * (4 * half + k):P * (4 * half + k + 1)], ident[:])
                    ins.then_inc(x_mm, 1)
            pe.wait_ge(aT_ok, 2 * NT)

            arrived(pe, PC_C)
            for c in range(5):
                if c == 4:
                    arrived(pe, PC_C + 1)
                w = piece(PC_C)[:, :, P * c:P * (c + 1)] if c < 4 else piece(PC_C + 1)[:, :, 0:P]
                ins = product(bank[c][:], [(w[:, k], aT[:, k]) for k in range(ND)])
                ins.then_inc(c_mm, 1)
            pe.wait_ge(c_sq, 4)
            pe.sem_inc(piece_used, 1)
            pe.wait_ge(wkr_ok, 6)
            product(bank[7][:], [(wkr[:, k, 0], aT[:, k]) for k in range(ND)]).then_inc(kr_mm, 1)
            pe.wait_ge(masks_ok, 4)
            pe.wait_ge(c_sq, 5)
            product(bank[5][:], [(ones[:], csq[:, c]) for c in range(3)]).then_inc(ss_mm, 1)
            product(bank[6][:], [(ones[:], csq[:, c]) for c in range(3, 5)]).then_inc(ss_mm, 1)
            pe.wait_ge(c_sb, 1)
            product(bank[0][:], [(wkr[:, k, 1], aT[:, k]) for k in range(ND)]).then_inc(kr_mm, 1)
            pe.wait_ge(c_sq, 5)
            pe.sem_inc(piece_used, 1)

            pe.wait_ge(cT_ok, 5)
            DB = [5, 6, 7, 0]
            na, nd = [0], [0]

            def to_act(pairs):
                a = na[0]
                na[0] += 1
                past(pe, qkA_sb, a - 3)
                return product(bank[1 + a % 4][:], pairs)

            def to_dve(pairs):
                d = nd[0]
                nd[0] += 1
                if d == 2:
                    pe.wait_ge(kr_mul, 2)
                past(pe, qkD_sb, d - 3)
                return product(bank[DB[d % 4]][:], pairs)

            for half in range(2):
                arrived(pe, PC_UQ + half)
                w = piece(PC_UQ + half)
                for j in range(4):
                    to_act([(w[:, k, QW * j:QW * j + NOPE], cT[:, k]) for k in range(3)]).then_inc(qkA_mm, 1)
                pe.wait_ge(wpe_ok, 3 * half + 3)
                for j in range(2):
                    to_dve([(wpe[:, k, 2 * j:2 * j + 2].rearrange("p h c -> p (h c)"), cT[:, k]) for k in range(3)])\
                        .then_inc(qkD_mm, 1)
                    to_dve([(wpes[:, k, 2 * j:2 * j + 2].rearrange("p h c -> p (h c)"), cT[:, k]) for k in range(3)])\
                        .then_inc(qkD_mm, 1)
                pe.wait_ge(qkA_sb, 4 * half + 4)
                pe.sem_inc(piece_used, 1)
            arrived(pe, PC_UKV)
            w = piece(PC_UKV)
            for j in range(NH):
                to_act([(w[:, k, KVW * j:KVW * j + NOPE], cT[:, 3 + k]) for k in range(2)]).then_inc(qkA_mm, 1)
                t, q = j // 2, j % 2
                wv = w.rearrange("p k (h c) -> p k h c", c=KVW)[:, :, 4 * q:4 * q + 4, NOPE:KVW]
                ins = to_dve([(cT[:, 3 + k, P * t:P * (t + 1)], wv[:, k]) for k in range(2)])
                ins.then_inc(qkD_mm, 1)
            pe.wait_ge(qkA_sb, 16)
            pe.wait_ge(qkD_sb, 16)
            pe.sem_inc(piece_used, 1)
            pe.wait_ge(kpe_ok, 1)
            pe.wait_ge(pe_add, NH // 2)

            def head_scores(hd):
                past(pe, s_exp, NT * hd)
                r = ROPE * (hd % 2)
                for i in s_order:
                    o, kw = scores(i), P * (i + 1)
                    pe.matmul(o, qn[:, hd, P * i:P * (i + 1)], kn[:, hd, 0:kw], start=True, stop=False)
                    pe.matmul(o, qpe[r:r + ROPE, hd // 2, P * i:P * (i + 1)], kpe[r:r + ROPE, 0:kw],
                              start=False, stop=False)
                    pe.matmul(o[:, P * i:kw], mrow[:], mcol[:], start=False, stop=True).then_inc(s_mm, 1)

            def head_values(hd):
                pe.wait_ge(p_ok, NT * (hd + 1))
                past(pe, pt_sb, NT * hd)
                for j in range(NT):
                    for i in range(j, NT):
                        ins = pe.transpose(turned(j)[:, P * (i - j):P * (i - j + 1)],
                                           pr[hd % 2][:, p_off[i] + P * j:p_off[i] + P * (j + 1)], ident[:])
                ins.then_inc(pt_mm, 1)
                past(pe, o_sb, hd - 1)
                for j in range(NT):
                    pe.wait_ge(pt_sb, NT * hd + j + 1)
                    ins = pe.matmul(bank[6 + hd % 2][:, P * j:S], vv[:, j, hd],
                                    prT[hd % 2][:, t_off[j]:t_off[j] + P * (NT - j)], start=(j == 0), stop=(j == NT - 1))
                ins.then_inc(o_mm, 1)

            head_scores(0)
            for hd in range(NH):
                if hd + 1 < NH:
                    head_scores(hd + 1)
                head_values(hd)

            def product3(dst, triples, start=True, stop=True):
                for n, (a_hi_, a_lo_, b_hi_, b_lo_) in enumerate(triples):
                    pe.matmul(dst, a_hi_, b_hi_, start=(start and n == 0), stop=False)
                    pe.matmul(dst, a_hi_, b_lo_, start=False, stop=False)
                    ins = pe.matmul(dst, a_lo_, b_hi_, start=False, stop=(stop and n == len(triples) - 1))
                return ins

            def feature_chunks(first, n_units, op_hi, op_lo, free, done):
                c = 0
                for n in range(first, first + n_units):
                    pe.wait_ge(unit_rest, n + 1)
                    hi, lo = unit_view(unit_hi[n % 2], n), unit_view(unit_lo[n % 2], n)
                    for cc in range(hi.shape[2] // P):
                        b, w = free(c), slice(P * cc, P * (cc + 1))
                        product3(bank[b][:], [(hi[:, k, w], lo[:, k, w], op_hi[:, k], op_lo[:, k])
                                              for k in range(hi.shape[1])]).then_inc(done, 1)
                        c += 1

            def token_tiles(first, groups, op_hi, op_lo, free, done):
                for j in range(groups):
                    for kh in range(2):
                        n = first + 2 * j + kh
                        pe.wait_ge(unit_rest, n + 1)
                        if done is w_mm and j == 0:
                            pe.wait_ge(op_rest, Y_SPLIT + HK * (kh + 1))
                        hi, lo = unit_view(unit_hi[n % 2], n), unit_view(unit_lo[n % 2], n)
                        for t in range(NT):
                            b, c = free(NT * j + t, kh), slice(P * t, P * (t + 1))
                            ins = product3(bank[b][:], [(op_hi[:, HK * kh + k, c], op_lo[:, HK * kh + k, c], hi[:, k],
                                                         lo[:, k]) for k in range(HK)], start=(kh == 0), stop=(kh == 1))
                            if kh:
                                ins.then_inc(done, 1)
                        if kh == 0:
                            ins.then_inc(half_mm, 1)

            def gb_bank(c):
                if c == 3:
                    pe.wait_ge(pt_sb, NT * NH)
                if c == 6:
                    pe.wait_ge(o_sb, NH)
                return c

            pe.wait_ge(s_exp, NT * NH)
            pe.wait_ge(op_rest, A_SPLIT)
            feature_chunks(U_GB, 4, a_hi, a_lo, gb_bank, gb_mm)

            def yb_bank(c):
                pe.wait_ge(gb_sb, c + 1)
                return c

            pe.wait_ge(op_rest, O_SPLIT)
            feature_chunks(U_O, 4, o_hi, o_lo, yb_bank, yb_mm)

            def v_bank(g, kh):
                if kh == 0 and g < 8:
                    pe.wait_ge(yb_sb, g + 1)
                elif kh == 0:
                    pe.wait_ge(v_sb, g - 7)
                return g % 8

            token_tiles(U_V, 3, a_hi, a_lo, v_bank, v_mm)

            def u_bank(c):
                if c < 8:
                    pe.wait_ge(v_sb, c + 5)
                else:
                    pe.wait_ge(u_sb, c - 7)
                return (4 + c) % 8

            feature_chunks(U_U, 6, a_hi, a_lo, u_bank, u_mm)

            pe.wait_ge(v_ln, NT)
            pe.wait_ge(ws_zero, 1)
            for g in range(NG):
                if g < 8:
                    pe.wait_ge(u_sb, g + 5)
                else:
                    pe.wait_ge(sp_sb, g - 7)
                for n in range(NT):
                    ins = pe.matmul(bank[g % 8][:, P * n:P * (n + 1)], vt[:, n, P * g:P * (g + 1)], wsT[:, g],
                                    start=True, stop=True)
                ins.then_inc(sp_mm, 1)

            def ga_bank(c):
                pe.wait_ge(sp_sb, c + 5)
                return (4 + c) % 8

            feature_chunks(U_GA, 4, a_hi, a_lo, ga_bank, ga_mm)

            def gp_bank(c):
                pe.wait_ge(ga_sb, c + 1)
                return (4 + c) % 8

            pe.wait_ge(op_rest, Y_SPLIT)
            feature_chunks(U_GP, 8, y_hi, y_lo, gp_bank, gp_mm)

            def w_bank(g, kh):
                if kh == 0:
                    pe.wait_ge(gp_sb, g + 1)
                return (4 + g) % 8

            token_tiles(U_W, 2, mg_hi, mg_lo, w_bank, w_mm)

            pe.wait_ge(p_in, 16)
            pe.wait_ge(w_sb, 2)
            for k in range(2):
                for t in range(NT):
                    ins = pe.transpose(bank[4 + k][:, P * t:P * (t + 1)], psb[:, t, P * k:P * (k + 1)], ident[:])
                ins.then_inc(pt2_mm, 1)
            pe.wait_ge(pt2_sb, 2)
            pe.wait_ge(wpp_in, 16)

            def embed(g, b):
                t, half = g // 2, g % 2
                return product(bank[b][:], [(pT[:, k, P * t:P * (t + 1)], wpp[:, k, 512 * half:512 * (half + 1)])
                                            for k in range(2)])

            pe.wait_ge(w_sb, NT)
            pe.wait_ge(h_ok, 2)
            for g in range(2):
                embed(g, 6 + g).then_inc(pp_mm, 1)
            pe.wait_ge(h_ok, NT)
            for t in range(NT):
                pe.wait_ge(hn_ok, t + 1)
                if t == 2:
                    pe.wait_ge(pp_sb, 2)
                for half in range(2):
                    for k in range(4):
                        ins = pe.transpose(bank[MB[2 * t + half]][:, P * k:P * (k + 1)],
                                           hn[:, t, 4 * half + k:D:ND], ident[:])
                    ins.then_inc(m_mm, 1)
            pe.wait_ge(op_rest, WR_SPLIT)
            pe.wait_ge(op_rest, H_SPLIT)
            product3(bank[2][0:NGRP + NE, :], [(wr_hi[:, k], wr_lo[:, k], m_hi[:, k], m_lo[:, k]) for k in range(ND)])\
                .then_inc(lg_mm, 1)
            pe.wait_ge(lgT_ok, 1)
            for t in range(NT):
                ins = pe.transpose(bank[3][:, (NGRP + NE) * t:(NGRP + NE) * (t + 1)], lgT[:, P * t:P * (t + 1)],
                                   ident[0:NGRP + NE, 0:NGRP + NE])
            ins.then_inc(lg_mm, 1)
            pe.wait_ge(sel_ok, 1)
            def ranks(a, b):
                return bank[2][:, NE * a:NE * b]

            def chosen(a, b):
                return sel[:, a:b].rearrange("p t e -> p (t e)")

            pe.matmul(ranks(0, NT + 1), before[:], chosen(0, NT + 1), start=True, stop=False)
            for d in range(1, NT + 1):
                ins = pe.matmul(ranks(d, NT + 1), ones[:], chosen(0, NT + 1 - d), start=False, stop=(d == NT))
            ins.then_inc(rank_mm, 1)
            for g in range(2, 8):
                if g == 4:
                    pe.wait_ge(at_ok, 4)
                    product(bank[3][0:CAP, 0:NE], [(at_rank[k][:, t], number[k][:, t])
                                                   for k in range(2) for t in range(NT)]).then_inc(tab_mm, 1)
                embed(g, (g + 2) % 8).then_inc(pp_mm, 1)

            def turn_rows(e, b, fills):
                pe.wait_ge(xg_in[b], fills)
                past(pe, xt_rest, e)
                for k in range(ND):
                    ins = pe.transpose(bank[k // 4][:, CAP * (k % 4):CAP * (k % 4 + 1)], xg[b][0:CAP, k:D:ND],
                                       ident[0:CAP, 0:CAP])
                ins.then_inc(xt_mm, 1)

            def gate_up(e, b, wait_mul=True):
                pe.wait_ge(xt_rest, e + 1)
                pe.wait_ge(w_lo, e * UNITS + 2)
                if wait_mul:
                    past(pe, h_mul, e - 1)
                product3(bank[2 + b][0:CAP, :], [(xt_hi[b][:, k], xt_lo[b][:, k], gu_hi[b][:, :, k], gu_lo[b][:, :, k])
                                                 for k in range(ND)]).then_inc(gu_mm, 1)

            def turn_hidden(e, b, wait_rest=True):
                pe.wait_ge(h_mul, e + 1)
                if wait_rest:
                    past(pe, ht_rest, e - 1)
                for j in range(2):
                    ins = pe.transpose(bank[4 + b][:, CAP * j:CAP * (j + 1)], hm[b][0:CAP, j:FE:2],
                                       ident[0:CAP, 0:CAP])
                ins.then_inc(ht_mm, 1)

            def down(e, b):
                pe.wait_ge(ht_rest, e + 1)
                pe.wait_ge(w_lo, e * UNITS + 3)
                past(pe, y_sb, e)
                for half in range(2):
                    c = slice(512 * half, 512 * (half + 1))
                    ins = product3(bank[6 + half][0:CAP, :],
                                   [(ht_hi[b][:, j], ht_lo[b][:, j], dn_hi[b][:, j, c], dn_lo[b][:, j, c])
                                    for j in range(2)])
                ins.then_inc(y_mm, 1)

            def expert_step(i, u, first=False, last=False):
                e = i * NBUF + u
                ni, nu = (i, u + 1) if u + 1 < NBUF else (i + 1, 0)
                if not first:
                    turn_hidden(e - 1, (u + 1) % 2)
                if not last:
                    turn_rows(e + 1, nu % 2, 16 * (ni * 2 + nu // 2 + 1))
                gate_up(e, u % 2)
                if not first:
                    down(e - 1, (u + 1) % 2)

            pe.wait_ge(pp_sb, 8)
            pe.wait_ge(most_ok, 2)
            turn_rows(0, 0, 16)
            for u in range(NBUF):
                expert_step(0, u, first=(u == 0))
            with pe.Fori(1, NE // NBUF - 1) as i:
                for u in range(NBUF):
                    expert_step(i, u)
            for u in range(NBUF):
                expert_step(NE // NBUF - 1, u, last=(u == NBUF - 1))
            turn_hidden(NE - 1, 1)
            down(NE - 1, 1)
            most_v = pe.value_load(most_i[0:1, 0:1], min_val=0, max_val=S)
            with pe.If(most_v > CAP):
                with pe.Fori(1, NBLK) as b:
                    with pe.Fori(0, NE) as e:
                        n = b * NE + e
                        turn_rows(n, 0, ((b - 1) * NE + e) * 16 + (16 * NE // 2 + 16))
                        gate_up(n, 0, wait_mul=False)
                        turn_hidden(n, 0, wait_rest=False)
                        down(n, 0)

            def turn_third(t):
                pe.wait_ge(n3_ok, t + 1)
                for half in range(2):
                    if 2 * t + half > 3:
                        pe.wait_ge(op_rest, N3_REST + 2 * t + half - 3)
                    for k in range(4):
                        ins = pe.transpose(bank[2 * (t % 2) + half][:, P * k:P * (k + 1)],
                                           n3[t][:, 4 * half + k:D:ND], ident[:])
                    ins.then_inc(n_mm, 1)

            turn_third(0)
            pe.wait_ge(op_rest, N3_REST)
            for t in range(NT):
                pe.wait_ge(op_rest, N3_REST + 2 * t + 2)
                past(pe, g_sb, 2 * (t - 1))
                tok = slice(P * t, P * (t + 1))
                for half in range(2):
                    if half and t + 1 < NT:
                        turn_third(t + 1)
                    c, b = slice(512 * half, 512 * (half + 1)), bank[4 + 2 * (t % 2) + half][:]
                    gate = [(n3_hi[:, k, tok], n3_lo[:, k, tok], wpg_hi[:, k, c], wpg_lo[:, k, c]) for k in range(ND)]
                    product3(b, gate[0:6], stop=False)
                    pe.wait_ge(wpg_rest, 1)
                    ins = product3(b, gate[6:8], start=False)
                ins.then_inc(g_mm, 1)


_INS = ["x", "p", "g_mix", "w_in", "g_gv", "w_spatial", "b_spatial", "w_gproj", "g_cq", "w_uq", "g_ckv", "w_ukv",
        "w_mla_o", "w_out", "g_moe", "w_router_g", "b_router_g", "w_router_e", "b_router_e", "w_e_gate", "w_e_up",
        "w_e_down", "g_ple", "w_ple_gate", "w_ple_proj", "g_final"]


def _rope_tables(np):
    inv = (10000.0 ** (-np.arange(0, 64, 2, dtype=np.float32) / np.float32(64))).astype(np.float32)
    ang = (np.arange(512, dtype=np.float32)[None, :] * inv[:, None]).astype(np.float32)
    cos, sin = np.cos(ang).astype(np.float32), np.sin(ang).astype(np.float32)
    return np.concatenate([cos] * 4), np.concatenate([-sin, sin, -sin, sin])


def kernel(**inputs):
    import numpy as _np
    import concourse.bacc as _bacc
    from concourse import mybir as _mybir
    from concourse.bass_utils import run_bass_kernel_spmd as _run

    nc = _bacc.Bacc("TRN2", target_bir_lowering=False, num_devices=1)
    arrays, args = {}, []
    cos, sin = _rope_tables(_np)
    for name, a in [(n, inputs[n]) for n in _INS] + [("cos", cos), ("sin", sin)]:
        a = _np.ascontiguousarray(a)
        arrays[f"in_{name}_dram"] = a
        args.append(nc.dram_tensor(f"in_{name}_dram", a.shape, _mybir.dt.from_np(a.dtype), kind="ExternalInput").ap())
    args.append(nc.dram_tensor("out_0_dram", (1, 512, 1024), _mybir.dt.float32, kind="ExternalOutput").ap())
    build(nc, *args)
    r = _run(nc, [arrays], core_ids=[0])
    return r.results[0]["out_0_dram"]
```

```python
from contextlib import ExitStack

import concourse.bass as bass
from concourse import mybir
from concourse.alu_op_type import AluOpType as ALU

ACT = mybir.ActivationFunctionType
F32 = mybir.dt.float32
F32R = mybir.dt.float32r
I32 = mybir.dt.int32
AX_X = mybir.AxisListType.X

P = 128
S = 512
D = 1024
NT = S // P
ND = D // P
GW = 1536
NG = GW // P
NH = 8
QL = 384
KVL = 256
NOPE = 128
ROPE = 64
HR = ROPE // 2
VH = 128
QW = NOPE + ROPE
KVW = NOPE + VH
PLE = 256
NE = 64
NGRP = 8
EPG = NE // NGRP
FE = 256
CHUNK = 64
EPS = 1e-6
SCALE = float(QW) ** -0.5
MASKED = -1e30
CAP = 80
NBLK = (S + CAP - 1) // CAP
SLOTS = NBLK * CAP * NE
EMPTY = 4096
TOKEN_BITS = EMPTY | (S - 1)
NBUF = 4
KB = 1024
SBUF0 = 16896
V_COL, C_COL = GW, 2 * GW
GA_COL = C_COL + QL + KVL + ROPE
GB_COL = GA_COL + D


def build(nc, x, p, g_mix, w_in, g_gv, w_spatial, b_spatial, w_gproj, g_cq, w_uq, g_ckv, w_ukv, w_mla_o, w_out,
          g_moe, w_router_g, b_router_g, w_router_e, b_router_e, w_e_gate, w_e_up, w_e_down, g_ple, w_ple_gate,
          w_ple_proj, g_final, cos_t, sin_t, out):
    with ExitStack() as ctx:
        def sem(name):
            return ctx.enter_context(nc.semaphore(name))

        def at(name, kb, shape, dt=F32):
            return nc.alloc_sbuf_tensor_at(name, shape, dt, offset=SBUF0 + int(kb * KB))

        CONST, SMALL = 184, 200
        PIECE_AT = [0, 16, 22, 31, 40]
        unit_raw = [at(f"unit_raw{i}", 8 * i, [P, ND * FE]) for i in range(3)]
        unit_hi = [at(f"unit_hi{i}", 24 + 16 * i, [P, ND * FE], F32R) for i in range(2)]
        unit_lo = [at(f"unit_lo{i}", 32 + 16 * i, [P, ND * FE], F32R) for i in range(2)]
        a_hi = at("a_hi", 56, [P, ND, S], F32R)
        a_lo = at("a_lo", 72, [P, ND, S], F32R)
        wkr = at("wkr", 88, [P, ND, 2, P])
        wkr_lo = at("wkr_lo", 88, [P, ND, 2, P], F32R)
        wkr_hi = at("wkr_hi", 144, [P, ND, 2, P], F32R)
        wpe = at("wpe", 96, [P, 2, 3, 4, ROPE])
        wpe_lo = at("wpe_lo", 96, [P, 2, 3, 4, ROPE], F32R)
        wpe_hi = at("wpe_hi", 144, [P, 2, 3, 4, ROPE], F32R)
        wc_hi = [at(f"wc_hi{c}", 104 + 4 * c, [P, ND, P], F32R) for c in range(5)]
        uq_hi = [at(f"uq_hi{i}", (138, 132)[i], [P, 3, 4, NOPE], F32R) for i in range(2)]
        ukv_hi = at("ukv_hi", 0, [P, 2, NH * KVW], F32R)
        vv = at("vv", 88, [P, NT, NH, VH])
        xs = at("xs", 104, [P, NT, D])
        xn = at("xn", 120, [P, NT, D])
        qn = at("qn", 104, [P, NH, S])
        o_lo = at("o_lo", 104, [P, NH, S], F32R)
        qpe = at("qpe", 120, [P, NH // 2, S])
        kpe = at("kpe", 128, [P, S])
        o_hi = at("o_hi", 120, [P, NH, S], F32R)
        kn = at("kn", 136, [P, NH, S])
        sigB = at("sigB", 136, [P, ND, S])
        cT = at("cT", 152, [P, 5, S])
        c_lo = at("c_lo", 152, [P, 5, S], F32R)
        c_hi = at("c_hi", 162, [P, 5, S], F32R)
        csq = at("csq", 162, [P, 5, S])
        wsn = at("wsn", 130, [P, NG, P])
        rbc = at("rbc", 172, [P, 2, S])
        gmxb = at("gmxb", 176, [P, D])
        ropeA = at("ropeA", 176, [P, S])
        ropeB = at("ropeB", 178, [P, S])
        junk = at("junk", 180, [P, D])
        pr = [at(f"pr{i}", 152 + 5 * i, [P, 1280]) for i in range(2)]
        prT = [at(f"prT{i}", 162 + 5 * i, [P, 1280]) for i in range(2)]
        merged = at("merged", 88, [P, ND, S])
        mg_lo = at("mg_lo", 88, [P, ND, S], F32R)
        mg_hi = at("mg_hi", 72, [P, ND, S], F32R)
        vt = at("vt", 104, [P, NT, GW])
        sigA = at("sigA", 104, [P, ND, S])
        uT = at("uT", 128, [P, NG, S])
        y_lo = at("y_lo", 128, [P, NG, S], F32R)
        y_hi = at("y_hi", 152, [P, NG, S], F32R)
        tmp = [at(f"tmp{i}", 176 + 2 * i, [P, S]) for i in range(2)]
        h = at("h", 56, [P, NT, D])
        pp = at("pp", 88, [P, NT, D])
        hn = at("hn", 104, [P, NT, D])
        psb = at("psb", 120, [P, NT, PLE])
        pT = at("pT", 124, [P, 2, S])
        m_hi = at("m_hi", 160, [P, ND, S], F32R)
        m_lo = at("m_lo", 72, [P, ND, S], F32R)
        trash2 = at("trash2", 160, [P, D])
        gmb = at("gmb", 172, [P, D])
        wpp = at("wpp", 176, [P, 2, D])
        gu = [at(f"gu{i}", (128, 16, 32, 160)[i], [P, 2, ND, FE]) for i in range(NBUF)]
        gu_lo = [at(f"gu_lo{i}", (128, 16, 32, 160)[i], [P, 2, ND, FE], F32R) for i in range(NBUF)]
        gu_hi = [at(f"gu_hi{i}", (0, 72)[i], [P, 2, ND, FE], F32R) for i in range(2)]
        dn = [at(f"dn{i}", (144, 152, 48, 176)[i], [P, 2, D]) for i in range(NBUF)]
        dn_lo = [at(f"dn_lo{i}", (144, 152, 48, 176)[i], [P, 2, D], F32R) for i in range(NBUF)]
        dn_hi = at("dn_hi", 120, [P, 2, D], F32R)
        xg = [at(f"xg{i}", 104 + 4 * i, [P, D]) for i in range(2)]
        XT_KB = ND * CAP * 4 / KB
        xt_place = [112, CONST + 16 - 2 * XT_KB]
        xt_hi = [at(f"xt_hi{i}", xt_place[i], [P, ND, CAP], F32R) for i in range(2)]
        xt_lo = [at(f"xt_lo{i}", xt_place[i] + XT_KB, [P, ND, CAP], F32R) for i in range(2)]
        HT_KB = 2 * CAP * 4 / KB
        ht_hi = [at(f"ht_hi{i}", 112 + 2 * XT_KB + HT_KB * i, [P, 2, CAP], F32R) for i in range(2)]
        ht_lo = [at(f"ht_lo{i}", 112 + 2 * XT_KB + HT_KB * (2 + i), [P, 2, CAP], F32R) for i in range(2)]
        ysb = [at(f"ysb{i}", CONST + 6 * i, [P, D]) for i in range(2)]
        cosT = at("cosT", CONST, [P, S])
        sinT = at("sinT", CONST + 2, [P, S])
        gfin = at("gfin", CONST, [P, D])
        bsp = at("bsp", CONST + 4, [P, NG, P])
        wr = at("wr", CONST + 4, [P, ND, NGRP + NE])
        wr_hi = at("wr_hi", 48, [P, ND, NGRP + NE], F32R)
        wr_lo = at("wr_lo", 51, [P, ND, NGRP + NE], F32R)
        lgT = at("lgT", 54, [NGRP + NE, S])
        at_rank = [at(f"at_rank{k}", 48 + 2 * k, [P, NT, CAP]) for k in range(2)]
        number = [at(f"number{k}", 52 + k, [P, NT, NE]) for k in range(2)]
        r8 = [at(f"r8_{i}", CONST + 6.5 + i / 8, [P, NT, EPG]) for i in range(8)]
        r1 = [at(f"r1_{i}", CONST + 7.5 + i / 32, [P, NT]) for i in range(8)]
        lg = at("lg", CONST + 8, [P, NT, NGRP + NE])
        hm = [at(f"hm{i}", CONST + 4 + i, [P, FE]) for i in range(2)]
        wsT = at("wsT", CONST + 10, [P, NG, P])
        rt_e = at("rt_e", CONST + 10, [P, NT, NGRP, EPG])
        sel1 = at("sel1", CONST + 11, [P, NT, NGRP, EPG])
        sel2 = at("sel2", CONST + 12, [P, NT, NGRP, EPG])
        sel = at("sel", CONST + 13, [P, NT + 1, NE])
        iota_e = at("iota_e", CONST + 15, [P, NT, NE])
        iota_r = at("iota_r", CONST + 9.5, [P, CAP])
        fill = at("fill", 152, [P, SLOTS // P], I32)
        wpg = at("wpg", 128, [P, ND, D])
        wpg_lo = at("wpg_lo", 128, [P, ND, D], F32R)
        wpg_hi = at("wpg_hi", 0, [P, ND, D], F32R)
        y1 = at("y1", 32, [P, NT, D])
        sgt = at("sgt", 32, [P, NT, D])
        ysum = at("ysum", 48, [P, 2, D])
        y2 = at("y2", 104, [P, NT, D])
        fin = at("fin", 104, [P, NT, D])
        n3 = [at(f"n3_{t}", (120, 124, 176, 180)[t], [P, D]) for t in range(NT)]
        n3_hi = at("n3_hi", 72, [P, ND, S], F32R)
        n3_lo = at("n3_lo", 160, [P, ND, S], F32R)
        trash3 = at("trash3", CONST + 12, [P, D])
        gplb = at("gplb", CONST + 4, [P, D])

        place = [SMALL * KB]

        def small(name, shape, dt=F32):
            n = 4
            for k in shape[1:]:
                n *= k
            t = nc.alloc_sbuf_tensor_at(name, shape, dt, offset=SBUF0 + place[0])
            place[0] += (n + 31) // 32 * 32
            return t

        ident = small("ident", [P, P])
        ones = small("ones", [P, P])
        before = small("before", [P, P])
        mrow = small("mrow", [1, P])
        mcol = small("mcol", [1, P])
        gvg = small("gvg", [P, NG])
        gcq = small("gcq", [P, 3])
        gckv = small("gckv", [P, 2])
        brg = small("brg", [P, NGRP])
        bre = small("bre", [P, NGRP, EPG])
        stat = small("stat", [P, 3 * NT])
        rstd = small("rstd", [P, 3 * NT])
        bst = small("bst", [P, NT, 3, 6])
        bag = small("bag", [P, NT, 2])
        vrs = small("vrs", [P, NT])
        rnt = small("rnt", [P, 4])
        eps = small("eps", [P, 1])
        mx = small("mx", [P, 2, NT])
        rs = small("rs", [P, 2, NT])
        ri = small("ri", [P, 2, NT])
        wts = small("wts", [P, 2, NT])
        tabs = small("tabs", [CAP, NBLK, NE], I32)
        toks = small("toks", [CAP, NBLK, NE], I32)
        idx_x = [small(f"idx_x{i}", [CAP, 1], I32) for i in range(2)]
        idx_y = [small(f"idx_y{i}", [CAP, 1], I32) for i in range(2)]
        iota8 = small("iota8", [P, EPG])
        iota8up = small("iota8up", [P, EPG])
        most = small("most", [1, 1])
        most_i = small("most_i", [1, 1], I32)
        dst_i = small("dst_i", [P, 2, NT], I32)
        aid = small("aid", [P, 2, NT], I32)
        aid_1 = small("aid_1", [P, 2, NT])
        r_of = small("r_of", [P, 2, NT])
        e_of = at("e_of", CONST + 7.75, [P, 2, NT])
        tab_f = at("tab_f", CONST + 6, [CAP, NE])
        assert SBUF0 + place[0] <= 229344, place[0]

        bank = [ctx.enter_context(nc.psum_tensor(f"bank{i}", [P, S], F32)) for i in range(8)]

        m_dram = nc.dram_tensor("m_rows", [S, D], F32)
        y_dram = nc.dram_tensor("y_rows", [2 * S, D], F32)
        tab_dram = nc.dram_tensor("slot_table", [SLOTS, 1], I32)

        piece_in = [sem(f"piece_in{i}") for i in range(5)]
        piece_used = sem("piece_used")
        unit_in = [sem(f"unit_in{i}") for i in range(3)]
        unit_top, unit_rest, half_mm = sem("unit_top"), sem("unit_rest"), sem("half_mm")
        op_top, op_rest = sem("op_top"), sem("op_rest")
        w_top, w_rest = sem("w_top"), sem("w_rest")
        W_KR, W_UQ, W_UKV = 6, 7, 11
        A_SPLIT = 2 * NT
        C_SPLIT = A_SPLIT + 5
        O_SPLIT = C_SPLIT + NH
        Y_SPLIT = O_SPLIT + NG
        M_SPLIT = Y_SPLIT + ND
        WR_SPLIT = M_SPLIT + 1
        H_SPLIT = WR_SPLIT + 2 * NT
        PG_SPLIT = H_SPLIT + 4
        N3_REST = H_SPLIT + 3
        x_in = [sem(f"x_in{t}") for t in range(NT)]
        gmx_in = sem("gmx_in")
        consts_in, rope_in, ws_in = sem("consts_in"), sem("rope_in"), sem("ws_in")
        x_again, p_in, wpp_in, wr_in, bias_in = (sem(n) for n in ("x_again", "p_in", "wpp_in", "wr_in", "bias_in"))
        gp_step, dv_step = sem("gp_step"), sem("dv_step")
        ident_ok, masks_ok, iota_ok, aid_ok = sem("ident_ok"), sem("masks_ok"), sem("iota_ok"), sem("aid_ok")
        ws_mm, ws_sb, ws_zero = sem("ws_mm"), sem("ws_sb"), sem("ws_zero")
        x_root, xn_ok, x_mm = sem("x_root"), sem("xn_ok"), sem("x_mm")
        c_mm, c_sb, c_sq, ss_mm, cT_ok = sem("c_mm"), sem("c_sb"), sem("c_sq"), sem("ss_mm"), sem("cT_ok")
        wkr_ok, kr_mm, kr_mul, kpe_ok = sem("wkr_ok"), sem("kr_mm"), sem("kr_mul"), sem("kpe_ok")
        wpe_ok, qkA_mm, qkD_mm, qkA_sb, qkD_sb, pe_add = (sem(n) for n in
                                                       ("wpe_ok", "qkA_mm", "qkD_mm", "qkA_sb", "qkD_sb", "pe_add"))
        s_mm, s_max, s_neg, s_exp, s_rec, p_ok, pt_mm, pt_sb, o_mm, o_sb = (sem(n) for n in (
            "s_mm", "s_max", "s_neg", "s_exp", "s_rec", "p_ok", "pt_mm", "pt_sb", "o_mm", "o_sb"))
        gb_mm, gb_sb, yb_mm, yb_sb = sem("gb_mm"), sem("gb_sb"), sem("yb_mm"), sem("yb_sb")
        v_mm, v_sb, v_ln, u_mm, u_sb = sem("v_mm"), sem("v_sb"), sem("v_ln"), sem("u_mm"), sem("u_sb")
        sp_mm, sp_sb, y_ok, ga_mm, ga_sb = sem("sp_mm"), sem("sp_sb"), sem("y_ok"), sem("ga_mm"), sem("ga_sb")
        gp_mm, gp_sb, mg_ok, w_mm, w_sb, h_ok = (sem(n) for n in ("gp_mm", "gp_sb", "mg_ok", "w_mm", "w_sb", "h_ok"))
        h_root, hn_ok, hn_out, m_mm = sem("h_root"), sem("hn_ok"), sem("hn_out"), sem("m_mm")
        pt2_mm, pt2_sb, pp_mm, pp_sb = sem("pt2_mm"), sem("pt2_sb"), sem("pp_mm"), sem("pp_sb")
        lg_mm, rt_sub, rt_exp, sel_ok, rank_mm, dst_ok = (sem(n) for n in (
            "lg_mm", "rt_sub", "rt_exp", "sel_ok", "rank_mm", "dst_ok"))
        fill_out, slots_out, tab_in, toks_ok, most_ok = (sem(n) for n in (
            "fill_out", "slots_out", "tab_in", "toks_ok", "most_ok"))
        gu_in = [sem(f"gu_in{i}") for i in range(NBUF)]
        dn_in = x_in
        gmb_in = sem("gmb_in")
        xg_in = [sem(f"xg_in{i}") for i in range(2)]
        y_out = [sem(f"y_out{i}") for i in range(2)]
        ix_ok, iy_ok = sem("ix_ok"), sem("iy_ok")
        gu_top, gu_rest, dn_top, dn_rest, xt_mm, xt_top, xt_rest, gu_mm, silu, h_mul, ht_mm, ht_top, ht_rest, y_mm, \
            y_sb = (sem(n) for n in ("gu_top", "gu_rest", "dn_top", "dn_rest", "xt_mm", "xt_top", "xt_rest", "gu_mm", "silu", "h_mul", "ht_mm",
                             "ht_top", "ht_rest", "y_mm", "y_sb"))
        block_free, dma_go = sem("block_free"), sem("dma_go")
        moe_done = sem("moe_done")
        gplb_in, at_ok, tab_mm, lgT_ok, wpg_rest = (sem(n) for n in (
            "gplb_in", "at_ok", "tab_mm", "lgT_ok", "wpg_rest"))
        y_in = [sem(f"y_in{t}") for t in range(NT)]
        ysum_ok, h2_ok, h2_root, n3_ok, n_mm = (sem(n) for n in (
            "ysum_ok", "h2_ok", "h2_root", "n3_ok", "n_mm"))
        g_mm, g_sb, pg_ok, h3_ok, h3_root, fin_ok, fin_out = (sem(n) for n in (
            "g_mm", "g_sb", "pg_ok", "h3_ok", "h3_root", "fin_ok", "fin_out"))
        mean_ok, root_ok = sem("mean_ok"), sem("root_ok")

        wi = w_in[0].rearrange("(k p) n -> p k n", p=P)
        uq = w_uq[0].rearrange("(k p) n -> p k n", p=P)
        ukv = w_ukv[0].rearrange("(k p) n -> p k n", p=P)
        wo = w_mla_o[0].rearrange("(k p) n -> p k n", p=P)
        wgp = w_gproj[0].rearrange("(k p) n -> p k n", p=P)
        wot = w_out[0].rearrange("(k p) n -> p k n", p=P)
        pieces = [wi[:, :, C_COL:C_COL + 512], wi[:, :, C_COL + 512:GA_COL], uq[:, :, 0:768], uq[:, :, 768:1536], ukv]
        PC_C, PC_UQ, PC_UKV = 0, 2, 4

        HK = ND // 2
        units, unit_read = [], []

        def add_units(views, reads):
            units.extend(views)
            unit_read.extend(reads)
            return len(units) - len(views)

        def halves(w, c, groups):
            return [w[:, HK * kh:HK * (kh + 1), c + 512 * j:c + 512 * (j + 1)] for j in range(groups) for kh in range(2)]

        U_GB = add_units([wi[:, :, GB_COL + FE * j:GB_COL + FE * (j + 1)] for j in range(4)],
                         [(gb_mm, 2 * j + 2) for j in range(4)])
        U_O = add_units([wo[:, :, FE * j:FE * (j + 1)] for j in range(4)], [(yb_mm, 2 * j + 2) for j in range(4)])
        U_V = add_units(halves(wi, V_COL, 3),
                        [r for j in range(3) for r in ((half_mm, j + 1), (v_mm, NT * (j + 1)))])
        U_U = add_units([wi[:, :, FE * j:FE * (j + 1)] for j in range(6)], [(u_mm, 2 * j + 2) for j in range(6)])
        U_GA = add_units([wi[:, :, GA_COL + FE * j:GA_COL + FE * (j + 1)] for j in range(4)],
                         [(ga_mm, 2 * j + 2) for j in range(4)])
        U_GP = add_units([wgp[:, :, P * j:P * (j + 1)] for j in range(8)], [(gp_mm, j + 1) for j in range(8)])
        U_W = add_units(halves(wot, 0, 2), [r for j in range(2) for r in ((half_mm, 4 + j), (w_mm, NT * (j + 1)))])
        N_UNITS = len(units)

        def piece(i):
            k, n = pieces[i].shape[1], pieces[i].shape[2]
            return piece_mem[i][:].rearrange("p (k n) -> p k n", k=k)

        piece_lo = [at(f"piece_lo{i}", PIECE_AT[i], [P, pieces[i].shape[1] * pieces[i].shape[2]], F32R)
                    for i in range(len(pieces))]
        piece_mem = [at(f"piece{i}", PIECE_AT[i], [P, pieces[i].shape[1] * pieces[i].shape[2]])
                     for i in range(len(pieces))]

        def rest_of(i):
            k, n = pieces[i].shape[1], pieces[i].shape[2]
            return piece_lo[i][:].rearrange("p (k n) -> p k n", k=k)

        def c_chunk(view, c):
            return view(PC_C)[:, :, P * c:P * (c + 1)] if c < 4 else view(PC_C + 1)[:, :, 0:P]

        def nope(v):
            return v.rearrange("p k (h c) -> p k h c", c=QW)[:, :, :, 0:NOPE]

        def unit_view(mem, n):
            k, c = units[n].shape[1], units[n].shape[2]
            return mem[:, 0:k * c].rearrange("p (k c) -> p k c", k=k)

        def arrived(eng, i):
            eng.wait_ge(piece_in[i], 16)

        def past(eng, s, v):
            if not isinstance(v, int) or v > 0:
                eng.wait_ge(s, v)

        s_bank = [(1, 384), (2, 0), (1, 0), (0, 0)]
        s_order = [0, 2, 3, 1]
        s_ready = [2, 4, 2, 3]
        p_off = [0, 128, 384, 768]
        t_bank = [(3, 0), (4, 0), (5, 0), (4, 384)]
        t_off = [0, 512, 896, 1152]

        MB = [2, 3, 4, 5, 6, 7, 0, 1]

        def scores(i):
            b, c = s_bank[i]
            return bank[b][:, c:c + P * (i + 1)]

        def turned(j):
            b, c = t_bank[j]
            return bank[b][:, c:c + P * (NT - j)]

        block = ctx.enter_context(nc.Block())

        @block.sync
        def _(sp):
            for t in range(NT):
                sp.dma_start(xs[:, t], x[0, P * t:P * (t + 1), :]).then_inc(x_in[t], 16)
                if t == 0:
                    sp.dma_start(gmxb[:], g_mix[0:1, :].to_broadcast([P, D])).then_inc(gmx_in, 16)
            for i in range(len(pieces)):
                sp.dma_start(piece(i), pieces[i]).then_inc(piece_in[i], 16)
            sp.wait_ge(piece_used, 1)
            for n in range(N_UNITS):
                if n >= 3:
                    sp.wait_ge(unit_rest, n - 2)
                sp.dma_start(unit_view(unit_raw[n % 3], n), units[n]).then_inc(unit_in[n % 3], 16)

            def matrix(e, r):
                w = (w_e_gate, w_e_up, w_e_down)[r]
                if isinstance(e, int):
                    return w[0, e].rearrange("(p k) n -> p (k n)", p=P)
                return w[0, bass.ds(e, 1)].rearrange("a (p k) n -> p (a k n)", p=P)

            def load_gate_up(e, u):
                for r in range(2):
                    sp.dma_start(gu[u][:, r].rearrange("p k n -> p (k n)"), matrix(e, r)).then_inc(gu_in[u], 16)

            def load_down(e, u):
                sp.dma_start(dn[u][:].rearrange("p k n -> p (k n)"), matrix(e, 2)).then_inc(dn_in[u], 16)

            sp.wait_ge(gp_mm, ND)
            load_gate_up(0, 0)
            load_down(0, 0)
            load_down(1, 1)
            sp.wait_ge(w_mm, 2 * NT)
            load_gate_up(1, 1)
            load_gate_up(2, 2)
            sp.wait_ge(lg_mm, 1)
            load_gate_up(3, 3)
            sp.wait_ge(tab_mm, 1)
            load_down(2, 2)
            sp.wait_ge(pp_mm, 2 * NT)
            load_down(3, 3)
            with sp.Fori(1, NE // NBUF) as i:
                for u in range(NBUF):
                    e = i * NBUF + u
                    sp.wait_ge(gu_mm, e - (NBUF - 1))
                    load_gate_up(e, u)
                    sp.wait_ge(y_mm, e - (NBUF - 1))
                    load_down(e, u)
            sp.wait_ge(most_ok, 2)
            most_v = sp.value_load(most_i[0:1, 0:1], min_val=0, max_val=S)
            with sp.If(most_v > CAP):
                with sp.Fori(1, NBLK) as b:
                    with sp.Fori(0, NE) as e:
                        sp.wait_ge(block_free, (b - 1) * NE + e + 1)
                        load_gate_up(e, 0)
                        load_down(e, 0)
                sp.wait_ge(y_mm, NE * NBLK)
            sp.wait_ge(y_mm, NE - 2)
            for q in range(4):
                sp.dma_start(wpg[:, 2 * q:2 * q + 2], w_ple_gate[0].rearrange("(p k) n -> p k n", p=P)[:, 2 * q:2 * q + 2])\
                    .then_inc(piece_in[q], 16)
            sp.wait_ge(moe_done, 1)
            for t in range(NT):
                sp.dma_start(y1[:, t], y_dram[P * t:P * (t + 1), :]).then_inc(y_in[t], 16)
                sp.dma_start(y2[:, t], y_dram[S + P * t:S + P * (t + 1), :]).then_inc(y_in[t], 16)
                if t == 0:
                    sp.dma_start(gplb[:], g_ple[0:1, :].to_broadcast([P, D])).then_inc(gplb_in, 16)
            sp.dma_start(gfin[:], g_final.rearrange("(a d) -> a d", a=1).to_broadcast([P, D])).then_inc(consts_in, 16)
            for t in range(NT):
                sp.wait_ge(fin_ok, t + 1)
                sp.dma_start(out[0, P * t:P * (t + 1), :], fin[:, t]).then_inc(fin_out, 16)
            sp.wait_ge(fin_out, 16 * NT)

        @block.gpsimd
        def _(pool):
            steps = [0]

            def link(ins):
                steps[0] += 1
                ins.then_inc(gp_step, 1)
                pool.wait_ge(gp_step, steps[0])

            pool.memset(eps[:], EPS).then_inc(ident_ok, 1)
            link(pool.memset(ident[:], 0.0))
            pool.affine_select(out=ident[:], in_=ident[:], compare_op=ALU.not_equal, fill=1.0, base=0,
                               pattern=[[-1, P]], channel_multiplier=1).then_inc(ident_ok, 1)
            link(pool.memset(mrow[:], 0.0))
            pool.memset(mrow[:, 0:CHUNK], 1.0).then_inc(masks_ok, 1)
            link(pool.memset(mcol[:], 0.0))
            pool.memset(mcol[:, CHUNK:P], MASKED).then_inc(masks_ok, 1)
            pool.memset(ones[:], 1.0).then_inc(masks_ok, 1)
            link(pool.memset(before[:], 1.0))
            pool.affine_select(out=before[:], in_=before[:], compare_op=ALU.is_gt, fill=0.0, base=0,
                               pattern=[[1, P]], channel_multiplier=-1).then_inc(masks_ok, 1)
            arrived(pool, PC_C + 1)
            kr = piece(PC_C + 1)[:, :, P:P + ROPE]
            for r in range(2):
                pool.tensor_copy(wkr[:, :, 0, ROPE * r:ROPE * (r + 1)], kr).then_inc(wkr_ok, 1)
                pool.tensor_copy(wkr[:, :, 1, ROPE * r:ROPE * r + HR], kr[:, :, HR:ROPE]).then_inc(wkr_ok, 1)
                pool.tensor_copy(wkr[:, :, 1, ROPE * r + HR:ROPE * (r + 1)], kr[:, :, 0:HR]).then_inc(wkr_ok, 1)
            for half in range(2):
                arrived(pool, PC_UQ + half)
                if half:
                    pool.wait_ge(qkD_mm, 4)
                wq = piece(PC_UQ + half).rearrange("p k (h c) -> p k h c", c=QW)[:, :, :, NOPE:QW]
                pool.tensor_copy(wpe[:, 0], wq).then_inc(wpe_ok, 1)
                pool.tensor_copy(wpe[:, 1, :, :, 0:HR], wq[:, :, :, HR:ROPE]).then_inc(wpe_ok, 1)
                pool.tensor_copy(wpe[:, 1, :, :, HR:ROPE], wq[:, :, :, 0:HR]).then_inc(wpe_ok, 1)
                if half == 0:
                    pool.wait_ge(kr_mul, 2)
                    pool.tensor_tensor(kpe[:], ropeA[:], ropeB[:], ALU.add).then_inc(kpe_ok, 1)
                for j in range(2 * half, 2 * half + 2):
                    pool.wait_ge(qkD_sb, 2 * j + 2)
                    pool.tensor_tensor(qpe[:, j], ropeA[:], ropeB[:], ALU.add).then_inc(pe_add, 1)
            pool.wait_ge(o_sb, NH)
            link(pool.memset(fill[:], EMPTY))
            pool.dma_start(tab_dram.rearrange("(p n) a -> p (n a)", p=P), fill[:]).then_inc(fill_out, 16)
            pool.iota(aid_1[:], pattern=[[S, 2], [P, NT]], base=1, channel_multiplier=1,
                      allow_small_or_imprecise_dtypes=True).then_inc(aid_ok, 1)
            pool.iota(aid[:], pattern=[[S, 2], [P, NT]], base=0, channel_multiplier=1).then_inc(aid_ok, 1)
            for g in range(NG):
                pool.wait_ge(sp_sb, g + 1)
                pool.wait_ge(u_sb, g + 1)
                pool.tensor_tensor(uT[:, g], uT[:, g], tmp[g % 2][:], ALU.mult).then_inc(y_ok, 1)
            for c in range(ND):
                pool.wait_ge(gp_sb, c + 1)
                pool.tensor_tensor(merged[:, c], merged[:, c], tmp[c % 2][:], ALU.add).then_inc(mg_ok, 1)
            pool.wait_ge(gp_mm, ND)
            pool.iota(iota_e[:], pattern=[[0, NT], [1, NE]], base=0, channel_multiplier=0,
                      allow_small_or_imprecise_dtypes=True).then_inc(iota_ok, 1)
            pool.wait_ge(w_mm, 2 * NT)
            pool.iota(iota_r[:], pattern=[[1, CAP]], base=0, channel_multiplier=0,
                      allow_small_or_imprecise_dtypes=True).then_inc(iota_ok, 1)
            pool.wait_ge(toks_ok, 1)
            pool.wait_ge(hn_out, 16 * NT)
            pool.wait_ge(m_mm, 2 * NT)

            def gather(e, u, i):
                b, n = u % 2, i * 2 + u // 2
                past(pool, xg_in[b], 16 * n)
                pool.tensor_copy(idx_x[b][:], toks[:, 0, bass.ds(e, 1)]).then_inc(ix_ok, 1)
                pool.wait_ge(ix_ok, e + 1)
                past(pool, xt_mm, e - 1)
                pool.sem_inc(dma_go, 1)
                pool.indirect_dma_start(out=xg[b][0:CAP, :], out_offset=None, in_=m_dram[:, :],
                                        in_offset=bass.IndirectOffsetOnAxis(ap=idx_x[b][:], axis=0),
                                        bounds_check=last_row, oob_is_err=False).then_inc(xg_in[b], 16)

            def scatter(e, u, i):
                b, n = u % 2, i * 2 + u // 2
                past(pool, y_out[b], 16 * n)
                pool.tensor_copy(idx_y[b][:], tabs[:, 0, bass.ds(e, 1)]).then_inc(iy_ok, 1)
                pool.wait_ge(iy_ok, e + 1)
                pool.wait_ge(y_sb, e + 1)
                pool.sem_inc(dma_go, 1)
                pool.indirect_dma_start(out=y_dram[:, :],
                                        out_offset=bass.IndirectOffsetOnAxis(ap=idx_y[b][:], axis=0),
                                        in_=ysb[b][0:CAP, :], in_offset=None,
                                        bounds_check=last_result, oob_is_err=False).then_inc(y_out[b], 16)

            last_row, last_result = pool.to_reg(S - 1), pool.to_reg(2 * S - 1)
            for u in range(NBUF):
                gather(u, u, 0)
            with pool.Fori(1, NE // NBUF) as i:
                for u in range(NBUF):
                    gather(i * NBUF + u, u, i)
                    scatter((i - 1) * NBUF + u, u, i - 1)
            last = NE // NBUF - 1
            for u in range(NBUF):
                scatter(last * NBUF + u, u, last)
            for b in range(2):
                pool.wait_ge(y_out[b], 16 * NE // 2)
            most_v = pool.value_load(most_i[0:1, 0:1], min_val=0, max_val=S)
            with pool.If(most_v > CAP):
                pool.wait_ge(fill_out, 16)
                pool.wait_ge(dst_ok, 1)
                for k in range(2):
                    for t in range(NT):
                        pool.indirect_dma_start(
                            out=tab_dram[:, :], out_offset=bass.IndirectOffsetOnAxis(ap=dst_i[:, k, t:t + 1], axis=0),
                            in_=aid[:, k, t:t + 1], in_offset=None,
                            bounds_check=SLOTS - 1, oob_is_err=False).then_inc(slots_out, 16)
                pool.wait_ge(slots_out, 16 * 2 * NT)
                pool.dma_start(tabs[:], tab_dram.rearrange("(b c e) a -> c b (e a)", b=NBLK, c=CAP)).then_inc(tab_in, 16)
                pool.wait_ge(toks_ok, 2)
                pool.sem_inc(block_free, 1)
                with pool.Fori(1, NBLK) as b:
                    with pool.Fori(0, NE) as e:
                        step = (b - 1) * NE + e
                        n = b * NE + e
                        pool.tensor_copy(idx_x[0][:], toks[:].rearrange("c b e -> c (b e)")[:, bass.ds(n, 1)])\
                            .then_inc(ix_ok, 1)
                        pool.tensor_copy(idx_y[0][:], tabs[:].rearrange("c b e -> c (b e)")[:, bass.ds(n, 1)])\
                            .then_inc(iy_ok, 1)
                        pool.wait_ge(ix_ok, n + 1)
                        pool.wait_ge(iy_ok, n + 1)
                        pool.sem_inc(dma_go, 1)
                        pool.indirect_dma_start(out=xg[0][0:CAP, :], out_offset=None, in_=m_dram[:, :],
                                                in_offset=bass.IndirectOffsetOnAxis(ap=idx_x[0][:], axis=0),
                                                bounds_check=last_row, oob_is_err=False).then_inc(xg_in[0], 16)
                        pool.wait_ge(y_sb, n + 1)
                        pool.sem_inc(dma_go, 1)
                        pool.indirect_dma_start(out=y_dram[:, :],
                                                out_offset=bass.IndirectOffsetOnAxis(ap=idx_y[0][:], axis=0),
                                                in_=ysb[0][0:CAP, :], in_offset=None,
                                                bounds_check=last_result, oob_is_err=False).then_inc(y_out[0], 16)
                        pool.wait_ge(y_out[0], step * 16 + (16 * NE // 2 + 16))
                        pool.sem_inc(block_free, 1)
            pool.sem_inc(moe_done, 1)
            pool.wait_ge(op_top, H_SPLIT + 4)
            pool.tensor_tensor(wpg_lo[:, 6:8], wpg[:, 6:8], wpg_hi[:, 6:8].bitcast(F32), ALU.subtract)\
                .then_inc(wpg_rest, 1)

        @block.scalar
        def _(act):
            with nc.allow_non_contiguous_dma(reason="gains, one per partition"):
                act.dma_start(gcq[:], g_cq[0].rearrange("(k p) -> p k", p=P)).then_inc(consts_in, 16)
                act.dma_start(gckv[:], g_ckv[0].rearrange("(k p) -> p k", p=P)).then_inc(consts_in, 16)
                act.dma_start(gvg[:], g_gv[0].rearrange("(k p) -> p k", p=P)).then_inc(consts_in, 16)
            act.dma_start(cosT[:], cos_t).then_inc(rope_in, 16)
            act.dma_start(sinT[:], sin_t).then_inc(rope_in, 16)
            act.dma_start(bsp[:], b_spatial[0:1].to_broadcast([P, NG, P])).then_inc(bias_in, 16)
            act.dma_start(brg[:], b_router_g[0:1, :].to_broadcast([P, NGRP])).then_inc(bias_in, 16)
            act.dma_start(bre[:], b_router_e[0:1].to_broadcast([P, NGRP, EPG])).then_inc(bias_in, 16)

            act.wait_ge(ident_ok, 1)

            def row_root(src, trash, n, t, root):
                act.activation(trash, src, ACT.Square, scale=float(D) ** -0.5,
                               accum_out=stat[:, n:n + 1]).then_inc(root, 1)
                act.wait_ge(root, 2 * t + 1)
                act.activation(rstd[:, n:n + 1], stat[:, n:n + 1], ACT.Sqrt, bias=eps[:]).then_inc(root, 1)

            def a_top(t):
                for half in range(2):
                    act.wait_ge(x_mm, 2 * t + half + 1)
                    act.activation(a_hi[:, 4 * half:4 * half + 4, P * t:P * (t + 1)],
                                   bank[2 * t + half][:].rearrange("p (k s) -> p k s", k=4), ACT.Copy)\
                        .then_inc(op_top, 1)

            def c_weight_top(c):
                if c < 4:
                    act.wait_ge(xn_ok, c + 1)
                else:
                    act.wait_ge(x_mm, 2)
                arrived(act, PC_C + c // 4)
                act.activation(wc_hi[c][:], c_chunk(piece, c), ACT.Copy).then_inc(w_top, 1)

            for t in range(NT):
                act.wait_ge(x_in[t], 16)
                row_root(xs[:, t], junk[:], t, t, x_root)
                if t:
                    a_top(t - 1)
            c_weight_top(0)
            a_top(NT - 1)
            act.wait_ge(x_mm, 2 * NT)
            act.dma_start(wsn[:], w_spatial[0].rearrange("g t s -> t g s")).then_inc(ws_in, 16)
            for c in range(1, 5):
                c_weight_top(c)
            act.wait_ge(wkr_ok, 6)
            act.activation(wkr_hi[:], wkr[:], ACT.Copy).then_inc(w_top, 1)

            def uq_top(half):
                arrived(act, PC_UQ + half)
                if half == 0:
                    act.wait_ge(x_mm, 2 * NT)
                else:
                    act.wait_ge(ws_mm, 3)
                act.activation(uq_hi[half][:], nope(piece(PC_UQ + half)), ACT.Copy).then_inc(w_top, 1)

            def wpe_top(half):
                act.wait_ge(wpe_ok, 3 * half + 3)
                if half == 0:
                    act.wait_ge(kr_mm, 2)
                else:
                    act.wait_ge(qkD_mm, 4)
                act.activation(wpe_hi[:], wpe[:], ACT.Copy).then_inc(w_top, 1)

            uq_top(0)
            def c_square(c):
                act.wait_ge(c_sb, c + 1)
                act.activation(csq[:, c], cT[:, c], ACT.Square).then_inc(c_sq, 1)

            def c_root(n):
                act.wait_ge(mean_ok, n + 1)
                act.activation((ropeA, ropeB)[n][:], rbc[:, n], ACT.Sqrt, bias=eps[:]).then_inc(root_ok, 1)

            def c_top(c):
                act.wait_ge(cT_ok, c + 1)
                act.activation(c_hi[:, c], cT[:, c], ACT.Copy).then_inc(op_top, 1)

            for c in range(4):
                c_square(c)
            c_root(0)
            c_square(4)
            for c in range(3):
                c_top(c)
            c_root(1)
            for b in range(3):
                act.wait_ge(ws_mm, b + 1)
                act.activation(wsT[:, 4 * b:4 * b + 4].rearrange("p g t -> p (g t)"), bank[1 + b][:], ACT.Copy)\
                    .then_inc(ws_sb, 1)
            for c in range(3, 5):
                c_top(c)
            wpe_top(0)
            for a in range(16):
                act.wait_ge(qkA_mm, a + 1)
                dst = qn[:, a] if a < NH else kn[:, a - NH]
                act.activation(dst, bank[1 + a % 4][:], ACT.Copy).then_inc(qkA_sb, 1)
                if a == 1:
                    uq_top(1)
                if a == 4:
                    wpe_top(1)
                if a in (5, 6):
                    arrived(act, PC_UKV)
                    act.activation(ukv_hi[:, a - 5], piece(PC_UKV)[:, a - 5], ACT.Copy).then_inc(w_top, 1)

            def softmax_exp(hd):
                for i in range(NT):
                    if i == 0:
                        act.wait_ge(s_neg, hd + 1)
                        past(act, pt_mm, hd - 1)
                    act.activation(pr[hd % 2][:, p_off[i]:p_off[i] + P * (i + 1)], scores(i), ACT.Exp,
                                   bias=mx[:, hd % 2, i:i + 1], scale=SCALE,
                                   accum_out=rs[:, hd % 2, i:i + 1]).then_inc(s_exp, 1)

            def probs_out(hd):
                act.wait_ge(pt_mm, hd + 1)
                past(act, o_mm, hd - 1)
                for j in range(NT):
                    act.activation(prT[hd % 2][:, t_off[j]:t_off[j] + P * (NT - j)], turned(j), ACT.Copy)\
                        .then_inc(pt_sb, 1)

            def head_out(hd):
                act.wait_ge(o_mm, hd + 1)
                act.activation(qn[:, hd], bank[6 + hd % 2][:], ACT.Copy).then_inc(o_sb, 1)

            def unit_split(n):
                if n >= N_UNITS:
                    return
                act.wait_ge(unit_in[n % 3], 16 * (n // 3 + 1))
                if n >= 2:
                    act.wait_ge(*unit_read[n - 2])
                else:
                    act.wait_ge(piece_used, 1)
                act.activation(unit_view(unit_hi[n % 2], n), unit_view(unit_raw[n % 3], n), ACT.Copy)\
                    .then_inc(unit_top, 1)

            softmax_exp(0)
            for hd in range(NH):
                if hd + 1 < NH:
                    softmax_exp(hd + 1)
                probs_out(hd)
                if hd:
                    head_out(hd - 1)
                if hd in (2, 4):
                    unit_split(hd // 2 - 1)
            head_out(NH - 1)
            for hd in range(NH):
                act.wait_ge(o_sb, hd + 1)
                act.activation(o_hi[:, hd], qn[:, hd], ACT.Copy).then_inc(op_top, 1)
            for c in range(ND):
                act.wait_ge(gb_mm, c + 1)
                act.activation(sigB[:, c], bank[c][:], ACT.Sigmoid).then_inc(gb_sb, 1)
                if c % 2:
                    unit_split(U_GB + c // 2 + 2)
            for j in range(4):
                unit_split(U_O + j + 2)
            for g in range(12):
                if g % 4 == 0:
                    unit_split(U_V + g // 2 + 2)
                act.wait_ge(v_mm, g + 1)
                act.activation(vt[:, g % 4, 512 * (g // 4):512 * (g // 4 + 1)], bank[g % 8][:],
                               ACT.Gelu_apprx_tanh).then_inc(v_sb, 1)
                if g % 4 == 3:
                    unit_split(U_V + g // 2 + 2)
            act.wait_ge(mean_ok, 2 + NT)
            act.activation(vrs[:], bag[:, :, 1], ACT.Sqrt, bias=eps[:]).then_inc(root_ok, 1)
            act.wait_ge(fill_out, 16)
            for c in range(NG):
                act.wait_ge(u_mm, c + 1)
                act.activation(uT[:, c], bank[(4 + c) % 8][:], ACT.Gelu_apprx_tanh).then_inc(u_sb, 1)
                if c % 2:
                    unit_split(U_U + c // 2 + 2)
            act.wait_ge(sp_mm, NG)
            act.dma_start(psb[:], p[0, 0].rearrange("(t p) d -> p t d", p=P)).then_inc(p_in, 16)

            def y_top(g):
                act.wait_ge(y_ok, g + 1)
                act.activation(y_hi[:, g], uT[:, g], ACT.Copy).then_inc(op_top, 1)

            for g in range(NG // 2):
                y_top(g)
            for c in range(ND):
                act.wait_ge(ga_mm, c + 1)
                act.activation(sigA[:, c], bank[(4 + c) % 8][:], ACT.Sigmoid).then_inc(ga_sb, 1)
                if c % 2:
                    unit_split(U_GA + c // 2 + 2)
                if 1 <= c < 7:
                    y_top(NG // 2 + c - 1)
            act.dma_start(h[:], x[0].rearrange("(t p) d -> p t d", p=P)).then_inc(x_again, 16)

            def merged_top(c):
                act.wait_ge(mg_ok, c + 1)
                act.activation(mg_hi[:, c], merged[:, c], ACT.Copy).then_inc(op_top, 1)

            for c in range(ND):
                unit_split(U_GP + c + 2)
                if c:
                    merged_top(c - 1)
            merged_top(ND - 1)
            act.dma_start(wpp[:], w_ple_proj[0].rearrange("(k p) n -> p k n", p=P)).then_inc(wpp_in, 16)
            act.dma_start(gmb[:], g_moe[0:1, :].to_broadcast([P, D])).then_inc(gmb_in, 16)
            with nc.allow_non_contiguous_dma(reason="the router's rows"):
                act.dma_start(wr[:, :, 0:NGRP], w_router_g[0].rearrange("(p k) n -> p k n", p=P)).then_inc(wr_in, 16)
                act.dma_start(wr[:, :, NGRP:NGRP + NE], w_router_e[0].rearrange("(p k) n -> p k n", p=P))\
                    .then_inc(wr_in, 16)
            unit_split(U_W + 2)
            unit_split(U_W + 3)
            for k in range(2):
                act.wait_ge(pt2_mm, k + 1)
                act.activation(pT[:, k], bank[4 + k][:], ACT.Copy).then_inc(pt2_sb, 1)

            def pp_out(g):
                act.wait_ge(pp_mm, g + 1)
                act.activation(pp[:, g // 2, 512 * (g % 2):512 * (g % 2 + 1)], bank[6 + g if g < 2 else (g + 2) % 8][:],
                               ACT.Copy).then_inc(pp_sb, 1)

            for t in range(NT):
                act.wait_ge(h_ok, t + 1)
                row_root(h[:, t], trash2[:], NT + t, t, h_root)
            act.wait_ge(wr_in, 32)
            act.wait_ge(w_mm, 2 * NT)
            act.activation(wr_hi[:], wr[:], ACT.Copy).then_inc(op_top, 1)
            for g in range(2):
                pp_out(g)
            act.wait_ge(hn_ok, NT)
            act.wait_ge(h_root, 2 * NT)
            for t in range(NT):
                act.dma_start(m_dram[P * t:P * (t + 1), :], hn[:, t]).then_inc(hn_out, 16)
            for t in range(NT):
                for half in range(2):
                    act.wait_ge(m_mm, 2 * t + half + 1)
                    act.activation(m_hi[:, 4 * half:4 * half + 4, P * t:P * (t + 1)],
                                   bank[MB[2 * t + half]][:].rearrange("p (k s) -> p k s", k=4), ACT.Copy)\
                        .then_inc(op_top, 1)
            for r in range(2):
                act.wait_ge(gu_in[0], 32)
                if r == 1:
                    act.wait_ge(lg_mm, 1)
                    act.activation(lgT[:], bank[2][0:NGRP + NE, :], ACT.Copy).then_inc(lgT_ok, 1)
                act.activation(gu_hi[0][:, r], gu[0][:, r], ACT.Copy).then_inc(gu_top, 1)
            for s in range(2):
                act.wait_ge(rt_sub, s + 1)
                act.activation(r8[1 + s][:], r8[1 + s][:], ACT.Exp).then_inc(rt_exp, 1)
            for g in range(2, 8):
                pp_out(g)
            def gate_up_top(e, u, i):
                act.wait_ge(gu_in[u], i * 32 + 32)
                past(act, gu_mm, e - 1)
                for r in range(2):
                    act.activation(gu_hi[u % 2][:, r], gu[u][:, r], ACT.Copy).then_inc(gu_top, 1)

            def down_top(e, u, i):
                act.wait_ge(dn_in[u], i * 16 + 32)
                act.activation(dn_hi[:], dn[u][:], ACT.Copy).then_inc(dn_top, 1)

            def rows_top(e, b, wait_gu=True):
                act.wait_ge(xt_mm, e + 1)
                if wait_gu:
                    past(act, gu_mm, e - 1)
                for half in range(2):
                    ins = act.activation(xt_hi[b][:, 4 * half:4 * half + 4],
                                         bank[half][:, 0:4 * CAP].rearrange("p (k c) -> p k c", k=4), ACT.Copy)
                ins.then_inc(xt_top, 1)

            def hidden_top(e, b, wait_y=True):
                act.wait_ge(ht_mm, e + 1)
                if wait_y:
                    past(act, y_mm, e - 1)
                act.activation(ht_hi[b][:], bank[4 + b][:, 0:2 * CAP].rearrange("p (j c) -> p j c", j=2), ACT.Copy)\
                    .then_inc(ht_top, 1)

            def silu_step(e, b, wait_mul=True):
                act.wait_ge(gu_mm, e + 1)
                if wait_mul:
                    past(act, ht_mm, e - 1)
                act.activation(hm[b][0:CAP], bank[2 + b][0:CAP, 0:FE], ACT.Silu).then_inc(silu, 1)

            def result_out(e, b, uses):
                act.wait_ge(y_mm, e + 1)
                past(act, y_out[b], uses)
                for half in range(2):
                    ins = act.activation(ysb[b][0:CAP, 512 * half:512 * (half + 1)], bank[6 + half][0:CAP, :], ACT.Copy)
                ins.then_inc(y_sb, 1)

            def expert_step(i, u, first=False, last=False):
                e = i * NBUF + u
                (i1, u1), (i2, u2) = [(i, u - d) if u >= d else (i - 1, u - d + NBUF) for d in (1, 2)]
                if not first:
                    hidden_top(e - 1, u1 % 2)
                if not first and not (isinstance(e, int) and e == 1):
                    result_out(e - 2, u2 % 2, 16 * (i2 * 2 + u2 // 2))
                if not first:
                    down_top(e - 1, u1, i1)
                silu_step(e, u % 2)
                if not last:
                    rows_top(e + 1, (u + 1) % 2)
                if not (isinstance(e, int) and e + 2 >= NE):
                    gate_up_top(e + 2, (u + 2) % NBUF, i if u < 2 else i + 1)

            rows_top(0, 0)
            gate_up_top(1, 1, 0)
            for u in range(NBUF):
                expert_step(0, u, first=(u == 0))
            with act.Fori(1, NE // NBUF - 1) as i:
                for u in range(NBUF):
                    expert_step(i, u)
            for u in range(NBUF):
                expert_step(NE // NBUF - 1, u, last=(u == NBUF - 1))
            hidden_top(NE - 1, 1)
            result_out(NE - 2, 0, 16 * (NE // 2 - 1))
            down_top(NE - 1, NBUF - 1, NE // NBUF - 1)
            result_out(NE - 1, 1, 16 * (NE // 2 - 1))
            most_v = act.value_load(most_i[0:1, 0:1], min_val=0, max_val=S)
            with act.If(most_v > CAP):
                with act.Fori(1, NBLK) as b:
                    with act.Fori(0, NE) as e:
                        n = b * NE + e
                        rows_top(n, 0, wait_gu=False)
                        step = (b - 1) * NE + e
                        act.wait_ge(gu_in[0], step * 32 + (32 * NE // NBUF + 32))
                        for r in range(2):
                            act.activation(gu_hi[0][:, r], gu[0][:, r], ACT.Copy).then_inc(gu_top, 1)
                        act.wait_ge(dn_in[0], step * 16 + (16 * NE // NBUF + 32))
                        act.activation(dn_hi[:], dn[0][:], ACT.Copy).then_inc(dn_top, 1)
                        silu_step(n, 0, wait_mul=False)
                        hidden_top(n, 0, wait_y=False)
                        act.wait_ge(y_mm, n + 1)
                        for half in range(2):
                            ins = act.activation(ysb[0][0:CAP, 512 * half:512 * (half + 1)], bank[6 + half][0:CAP, :],
                                                 ACT.Copy)
                        ins.then_inc(y_sb, 1)
            act.wait_ge(y_mm, NE)
            for q in range(4):
                act.wait_ge(piece_in[q], 32)
                act.activation(wpg_hi[:, 2 * q:2 * q + 2], wpg[:, 2 * q:2 * q + 2], ACT.Copy).then_inc(op_top, 1)

            def third_root(t):
                act.wait_ge(h2_ok, t + 1)
                row_root(h[:, t], trash3[:], 2 * NT + t, t, h2_root)

            def third_top(t):
                for half in range(2):
                    act.wait_ge(n_mm, 2 * t + half + 1)
                    act.activation(n3_hi[:, 4 * half:4 * half + 4, P * t:P * (t + 1)],
                                   bank[2 * (t % 2) + half][:].rearrange("p (k s) -> p k s", k=4), ACT.Copy)\
                        .then_inc(op_top, 1)

            third_root(0)
            third_root(1)
            third_top(0)
            third_root(2)
            third_root(3)
            for t in range(NT):
                if t + 1 < NT:
                    third_top(t + 1)
                act.wait_ge(g_mm, t + 1)
                for half in range(2):
                    act.activation(sgt[:, t, 512 * half:512 * (half + 1)], bank[4 + 2 * (t % 2) + half][:],
                                   ACT.Sigmoid).then_inc(g_sb, 1)
                act.wait_ge(h3_ok, t + 1)
                row_root(h[:, t], fin[:, t], t, t, h3_root)

        @block.vector
        def _(dve):
            steps = [0]

            def link(ins):
                steps[0] += 1
                ins.then_inc(dv_step, 1)
                dve.wait_ge(dv_step, steps[0])

            def invert(y, v, w):
                link(dve.reciprocal(y, y))
                link(dve.scalar_tensor_tensor(w, v, EPS, y, ALU.add, ALU.mult))
                link(dve.scalar_tensor_tensor(w, w, -0.5, y, ALU.mult, ALU.mult))
                link(dve.scalar_tensor_tensor(y, w, 1.5, y, ALU.add, ALU.mult))

            def inv_rms(n, count=1):
                invert(rstd[:, n:n + count], stat[:, n:n + count], rnt[:, 0:count])

            def weight_rest(n, lo, full, hi):
                dve.wait_ge(w_top, n)
                dve.tensor_tensor(lo, full, hi.bitcast(F32), ALU.subtract).then_inc(w_rest, 1)

            def a_rest(t):
                for half in range(2):
                    dve.wait_ge(op_top, 2 * t + half + 1)
                    dst = (slice(None), slice(4 * half, 4 * half + 4), slice(P * t, P * (t + 1)))
                    dve.tensor_tensor(a_lo[dst], bank[2 * t + half][:].rearrange("p (k s) -> p k s", k=4),
                                      a_hi[dst].bitcast(F32), ALU.subtract).then_inc(op_rest, 1)

            def c_weight_rest(c):
                weight_rest(c + 1, c_chunk(rest_of, c), c_chunk(piece, c), wc_hi[c][:])

            def uq_rest(half):
                weight_rest(W_UQ + 2 * half, nope(rest_of(PC_UQ + half)), nope(piece(PC_UQ + half)), uq_hi[half][:])

            def wpe_rest(half):
                weight_rest(W_UQ + 2 * half + 1, wpe_lo[:], wpe[:], wpe_hi[:])

            for t in range(NT):
                dve.wait_ge(x_root, 2 * t + 2)
                inv_rms(t)
                if t == 0:
                    dve.wait_ge(gmx_in, 16)
                dve.scalar_tensor_tensor(xn[:, t], xs[:, t], rstd[:, t:t + 1], gmxb[:], ALU.mult, ALU.mult)\
                    .then_inc(xn_ok, 1)
                if t:
                    a_rest(t - 1)
            c_weight_rest(0)
            a_rest(NT - 1)
            for c in range(1, 5):
                c_weight_rest(c)
            weight_rest(W_KR, wkr_lo[:], wkr[:], wkr_hi[:])
            uq_rest(0)
            dve.wait_ge(consts_in, 16 * 3)
            def c_out(c):
                dve.wait_ge(c_mm, c + 1)
                dve.tensor_copy(cT[:, c], bank[c][:]).then_inc(c_sb, 1)

            def c_inverse(n, scratch):
                dve.wait_ge(ss_mm, n + 1)
                dve.tensor_scalar(rbc[:, n], bank[5 + n][:], 1.0 / (QL, KVL)[n], None, ALU.mult).then_inc(mean_ok, 1)
                dve.wait_ge(root_ok, n + 1)
                invert((ropeA, ropeB)[n][:], rbc[:, n], scratch)

            def c_scale(c):
                g = gcq[:, c:c + 1] if c < 3 else gckv[:, c - 3:c - 2]
                dve.scalar_tensor_tensor(cT[:, c], cT[:, c], g, (ropeA if c < 3 else ropeB)[:], ALU.mult, ALU.mult)\
                    .then_inc(cT_ok, 1)

            def c_rest(c):
                dve.wait_ge(op_top, A_SPLIT + c + 1)
                dve.tensor_tensor(c_lo[:, c], cT[:, c], c_hi[:, c].bitcast(F32), ALU.subtract).then_inc(op_rest, 1)

            for c in range(4):
                c_out(c)
            dve.wait_ge(c_sb, 3)
            c_inverse(0, csq[:, 0])
            c_out(4)
            for c in range(3):
                c_scale(c)
            for c in range(3):
                c_rest(c)
            dve.wait_ge(c_sb, 5)
            c_inverse(1, csq[:, 3])
            for c in range(3, 5):
                c_scale(c)
            for c in range(3, 5):
                c_rest(c)
            wpe_rest(0)
            dve.wait_ge(rope_in, 32)
            dve.wait_ge(kr_mm, 1)
            dve.tensor_tensor(ropeA[:], bank[7][:], cosT[:], ALU.mult).then_inc(kr_mul, 1)
            dve.wait_ge(kr_mm, 2)
            dve.tensor_tensor(ropeB[:], bank[0][:], sinT[:], ALU.mult).then_inc(kr_mul, 1)
            dve.wait_ge(ws_sb, 3)
            dve.memset(wsT[CHUNK:P, :, 0:CHUNK], 0.0).then_inc(ws_zero, 1)
            uq_rest(1)
            DB = [5, 6, 7, 0]
            for d in range(16):
                dve.wait_ge(qkD_mm, d + 1)
                if d < 8:
                    if d % 2 == 0:
                        dve.wait_ge(kpe_ok, 1)
                        past(dve, pe_add, d // 2)
                    dve.tensor_tensor((ropeA, ropeB)[d % 2][:], bank[DB[d % 4]][:], (cosT, sinT)[d % 2][:], ALU.mult)\
                        .then_inc(qkD_sb, 1)
                    if d == 3:
                        wpe_rest(1)
                    if d in (5, 6):
                        weight_rest(W_UKV + d - 5, rest_of(PC_UKV)[:, d - 5], piece(PC_UKV)[:, d - 5], ukv_hi[:, d - 5])
                else:
                    t, q = (d - 8) // 2, (d - 8) % 2
                    dve.tensor_copy(vv[:, t, 4 * q:4 * q + 4].rearrange("p h v -> p (h v)"), bank[DB[d % 4]][:])\
                        .then_inc(qkD_sb, 1)

            def maxima(hd):
                past(dve, s_exp, NT * (hd - 1))
                for i in s_order:
                    dve.wait_ge(s_mm, NT * hd + s_ready[i])
                    dve.tensor_reduce(mx[:, hd % 2, i:i + 1], scores(i), AX_X, ALU.max).then_inc(s_max, 1)
                dve.wait_ge(s_max, NT * (hd + 1))
                dve.tensor_scalar(mx[:, hd % 2], mx[:, hd % 2], -SCALE, None, ALU.mult).then_inc(s_neg, 1)

            def normalise(hd):
                dve.wait_ge(s_exp, NT * (hd + 1))
                dve.reciprocal(ri[:, hd % 2], rs[:, hd % 2]).then_inc(s_rec, 1)
                dve.wait_ge(s_rec, hd + 1)
                for i in range(NT):
                    v = pr[hd % 2][:, p_off[i]:p_off[i] + P * (i + 1)]
                    dve.tensor_scalar(v, v, ri[:, hd % 2, i:i + 1], None, ALU.mult).then_inc(p_ok, 1)

            def unit_left(n):
                if n >= N_UNITS:
                    return
                dve.wait_ge(unit_top, n + 1)
                dve.tensor_tensor(unit_view(unit_lo[n % 2], n), unit_view(unit_raw[n % 3], n),
                                  unit_view(unit_hi[n % 2], n).bitcast(F32), ALU.subtract).then_inc(unit_rest, 1)

            def operand_left(lo, full, hi, n):
                dve.wait_ge(op_top, n + 1)
                dve.tensor_tensor(lo, full, hi.bitcast(F32), ALU.subtract).then_inc(op_rest, 1)

            maxima(0)
            for hd in range(NH):
                normalise(hd)
                if hd + 1 < NH:
                    maxima(hd + 1)
                if hd in (4, 6):
                    unit_left(hd // 2 - 2)
            for hd in range(NH):
                operand_left(o_lo[:, hd], qn[:, hd], o_hi[:, hd], C_SPLIT + hd)
            for j in range(4):
                unit_left(U_GB + j + 2)
            for c in range(ND):
                dve.wait_ge(yb_mm, c + 1)
                dve.wait_ge(gb_sb, c + 1)
                dve.tensor_tensor(merged[:, c], bank[c][:], sigB[:, c], ALU.mult).then_inc(yb_sb, 1)
                if c % 2:
                    unit_left(U_O + c // 2 + 2)
            for g in range(12):
                if g % 4 == 0:
                    unit_left(U_V + g // 2 + 2)
                dve.wait_ge(v_sb, g + 1)
                link(dve.bn_stats(bst[:, g % 4, g // 4], vt[:, g % 4, 512 * (g // 4):512 * (g // 4 + 1)]))
                if g % 4 == 3:
                    unit_left(U_V + g // 2 + 2)
            for t in range(NT):
                dve.bn_aggr(bag[:, t], bst[:, t].rearrange("p a b -> p (a b)")).then_inc(mean_ok, 1)
            dve.wait_ge(root_ok, 3)
            invert(vrs[:], bag[:, :, 1], rnt[:])
            for t in range(NT):
                dve.tensor_scalar(vt[:, t], vt[:, t], bag[:, t, 0:1], vrs[:, t:t + 1], ALU.subtract, ALU.mult)\
                    .then_inc(v_ln, 1)
            for j in range(6):
                unit_left(U_U + j + 2)
            dve.wait_ge(bias_in, 48)
            for g in range(NG):
                dve.wait_ge(sp_mm, g + 1)
                past(dve, y_ok, g - 1)
                dve.scalar_tensor_tensor(tmp[g % 2][:].rearrange("p (n t) -> p n t", n=NT),
                                         bank[g % 8][:].rearrange("p (n t) -> p n t", n=NT), gvg[:, g:g + 1],
                                         bsp[:, g].unsqueeze(1).to_broadcast([P, NT, P]), ALU.mult, ALU.add)\
                    .then_inc(sp_sb, 1)
            for g in range(NG // 2):
                operand_left(y_lo[:, g], uT[:, g], y_hi[:, g], O_SPLIT + g)
            for j in range(4):
                unit_left(U_GA + j + 2)
                for g in range(NG // 2 + 2 * j, min(NG // 2 + 2 * j + 2, NG)):
                    operand_left(y_lo[:, g], uT[:, g], y_hi[:, g], O_SPLIT + g)
            for c in range(ND):
                dve.wait_ge(gp_mm, c + 1)
                dve.wait_ge(ga_sb, c + 1)
                past(dve, mg_ok, c - 1)
                dve.tensor_tensor(tmp[c % 2][:], bank[(4 + c) % 8][:], sigA[:, c], ALU.mult).then_inc(gp_sb, 1)
                unit_left(U_GP + c + 2)
                if c:
                    operand_left(mg_lo[:, c - 1], merged[:, c - 1], mg_hi[:, c - 1], Y_SPLIT + c - 1)
            operand_left(mg_lo[:, ND - 1], merged[:, ND - 1], mg_hi[:, ND - 1], M_SPLIT - 1)
            unit_left(U_W + 2)
            dve.wait_ge(x_again, 16)
            for g in range(2 * NT):
                t, half = g % NT, g // NT
                dve.wait_ge(w_mm, g + 1)
                hs = h[:, t, 512 * half:512 * (half + 1)]
                ins = dve.tensor_tensor(hs, hs, bank[(4 + g) % 8][:], ALU.add)
                if half == 0:
                    ins.then_inc(w_sb, 1)
                else:
                    ins.then_inc(h_ok, 1)
                if g == 0:
                    unit_left(U_W + 3)
            for t in range(NT):
                dve.wait_ge(h_root, 2 * t + 2)
                inv_rms(NT + t)
                if t == 0:
                    dve.wait_ge(gmb_in, 16)
                dve.scalar_tensor_tensor(hn[:, t], h[:, t], rstd[:, NT + t:NT + t + 1], gmb[:], ALU.mult, ALU.mult)\
                    .then_inc(hn_ok, 1)
            dve.wait_ge(op_top, WR_SPLIT)
            dve.tensor_tensor(wr_lo[:], wr[:], wr_hi[:].bitcast(F32), ALU.subtract).then_inc(op_rest, 1)
            for t in range(NT):
                for half in range(2):
                    dve.wait_ge(op_top, WR_SPLIT + 2 * t + half + 1)
                    dst = (slice(None), slice(4 * half, 4 * half + 4), slice(P * t, P * (t + 1)))
                    dve.tensor_tensor(m_lo[dst], bank[MB[2 * t + half]][:].rearrange("p (k s) -> p k s", k=4),
                                      m_hi[dst].bitcast(F32), ALU.subtract).then_inc(op_rest, 1)

            grp, prob, eprob, score, cand, oh1, oh2, esel = r8
            m1, s1, i1, gw, p1, p2, ps, d1 = r1[:8]

            def bc8(v):
                return v[:].unsqueeze(2).to_broadcast([P, NT, EPG])

            def bct(v):
                return v[:].unsqueeze(1).to_broadcast([P, NT, EPG])

            def softmax8(src, dst, n):
                link(dve.tensor_reduce(m1[:], src, AX_X, ALU.max))
                dve.tensor_tensor(dst[:], src, bc8(m1), ALU.subtract).then_inc(rt_sub, 1)
                dve.wait_ge(rt_exp, n + 1)
                link(dve.tensor_reduce(s1[:], dst[:], AX_X, ALU.add))
                link(dve.reciprocal(s1[:], s1[:]))
                link(dve.tensor_tensor(dst[:], dst[:], bc8(s1), ALU.mult))

            def first_max(src, onehot):
                link(dve.tensor_reduce(m1[:], src[:], AX_X, ALU.max))
                link(dve.tensor_tensor(cand[:], src[:], bc8(m1), ALU.is_equal))
                link(dve.scalar_tensor_tensor(cand[:], cand[:], float(-EPG), bct(iota8up), ALU.mult, ALU.add))
                link(dve.tensor_reduce(i1[:], cand[:], AX_X, ALU.min))
                link(dve.tensor_tensor(onehot[:], bct(iota8), bc8(i1), ALU.is_equal))

            link(dve.memset(sel[:, NT], 0.0))
            link(dve.memset(iota8[:, 0:1], 0.0))
            for k in range(1, EPG):
                link(dve.memset(iota8[:, k:k + 1], float(k)))
            link(dve.tensor_scalar(iota8up[:], iota8[:], float(EPG), None, ALU.add))
            def gate_up_rest(e, u, r):
                dve.wait_ge(gu_top, e * 2 + (r + 1))
                dve.tensor_tensor(gu_lo[u][:, r], gu[u][:, r], gu_hi[u % 2][:, r].bitcast(F32), ALU.subtract)\
                    .then_inc(gu_rest, 1)

            def down_rest(e, u):
                dve.wait_ge(dn_top, e + 1)
                dve.tensor_tensor(dn_lo[u][:], dn[u][:], dn_hi[:].bitcast(F32), ALU.subtract).then_inc(dn_rest, 1)

            for r in range(2):
                gate_up_rest(0, 0, r)
            dve.wait_ge(lg_mm, 2)
            link(dve.tensor_copy(lg[:], bank[3][:, 0:NT * (NGRP + NE)].rearrange("p (t n) -> p t n", t=NT)))
            softmax8(lg[:, :, 0:NGRP], prob, 0)
            link(dve.tensor_tensor(score[:], prob[:], bct(brg), ALU.add))
            first_max(score, grp)
            def choose(src):
                for t in range(NT):
                    ins = dve.tensor_tensor(rt_e[:, t], src(t), grp[:, t].unsqueeze(2).to_broadcast([P, NGRP, EPG]),
                                            ALU.mult)
                link(ins)
                link(dve.tensor_reduce(esel[:], rt_e[:].rearrange("p t g e -> p t e g"), AX_X, ALU.add))

            choose(lambda t: lg[:, t, NGRP:NGRP + NE].rearrange("p (g e) -> p g e", g=NGRP))
            softmax8(esel[:], eprob, 1)
            choose(lambda t: bre[:])
            link(dve.tensor_tensor(score[:], eprob[:], esel[:], ALU.add))
            first_max(score, oh1)
            link(dve.scalar_tensor_tensor(score[:], oh1[:], MASKED, score[:], ALU.mult, ALU.add))
            first_max(score, oh2)
            for oh, s4 in ((oh1, sel1), (oh2, sel2)):
                for t in range(NT):
                    ins = dve.tensor_tensor(s4[:, t], grp[:, t].unsqueeze(2).to_broadcast([P, NGRP, EPG]),
                                            oh[:, t].unsqueeze(1).to_broadcast([P, NGRP, EPG]), ALU.mult)
            link(ins)
            flat = "p t g e -> p t (g e)"
            dve.tensor_tensor(sel[:, 0:NT], sel1[:].rearrange(flat), sel2[:].rearrange(flat), ALU.add).then_inc(sel_ok, 1)
            link(dve.tensor_tensor(score[:], prob[:], grp[:], ALU.mult))
            link(dve.tensor_reduce(gw[:], score[:], AX_X, ALU.add))
            for oh, pk in ((oh1, p1), (oh2, p2)):
                link(dve.tensor_tensor(cand[:], oh[:], eprob[:], ALU.mult))
                link(dve.tensor_reduce(pk[:], cand[:], AX_X, ALU.add))
            link(dve.tensor_tensor(ps[:], p1[:], p2[:], ALU.add))
            link(dve.reciprocal(ps[:], ps[:]))
            link(dve.tensor_tensor(ps[:], ps[:], gw[:], ALU.mult))
            link(dve.tensor_tensor(wts[:, 0], p1[:], ps[:], ALU.mult))
            link(dve.tensor_tensor(wts[:, 1], p2[:], ps[:], ALU.mult))
            dve.wait_ge(iota_ok, 2)
            dve.wait_ge(aid_ok, 2)
            for k, s4 in enumerate((sel1, sel2)):
                dve.tensor_tensor(number[k][:], s4[:].rearrange(flat),
                                  aid_1[:, k].unsqueeze(2).to_broadcast([P, NT, NE]), ALU.mult).then_inc(at_ok, 1)
            dve.wait_ge(rank_mm, 1)
            for k, s4 in enumerate((sel1, sel2)):
                link(dve.tensor_tensor(rt_e[:].rearrange(flat), s4[:].rearrange(flat),
                                       bank[2][:, 0:NT * NE].rearrange("p (t e) -> p t e", t=NT), ALU.mult))
                link(dve.tensor_reduce(r_of[:, k], rt_e[:].rearrange(flat), AX_X, ALU.add))
                dve.tensor_tensor(at_rank[k][:], iota_r[:].unsqueeze(1).to_broadcast([P, NT, CAP]),
                                  r_of[:, k].unsqueeze(2).to_broadcast([P, NT, CAP]), ALU.is_equal).then_inc(at_ok, 1)
            dve.tensor_reduce(most[:], bank[2][0:1, NT * NE:NT * NE + NE], AX_X, ALU.max).then_inc(most_ok, 1)
            dve.wait_ge(most_ok, 1)
            dve.tensor_copy(most_i[:], most[:]).then_inc(most_ok, 1)
            dve.wait_ge(tab_mm, 1)
            link(dve.tensor_scalar(tab_f[:], bank[3][0:CAP, 0:NE], 0.0, float(EMPTY + 1), ALU.is_equal, ALU.mult))
            link(dve.tensor_tensor(tab_f[:], tab_f[:], bank[3][0:CAP, 0:NE], ALU.add))
            link(dve.tensor_scalar(tabs[:, 0], tab_f[:], -1.0, None, ALU.add))
            dve.tensor_scalar(toks[:, 0], tabs[:, 0], TOKEN_BITS, None, ALU.bitwise_and).then_inc(toks_ok, 1)
            for k in range(2):
                link(dve.tensor_scalar(r_of[:, k], r_of[:, k], float(NE), None, ALU.mult))
                s4 = (sel1, sel2)[k]
                link(dve.tensor_tensor(rt_e[:].rearrange(flat), s4[:].rearrange(flat), iota_e[:], ALU.mult))
                link(dve.tensor_reduce(e_of[:, k], rt_e[:].rearrange(flat), AX_X, ALU.add))
                link(dve.tensor_tensor(r_of[:, k], r_of[:, k], e_of[:, k], ALU.add))
                ins = dve.tensor_copy(dst_i[:, k], r_of[:, k])
            ins.then_inc(dst_ok, 1)

            def rows_rest(e, b):
                dve.wait_ge(xt_top, e + 1)
                for half in range(2):
                    ins = dve.tensor_tensor(xt_lo[b][:, 4 * half:4 * half + 4],
                                            bank[half][:, 0:4 * CAP].rearrange("p (k c) -> p k c", k=4),
                                            xt_hi[b][:, 4 * half:4 * half + 4].bitcast(F32), ALU.subtract)
                ins.then_inc(xt_rest, 1)

            def hidden_rest(e, b):
                dve.wait_ge(ht_top, e + 1)
                dve.tensor_tensor(ht_lo[b][:], bank[4 + b][:, 0:2 * CAP].rearrange("p (j c) -> p j c", j=2),
                                  ht_hi[b][:].bitcast(F32), ALU.subtract).then_inc(ht_rest, 1)

            def gated(e, b):
                dve.wait_ge(silu, e + 1)
                dve.tensor_tensor(hm[b][0:CAP], hm[b][0:CAP], bank[2 + b][0:CAP, FE:2 * FE], ALU.mult)\
                    .then_inc(h_mul, 1)

            def expert_step(i, u, first=False, last=False):
                e = i * NBUF + u
                if not first:
                    hidden_rest(e - 1, (u + 1) % 2)
                if not last:
                    gate_up_rest(e + 1, (u + 1) % NBUF, 0)
                if not first:
                    down_rest(e - 1, (u - 1) % NBUF)
                if not last:
                    gate_up_rest(e + 1, (u + 1) % NBUF, 1)
                gated(e, u % 2)
                if not last:
                    rows_rest(e + 1, (u + 1) % 2)

            rows_rest(0, 0)
            for u in range(NBUF):
                expert_step(0, u, first=(u == 0))
            with dve.Fori(1, NE // NBUF - 1) as i:
                for u in range(NBUF):
                    expert_step(i, u)
            for u in range(NBUF):
                expert_step(NE // NBUF - 1, u, last=(u == NBUF - 1))
            hidden_rest(NE - 1, 1)
            down_rest(NE - 1, NBUF - 1)
            most_v = dve.value_load(most_i[0:1, 0:1], min_val=0, max_val=S)
            with dve.If(most_v > CAP):
                dve.wait_ge(tab_in, 16)
                dve.tensor_scalar(toks[:], tabs[:], TOKEN_BITS, None, ALU.bitwise_and).then_inc(toks_ok, 1)
                with dve.Fori(1, NBLK) as b:
                    with dve.Fori(0, NE) as e:
                        n = b * NE + e
                        rows_rest(n, 0)
                        for r in range(2):
                            gate_up_rest(n, 0, r)
                        down_rest(n, 0)
                        gated(n, 0)
                        hidden_rest(n, 0)

            for q in range(3):
                dve.wait_ge(op_top, H_SPLIT + q + 1)
                dve.tensor_tensor(wpg_lo[:, 2 * q:2 * q + 2], wpg[:, 2 * q:2 * q + 2],
                                  wpg_hi[:, 2 * q:2 * q + 2].bitcast(F32), ALU.subtract).then_inc(op_rest, 1)

            def third_norm(t):
                dve.wait_ge(h2_root, 2 * t + 2)
                inv_rms(2 * NT + t)
                dve.scalar_tensor_tensor(n3[t][:], h[:, t], rstd[:, 2 * NT + t:2 * NT + t + 1], gplb[:],
                                         ALU.mult, ALU.mult).then_inc(n3_ok, 1)

            def third_rest(t):
                for half in range(2):
                    dve.wait_ge(op_top, PG_SPLIT + 2 * t + half + 1)
                    dst = (slice(None), slice(4 * half, 4 * half + 4), slice(P * t, P * (t + 1)))
                    dve.tensor_tensor(n3_lo[dst], bank[2 * (t % 2) + half][:].rearrange("p (k s) -> p k s", k=4),
                                      n3_hi[dst].bitcast(F32), ALU.subtract).then_inc(op_rest, 1)

            def add_experts(t):
                dve.wait_ge(y_in[t], 32)
                link(dve.scalar_tensor_tensor(ysum[:, t % 2], y1[:, t], wts[:, 0, t:t + 1], h[:, t],
                                              ALU.mult, ALU.add))
                dve.scalar_tensor_tensor(h[:, t], y2[:, t], wts[:, 1, t:t + 1], ysum[:, t % 2], ALU.mult, ALU.add)\
                    .then_inc(h2_ok, 1)

            add_experts(0)
            add_experts(1)
            dve.wait_ge(gplb_in, 16)
            third_norm(0)
            third_rest(0)
            third_norm(1)
            add_experts(2)
            third_norm(2)
            add_experts(3)
            third_norm(3)
            dve.wait_ge(pp_sb, 8)
            dve.wait_ge(consts_in, 16 * 4)
            for t in range(NT):
                if t + 1 < NT:
                    third_rest(t + 1)
                dve.wait_ge(g_sb, 2 * t + 2)
                dve.tensor_tensor(sgt[:, t], sgt[:, t], pp[:, t], ALU.mult).then_inc(pg_ok, 1)
                dve.wait_ge(pg_ok, t + 1)
                dve.tensor_tensor(h[:, t], h[:, t], sgt[:, t], ALU.add).then_inc(h3_ok, 1)
                dve.wait_ge(h3_root, 2 * t + 2)
                inv_rms(t)
                dve.scalar_tensor_tensor(fin[:, t], h[:, t], rstd[:, t:t + 1], gfin[:], ALU.mult, ALU.mult)\
                    .then_inc(fin_ok, 1)

        @block.tensor
        def _(pe):
            def product(dst, pairs):
                for n, (l, r) in enumerate(pairs):
                    ins = pe.matmul(dst, l, r, start=(n == 0), stop=(n == len(pairs) - 1))
                return ins

            def product3(dst, quads, start=True, stop=True):
                for n, (a_top, a_rest, b_top, b_rest) in enumerate(quads):
                    pe.matmul(dst, a_top, b_top, start=(start and n == 0), stop=False)
                    pe.matmul(dst, a_top, b_rest, start=False, stop=False)
                    ins = pe.matmul(dst, a_rest, b_top, start=False, stop=(stop and n == len(quads) - 1))
                return ins

            pe.wait_ge(ident_ok, 2)
            for t in range(NT):
                pe.wait_ge(xn_ok, t + 1)
                for half in range(2):
                    for k in range(4):
                        ins = pe.transpose(bank[2 * t + half][:, P * k:P * (k + 1)],
                                           xn[:, t, P * (4 * half + k):P * (4 * half + k + 1)], ident[:])
                    ins.then_inc(x_mm, 1)
            pe.wait_ge(op_rest, A_SPLIT)

            for c in range(5):
                if c == 4:
                    pe.wait_ge(masks_ok, 4)
                    pe.wait_ge(c_sq, 3)
                    product(bank[5][:], [(ones[:], csq[:, n]) for n in range(3)]).then_inc(ss_mm, 1)
                pe.wait_ge(w_rest, c + 1)
                lo = c_chunk(rest_of, c)
                product3(bank[c][:], [(wc_hi[c][:, k], lo[:, k], a_hi[:, k], a_lo[:, k]) for k in range(ND)])\
                    .then_inc(c_mm, 1)

            def key_rope(r, b):
                product3(bank[b][:], [(wkr_hi[:, k, r], wkr_lo[:, k, r], a_hi[:, k], a_lo[:, k]) for k in range(ND)])\
                    .then_inc(kr_mm, 1)

            pe.wait_ge(w_rest, W_KR)
            key_rope(0, 7)
            pe.wait_ge(c_sq, 5)
            product(bank[6][:], [(ones[:], csq[:, c]) for c in range(3, 5)]).then_inc(ss_mm, 1)
            pe.wait_ge(c_sb, 1)
            key_rope(1, 0)
            pe.wait_ge(ws_in, 16)
            pe.wait_ge(c_sb, 4)
            for b in range(3):
                for g in range(4 * b, 4 * b + 4):
                    ins = pe.transpose(bank[1 + b][:, P * (g % 4):P * (g % 4 + 1)], wsn[:, g], ident[:])
                ins.then_inc(ws_mm, 1)

            pe.wait_ge(c_sb, 5)
            pe.wait_ge(ws_sb, 3)
            DB = [5, 6, 7, 0]
            na, nd = [0], [0]

            def to_act(quads):
                a = na[0]
                na[0] += 1
                past(pe, qkA_sb, a - 3)
                return product3(bank[1 + a % 4][:], quads)

            def to_dve(quads):
                d = nd[0]
                nd[0] += 1
                if d == 2:
                    pe.wait_ge(kr_mul, 2)
                past(pe, qkD_sb, d - 3)
                return product3(bank[DB[d % 4]][:], quads)

            pe.wait_ge(op_rest, A_SPLIT + 3)
            for half in range(2):
                pe.wait_ge(w_rest, W_UQ + 2 * half)
                lo = nope(rest_of(PC_UQ + half))
                for j in range(4):
                    to_act([(uq_hi[half][:, k, j], lo[:, k, j], c_hi[:, k], c_lo[:, k]) for k in range(3)])\
                        .then_inc(qkA_mm, 1)
                pe.wait_ge(w_rest, W_UQ + 2 * half + 1)
                for j in range(2):
                    for r in range(2):
                        hi, lo2 = wpe_hi[:, r, :, 2 * j:2 * j + 2], wpe_lo[:, r, :, 2 * j:2 * j + 2]
                        to_dve([(hi[:, k].rearrange("p h c -> p (h c)"), lo2[:, k].rearrange("p h c -> p (h c)"),
                                 c_hi[:, k], c_lo[:, k]) for k in range(3)]).then_inc(qkD_mm, 1)
            pe.wait_ge(w_rest, W_UKV + 1)
            pe.wait_ge(op_rest, C_SPLIT)
            hi, lo = ukv_hi[:], rest_of(PC_UKV)
            for j in range(NH):
                c = slice(KVW * j, KVW * j + NOPE)
                to_act([(hi[:, k, c], lo[:, k, c], c_hi[:, 3 + k], c_lo[:, 3 + k]) for k in range(2)])\
                    .then_inc(qkA_mm, 1)
                t, q = j // 2, j % 2
                v_hi, v_lo = (w.rearrange("p k (h c) -> p k h c", c=KVW)[:, :, 4 * q:4 * q + 4, NOPE:KVW]
                              for w in (hi, lo))
                c = slice(P * t, P * (t + 1))
                to_dve([(c_hi[:, 3 + k, c], c_lo[:, 3 + k, c], v_hi[:, k], v_lo[:, k]) for k in range(2)])\
                    .then_inc(qkD_mm, 1)
            pe.wait_ge(qkA_sb, 16)
            pe.wait_ge(qkD_sb, 16)
            pe.sem_inc(piece_used, 1)
            pe.wait_ge(kpe_ok, 1)
            pe.wait_ge(pe_add, NH // 2)

            def head_scores(hd):
                past(pe, s_exp, NT * hd)
                r = ROPE * (hd % 2)
                for i in s_order:
                    o, kw = scores(i), P * (i + 1)
                    pe.matmul(o, qn[:, hd, P * i:P * (i + 1)], kn[:, hd, 0:kw], start=True, stop=False)
                    pe.matmul(o, qpe[r:r + ROPE, hd // 2, P * i:P * (i + 1)], kpe[r:r + ROPE, 0:kw],
                              start=False, stop=False)
                    pe.matmul(o[:, P * i + CHUNK:kw], mrow[:], mcol[:, CHUNK:P], start=False, stop=True).then_inc(s_mm, 1)

            def head_turn(hd):
                pe.wait_ge(p_ok, NT * (hd + 1))
                past(pe, pt_sb, NT * hd)
                for j in range(NT):
                    for i in range(j, NT):
                        ins = pe.transpose(turned(j)[:, P * (i - j):P * (i - j + 1)],
                                           pr[hd % 2][:, p_off[i] + P * j:p_off[i] + P * (j + 1)], ident[:])
                ins.then_inc(pt_mm, 1)

            def head_values(hd):
                past(pe, o_sb, hd - 1)
                for j in range(NT):
                    pe.wait_ge(pt_sb, NT * hd + j + 1)
                    ins = pe.matmul(bank[6 + hd % 2][:, P * j:S], vv[:, j, hd],
                                    prT[hd % 2][:, t_off[j]:t_off[j] + P * (NT - j)], start=(j == 0), stop=(j == NT - 1))
                ins.then_inc(o_mm, 1)

            head_scores(0)
            for hd in range(NH):
                if hd + 1 < NH:
                    head_scores(hd + 1)
                head_turn(hd)
                if hd:
                    head_values(hd - 1)
            head_values(NH - 1)

            def feature_chunks(first, n_units, op_hi, op_lo, free, done):
                c = 0
                for n in range(first, first + n_units):
                    pe.wait_ge(unit_rest, n + 1)
                    hi, lo = unit_view(unit_hi[n % 2], n), unit_view(unit_lo[n % 2], n)
                    for cc in range(hi.shape[2] // P):
                        b, w = free(c), slice(P * cc, P * (cc + 1))
                        product3(bank[b][:], [(hi[:, k, w], lo[:, k, w], op_hi[:, k], op_lo[:, k])
                                              for k in range(hi.shape[1])]).then_inc(done, 1)
                        c += 1

            def token_tiles(first, groups, op_hi, op_lo, free, done):
                for j in range(groups):
                    for kh in range(2):
                        n = first + 2 * j + kh
                        pe.wait_ge(unit_rest, n + 1)
                        if done is w_mm and j == 0:
                            pe.wait_ge(op_rest, Y_SPLIT + HK * (kh + 1))
                        hi, lo = unit_view(unit_hi[n % 2], n), unit_view(unit_lo[n % 2], n)
                        for t in range(NT):
                            b, c = free(NT * j + t, kh), slice(P * t, P * (t + 1))
                            ins = product3(bank[b][:], [(op_hi[:, HK * kh + k, c], op_lo[:, HK * kh + k, c], hi[:, k],
                                                         lo[:, k]) for k in range(HK)], start=(kh == 0), stop=(kh == 1))
                            if kh:
                                ins.then_inc(done, 1)
                        if kh == 0:
                            ins.then_inc(half_mm, 1)

            def gb_bank(c):
                if c == 3:
                    pe.wait_ge(pt_sb, NT * NH)
                if c == 6:
                    pe.wait_ge(o_sb, NH)
                return c

            pe.wait_ge(s_exp, NT * NH)
            feature_chunks(U_GB, 4, a_hi, a_lo, gb_bank, gb_mm)

            def yb_bank(c):
                pe.wait_ge(gb_sb, c + 1)
                return c

            pe.wait_ge(op_rest, O_SPLIT)
            feature_chunks(U_O, 4, o_hi, o_lo, yb_bank, yb_mm)

            def v_bank(g, kh):
                if kh == 0 and g < 8:
                    pe.wait_ge(yb_sb, g + 1)
                elif kh == 0:
                    pe.wait_ge(v_sb, g - 7)
                return g % 8

            token_tiles(U_V, 3, a_hi, a_lo, v_bank, v_mm)

            def u_bank(c):
                if c < 8:
                    pe.wait_ge(v_sb, c + 5)
                else:
                    pe.wait_ge(u_sb, c - 7)
                return (4 + c) % 8

            feature_chunks(U_U, 6, a_hi, a_lo, u_bank, u_mm)

            pe.wait_ge(v_ln, NT)
            pe.wait_ge(ws_zero, 1)
            for g in range(NG):
                if g < 8:
                    pe.wait_ge(u_sb, g + 5)
                else:
                    pe.wait_ge(sp_sb, g - 7)
                for n in range(NT):
                    ins = pe.matmul(bank[g % 8][:, P * n:P * (n + 1)], vt[:, n, P * g:P * (g + 1)], wsT[:, g],
                                    start=True, stop=True)
                ins.then_inc(sp_mm, 1)

            def ga_bank(c):
                pe.wait_ge(sp_sb, c + 5)
                return (4 + c) % 8

            feature_chunks(U_GA, 4, a_hi, a_lo, ga_bank, ga_mm)

            def gp_bank(c):
                pe.wait_ge(ga_sb, c + 1)
                return (4 + c) % 8

            pe.wait_ge(op_rest, Y_SPLIT)
            feature_chunks(U_GP, 8, y_hi, y_lo, gp_bank, gp_mm)

            def w_bank(g, kh):
                if kh == 0:
                    pe.wait_ge(gp_sb, g + 1)
                return (4 + g) % 8

            token_tiles(U_W, 2, mg_hi, mg_lo, w_bank, w_mm)

            pe.wait_ge(p_in, 16)
            pe.wait_ge(w_sb, 2)
            for k in range(2):
                for t in range(NT):
                    ins = pe.transpose(bank[4 + k][:, P * t:P * (t + 1)], psb[:, t, P * k:P * (k + 1)], ident[:])
                ins.then_inc(pt2_mm, 1)
            pe.wait_ge(pt2_sb, 2)
            pe.wait_ge(wpp_in, 16)

            def embed(g, b):
                t, half = g // 2, g % 2
                return product(bank[b][:], [(pT[:, k, P * t:P * (t + 1)], wpp[:, k, 512 * half:512 * (half + 1)])
                                            for k in range(2)])

            pe.wait_ge(w_sb, NT)
            pe.wait_ge(h_ok, 2)
            for g in range(2):
                embed(g, 6 + g).then_inc(pp_mm, 1)
            pe.wait_ge(h_ok, NT)
            for t in range(NT):
                pe.wait_ge(hn_ok, t + 1)
                if t == 2:
                    pe.wait_ge(pp_sb, 2)
                for half in range(2):
                    for k in range(4):
                        ins = pe.transpose(bank[MB[2 * t + half]][:, P * k:P * (k + 1)],
                                           hn[:, t, 4 * half + k:D:ND], ident[:])
                    ins.then_inc(m_mm, 1)
            pe.wait_ge(op_rest, WR_SPLIT)
            pe.wait_ge(op_rest, H_SPLIT)
            product3(bank[2][0:NGRP + NE, :], [(wr_hi[:, k], wr_lo[:, k], m_hi[:, k], m_lo[:, k]) for k in range(ND)])\
                .then_inc(lg_mm, 1)
            pe.wait_ge(lgT_ok, 1)
            for t in range(NT):
                ins = pe.transpose(bank[3][:, (NGRP + NE) * t:(NGRP + NE) * (t + 1)], lgT[:, P * t:P * (t + 1)],
                                   ident[0:NGRP + NE, 0:NGRP + NE])
            ins.then_inc(lg_mm, 1)
            pe.wait_ge(sel_ok, 1)
            def ranks(a, b):
                return bank[2][:, NE * a:NE * b]

            def chosen(a, b):
                return sel[:, a:b].rearrange("p t e -> p (t e)")

            pe.matmul(ranks(0, NT + 1), before[:], chosen(0, NT + 1), start=True, stop=False)
            for d in range(1, NT + 1):
                ins = pe.matmul(ranks(d, NT + 1), ones[:], chosen(0, NT + 1 - d), start=False, stop=(d == NT))
            ins.then_inc(rank_mm, 1)
            for g in range(2, 8):
                if g == 4:
                    pe.wait_ge(at_ok, 4)
                    product(bank[3][0:CAP, 0:NE], [(at_rank[k][:, t], number[k][:, t])
                                                   for k in range(2) for t in range(NT)]).then_inc(tab_mm, 1)
                embed(g, (g + 2) % 8).then_inc(pp_mm, 1)

            def turn_rows(e, b, fills):
                pe.wait_ge(xg_in[b], fills)
                past(pe, xt_rest, e)
                for k in range(ND):
                    ins = pe.transpose(bank[k // 4][:, CAP * (k % 4):CAP * (k % 4 + 1)], xg[b][0:CAP, k:D:ND],
                                       ident[0:CAP, 0:CAP])
                ins.then_inc(xt_mm, 1)

            def gate_up(e, u, wait_mul=True):
                b = u % 2
                pe.wait_ge(xt_rest, e + 1)
                pe.wait_ge(gu_rest, e * 2 + 2)
                if wait_mul:
                    past(pe, h_mul, e - 1)
                product3(bank[2 + b][0:CAP, :], [(xt_hi[b][:, k], xt_lo[b][:, k], gu_hi[b][:, :, k], gu_lo[u][:, :, k])
                                                 for k in range(ND)]).then_inc(gu_mm, 1)

            def turn_hidden(e, b, wait_rest=True):
                pe.wait_ge(h_mul, e + 1)
                if wait_rest:
                    past(pe, ht_rest, e - 1)
                for j in range(2):
                    ins = pe.transpose(bank[4 + b][:, CAP * j:CAP * (j + 1)], hm[b][0:CAP, j:FE:2],
                                       ident[0:CAP, 0:CAP])
                ins.then_inc(ht_mm, 1)

            def down(e, u):
                b = u % 2
                pe.wait_ge(ht_rest, e + 1)
                pe.wait_ge(dn_rest, e + 1)
                past(pe, y_sb, e)
                for half in range(2):
                    c = slice(512 * half, 512 * (half + 1))
                    ins = product3(bank[6 + half][0:CAP, :],
                                   [(ht_hi[b][:, j], ht_lo[b][:, j], dn_hi[:, j, c], dn_lo[u][:, j, c])
                                    for j in range(2)])
                ins.then_inc(y_mm, 1)

            def expert_step(i, u, first=False, last=False):
                e = i * NBUF + u
                ni, nu = (i, u + 1) if u + 1 < NBUF else (i + 1, 0)
                if not first:
                    turn_hidden(e - 1, (u + 1) % 2)
                gate_up(e, u)
                if not last:
                    turn_rows(e + 1, nu % 2, 16 * (ni * 2 + nu // 2 + 1))
                if not first:
                    down(e - 1, (u - 1) % NBUF)

            pe.wait_ge(pp_sb, 8)
            pe.wait_ge(most_ok, 2)
            turn_rows(0, 0, 16)
            for u in range(NBUF):
                expert_step(0, u, first=(u == 0))
            with pe.Fori(1, NE // NBUF - 1) as i:
                for u in range(NBUF):
                    expert_step(i, u)
            for u in range(NBUF):
                expert_step(NE // NBUF - 1, u, last=(u == NBUF - 1))
            turn_hidden(NE - 1, 1)
            down(NE - 1, NBUF - 1)
            most_v = pe.value_load(most_i[0:1, 0:1], min_val=0, max_val=S)
            with pe.If(most_v > CAP):
                with pe.Fori(1, NBLK) as b:
                    with pe.Fori(0, NE) as e:
                        n = b * NE + e
                        turn_rows(n, 0, ((b - 1) * NE + e) * 16 + (16 * NE // 2 + 16))
                        gate_up(n, 0, wait_mul=False)
                        turn_hidden(n, 0, wait_rest=False)
                        down(n, 0)

            def turn_third(t):
                pe.wait_ge(n3_ok, t + 1)
                for half in range(2):
                    if 2 * t + half > 3:
                        pe.wait_ge(op_rest, N3_REST + 2 * t + half - 3)
                    for k in range(4):
                        ins = pe.transpose(bank[2 * (t % 2) + half][:, P * k:P * (k + 1)],
                                           n3[t][:, 4 * half + k:D:ND], ident[:])
                    ins.then_inc(n_mm, 1)

            turn_third(0)
            pe.wait_ge(op_rest, N3_REST)
            for t in range(NT):
                pe.wait_ge(op_rest, N3_REST + 2 * t + 2)
                past(pe, g_sb, 2 * (t - 1))
                tok = slice(P * t, P * (t + 1))
                for half in range(2):
                    if half and t + 1 < NT:
                        turn_third(t + 1)
                    c, b = slice(512 * half, 512 * (half + 1)), bank[4 + 2 * (t % 2) + half][:]
                    gate = [(n3_hi[:, k, tok], n3_lo[:, k, tok], wpg_hi[:, k, c], wpg_lo[:, k, c]) for k in range(ND)]
                    product3(b, gate[0:6], stop=False)
                    pe.wait_ge(wpg_rest, 1)
                    ins = product3(b, gate[6:8], start=False)
                ins.then_inc(g_mm, 1)


_INS = ["x", "p", "g_mix", "w_in", "g_gv", "w_spatial", "b_spatial", "w_gproj", "g_cq", "w_uq", "g_ckv", "w_ukv",
        "w_mla_o", "w_out", "g_moe", "w_router_g", "b_router_g", "w_router_e", "b_router_e", "w_e_gate", "w_e_up",
        "w_e_down", "g_ple", "w_ple_gate", "w_ple_proj", "g_final"]


def _rope_tables(np):
    inv = (10000.0 ** (-np.arange(0, 64, 2, dtype=np.float32) / np.float32(64))).astype(np.float32)
    ang = (np.arange(512, dtype=np.float32)[None, :] * inv[:, None]).astype(np.float32)
    cos, sin = np.cos(ang).astype(np.float32), np.sin(ang).astype(np.float32)
    return np.concatenate([cos] * 4), np.concatenate([-sin, sin, -sin, sin])


def kernel(**inputs):
    import numpy as _np
    import concourse.bacc as _bacc
    from concourse import mybir as _mybir
    from concourse.bass_utils import run_bass_kernel_spmd as _run

    nc = _bacc.Bacc("TRN2", target_bir_lowering=False, num_devices=1)
    arrays, args = {}, []
    cos, sin = _rope_tables(_np)
    for name, a in [(n, inputs[n]) for n in _INS] + [("cos", cos), ("sin", sin)]:
        a = _np.ascontiguousarray(a)
        arrays[f"in_{name}_dram"] = a
        args.append(nc.dram_tensor(f"in_{name}_dram", a.shape, _mybir.dt.from_np(a.dtype), kind="ExternalInput").ap())
    args.append(nc.dram_tensor("out_0_dram", (1, 512, 1024), _mybir.dt.float32, kind="ExternalOutput").ap())
    build(nc, *args)
    r = _run(nc, [arrays], core_ids=[0])
    return r.results[0]["out_0_dram"]
```
